# Optimizing a Trainium2 kernel written in Bass

```python
import numpy as np
import jax
import jax.numpy as jnp
from jax import lax

D_MODEL = 1024
BATCH = 1
SEQ = 256
DEPTH = 2

HEAD_DIM = 64
NSA_HEADS = 8
NSA_KV_HEADS = 2
NSA_GROUP = NSA_HEADS // NSA_KV_HEADS
NSA_WIDTH = NSA_HEADS * HEAD_DIM
KV_WIDTH = NSA_KV_HEADS * HEAD_DIM
CMP_LEN = 32
CMP_STRIDE = 16
CMP_HIDDEN = 2 * HEAD_DIM
SEL_BLOCK = 64
N_SELECT = 16
WINDOW = 512
Q_BLOCK = 128
MASK_VALUE = -1e30
SEL_FORCE = 1e6
CONV_WIDTH = 256
CONV_K = 3
HGRN_HEADS = 4
HGRN_WIDTH = HGRN_HEADS * HEAD_DIM
HGRN_CHUNK = 64
LB_FLOOR = 1e-30
MIX_WIDTH = NSA_WIDTH + CONV_WIDTH + HGRN_WIDTH
ROPE_THETA = 10000.0
MEM_LEN = 256
CROSS_HEADS = 4
CROSS_WIDTH = CROSS_HEADS * HEAD_DIM
N_GROUPS = 4
EXPERTS_PER_GROUP = 8
N_EXPERTS = N_GROUPS * EXPERTS_PER_GROUP
EXPERT_TOP_K = 2
D_EXPERT = 512
RMS_EPS = 1e-6

IN_SIZES = (NSA_WIDTH, KV_WIDTH, KV_WIDTH, KV_WIDTH, KV_WIDTH, KV_WIDTH, KV_WIDTH, NSA_HEADS * 3,
            CONV_WIDTH, CONV_WIDTH, CONV_WIDTH, HGRN_WIDTH, HGRN_WIDTH, HGRN_WIDTH, HGRN_WIDTH)
IN_WIDTH = sum(IN_SIZES)
IN_OFFSETS = tuple(sum(IN_SIZES[:i + 1]) for i in range(len(IN_SIZES) - 1))

kernel_name = 'hymba_nsa_conv_hgrn2_hmoe'

def rmsnorm(x, g):
    x32 = x.astype(jnp.float32)
    y = x32 * lax.rsqrt(jnp.mean(x32 * x32, axis=-1, keepdims=True) + RMS_EPS)
    return (y * g.astype(jnp.float32)).astype(x.dtype)

def rope(x, pos):
    T = x.shape[1]
    half = x.shape[-1] // 2
    inv = ROPE_THETA ** (-jnp.arange(half, dtype=jnp.float32) / half)
    ang = pos.astype(jnp.float32)[:, None] * inv[None, :]
    bshape = (1, T) + (1,) * (x.ndim - 3) + (half,)
    cos = jnp.cos(ang).reshape(bshape)
    sin = jnp.sin(ang).reshape(bshape)
    x32 = x.astype(jnp.float32)
    x1, x2 = x32[..., :half], x32[..., half:]
    return jnp.concatenate([x1 * cos - x2 * sin, x2 * cos + x1 * sin], axis=-1).astype(x.dtype)

def masked_softmax(s, mask):
    s = jnp.where(mask, s.astype(jnp.float32), MASK_VALUE)
    m = jnp.max(s, axis=-1, keepdims=True)
    e = jnp.where(mask, jnp.exp(s - m), 0.0)
    den = jnp.sum(e, axis=-1, keepdims=True)
    return e / jnp.where(den > 0, den, 1.0)

def to_blocks(a):
    B, T = a.shape[:2]
    return jnp.moveaxis(a.reshape((B, T // Q_BLOCK, Q_BLOCK) + a.shape[2:]), 1, 0)

def nsa_compress(k, pe, w1, w2):
    B, T, H, dh = k.shape
    nc = (T - CMP_LEN) // CMP_STRIDE + 1
    idx = np.arange(nc)[:, None] * CMP_STRIDE + np.arange(CMP_LEN)[None, :]
    blk = k[:, idx] + pe[None, None, :, None, :]
    blk = jnp.swapaxes(blk, 2, 3).reshape(B, nc, H, CMP_LEN * dh)
    return jnp.dot(jax.nn.silu(jnp.dot(blk, w1)), w2)

def nsa_attention(q, q_rot, gate, kc, vc, ks, vs, kw, vw):
    B, T, H, G, dh = q.shape
    nc = kc.shape[1]
    ns = T // SEL_BLOCK
    n_sel = min(N_SELECT, ns)
    nblk = T // Q_BLOCK
    scale = dh ** -0.5
    cmp_end = jnp.arange(nc) * CMP_STRIDE + CMP_LEN - 1
    cs = np.arange(nc) * CMP_STRIDE
    ss = np.arange(ns) * SEL_BLOCK
    ov = np.clip(np.minimum(cs[:, None] + CMP_LEN, ss[None, :] + SEL_BLOCK)
                 - np.maximum(cs[:, None], ss[None, :]), 0, None) / CMP_LEN
    cmp_to_sel = jnp.asarray(ov, dtype=jnp.float32)
    ks_blk = jnp.swapaxes(ks, 1, 2).reshape(B, H, ns, SEL_BLOCK, dh)
    vs_blk = jnp.swapaxes(vs, 1, 2).reshape(B, H, ns, SEL_BLOCK, dh)
    kw_pad = jnp.pad(kw, ((0, 0), (WINDOW, 0), (0, 0), (0, 0)))
    vw_pad = jnp.pad(vw, ((0, 0), (WINDOW, 0), (0, 0), (0, 0)))
    bi = jnp.arange(B)[:, None, None, None]
    hi = jnp.arange(H)[None, :, None, None]
    j = jnp.arange(ns)

    def block(args):
        i, qb, qrb, gb = args
        t = i * Q_BLOCK + jnp.arange(Q_BLOCK)
        s_c = jnp.einsum('bqhgd,bchd->bhgqc', qb, kc) * scale
        p_c = masked_softmax(s_c, cmp_end[None, :] <= t[:, None])
        o_c = jnp.einsum('bhgqc,bchd->bqhgd', p_c.astype(vc.dtype), vc)
        imp = jnp.einsum('bhgqc,cj->bhqj', p_c, cmp_to_sel)
        cur = t // SEL_BLOCK
        forced = (j[None, :] == 0) | (j[None, :] == cur[:, None]) | (j[None, :] == cur[:, None] - 1)
        imp = jnp.where(j[None, :] > cur[:, None], -SEL_FORCE, jnp.where(forced, SEL_FORCE, imp))
        _, sel = lax.top_k(imp, n_sel)
        m = n_sel * SEL_BLOCK
        ks_g = ks_blk[bi, hi, sel].reshape(B, H, Q_BLOCK, m, dh)
        vs_g = vs_blk[bi, hi, sel].reshape(B, H, Q_BLOCK, m, dh)
        kpos_s = (sel[..., None] * SEL_BLOCK + jnp.arange(SEL_BLOCK)).reshape(B, H, 1, Q_BLOCK, m)
        s_s = jnp.einsum('bqhgd,bhqmd->bhgqm', qrb, ks_g) * scale
        p_s = masked_softmax(s_s, kpos_s <= t[:, None])
        o_s = jnp.einsum('bhgqm,bhqmd->bqhgd', p_s.astype(vs.dtype), vs_g)
        start = i * Q_BLOCK
        kwb = lax.dynamic_slice_in_dim(kw_pad, start, WINDOW + Q_BLOCK, axis=1)
        vwb = lax.dynamic_slice_in_dim(vw_pad, start, WINDOW + Q_BLOCK, axis=1)
        kpos_w = start - WINDOW + jnp.arange(WINDOW + Q_BLOCK)
        dist = t[:, None] - kpos_w[None, :]
        mask_w = (dist >= 0) & (dist < WINDOW) & (kpos_w[None, :] >= 0)
        s_w = jnp.einsum('bqhgd,bkhd->bhgqk', qrb, kwb) * scale
        p_w = masked_softmax(s_w, mask_w)
        o_w = jnp.einsum('bhgqk,bkhd->bqhgd', p_w.astype(vw.dtype), vwb)
        g = jax.nn.sigmoid(gb.astype(jnp.float32)).astype(qb.dtype)
        return g[..., 0:1] * o_c + g[..., 1:2] * o_s + g[..., 2:3] * o_w

    out = lax.map(block, (jnp.arange(nblk), to_blocks(q), to_blocks(q_rot), to_blocks(gate)))
    return jnp.moveaxis(out, 0, 1).reshape(B, T, H * G * dh)

def short_conv(b_gate, c_gate, h, w):
    u = c_gate * h
    y = lax.conv_general_dilated(u, w[:, None, :].astype(u.dtype), window_strides=(1,),
                                 padding=[(CONV_K - 1, 0)], dimension_numbers=('NWC', 'WIO', 'NWC'),
                                 feature_group_count=u.shape[-1])
    return b_gate * y

def hgrn2(q, f_logit, i_in, g, lb, norm_g):
    B, T, H, d = q.shape
    dt = q.dtype
    z = f_logit.astype(jnp.float32)
    lb32 = lb.astype(jnp.float32)
    log_f = jnp.logaddexp(jnp.log(jnp.maximum(lb32, LB_FLOOR)), jnp.log1p(-lb32) + jax.nn.log_sigmoid(z))
    k = (1.0 - lb32) * jax.nn.sigmoid(-z)
    qs = q.astype(jnp.float32) * d ** -0.5
    v = i_in.astype(jnp.float32)
    nch = T // HGRN_CHUNK

    def chunks(a):
        return a.reshape(B, nch, HGRN_CHUNK, H, d).transpose(1, 0, 3, 2, 4)

    causal = jnp.tril(jnp.ones((HGRN_CHUNK, HGRN_CHUNK), dtype=bool))[:, :, None]

    def step(S, inp):
        qc, kc, vc, lfc = inp
        b = jnp.cumsum(lfc, axis=2)
        diff = b[:, :, :, None, :] - b[:, :, None, :, :]
        decay = jnp.where(causal, jnp.exp(jnp.where(causal, diff, 0.0)), 0.0)
        a = jnp.einsum('bhtd,bhsd,bhtsd->bhts', qc, kc, decay)
        o = jnp.einsum('bhts,bhse->bhte', a, vc) + jnp.einsum('bhtd,bhde->bhte', qc * jnp.exp(b), S)
        b_last = b[:, :, -1:, :]
        S = jnp.exp(b_last[:, :, 0, :])[..., None] * S + jnp.einsum('bhsd,bhse->bhde', kc * jnp.exp(b_last - b), vc)
        return S, o

    S0 = jnp.zeros((B, H, d, d), jnp.float32)
    _, o = lax.scan(step, S0, (chunks(qs), chunks(k), chunks(v), chunks(log_f)))
    o = o.transpose(1, 0, 3, 2, 4).reshape(B, T, H, d)
    o = o * lax.rsqrt(jnp.mean(o * o, axis=-1, keepdims=True) + RMS_EPS) * norm_g.astype(jnp.float32)
    o = o * jax.nn.silu(g.astype(jnp.float32))
    return o.reshape(B, T, H * d).astype(dt)

def cross_attention(xn, mem_n, wq, wkv, wo):
    B, T, _ = xn.shape
    M = mem_n.shape[1]
    q = jnp.dot(xn, wq).reshape(B, T, CROSS_HEADS, HEAD_DIM)
    k, v = jnp.split(jnp.dot(mem_n, wkv).reshape(B, M, 2 * CROSS_HEADS, HEAD_DIM), 2, axis=2)
    s = jnp.einsum('bqhd,bkhd->bhqk', q, k) * HEAD_DIM ** -0.5
    p = jax.nn.softmax(s.astype(jnp.float32), axis=-1).astype(v.dtype)
    o = jnp.einsum('bhqk,bkhd->bqhd', p, v).reshape(B, T, CROSS_WIDTH)
    return jnp.dot(o, wo)

def hier_moe(xn, w_rg, b_rg, w_re, b_re, w_gu, w_dn):
    B, T, D = xn.shape
    n_tok = B * T
    xf = xn.reshape(n_tok, D)
    lg = jnp.dot(xf, w_rg).astype(jnp.float32) + b_rg.astype(jnp.float32)
    p_grp = jax.nn.softmax(lg, axis=-1)
    grp = jnp.argmax(lg, axis=-1)
    p_grp_sel = jnp.take_along_axis(p_grp, grp[:, None], axis=1)
    le = (jnp.dot(xf, w_re).astype(jnp.float32) + b_re.astype(jnp.float32)).reshape(n_tok, N_GROUPS, EXPERTS_PER_GROUP)
    le = jnp.take_along_axis(le, grp[:, None, None], axis=1)[:, 0]
    top_p, top_e = lax.top_k(jax.nn.softmax(le, axis=-1), EXPERT_TOP_K)
    gate = p_grp_sel * top_p / jnp.sum(top_p, axis=-1, keepdims=True)
    eid = (grp[:, None] * EXPERTS_PER_GROUP + top_e).reshape(-1)
    tok = jnp.arange(n_tok * EXPERT_TOP_K) // EXPERT_TOP_K
    order = jnp.argsort(eid)
    tok_s = tok[order]
    sizes = jnp.bincount(eid, length=N_EXPERTS).astype(jnp.int32)
    xs = xf[tok_s]
    gu = lax.ragged_dot(xs, w_gu, sizes)
    g_, u_ = jnp.split(gu, 2, axis=-1)
    ys = lax.ragged_dot(jax.nn.silu(g_) * u_, w_dn, sizes)
    ys = ys * gate.reshape(-1)[order][:, None].astype(ys.dtype)
    return jnp.zeros_like(xf).at[tok_s].add(ys).reshape(B, T, D)

def setup_inputs(seed: int = 0) -> dict:
    key = jax.random.key(seed)
    ks = jax.random.split(key, 24)
    f32 = jnp.float32

    def nrm(k, shape, scale):
        return jax.random.normal(k, shape, f32) * scale

    def gain(k, shape):
        return 1.0 + 0.1 * jax.random.normal(k, shape, f32)

    D = D_MODEL
    return {
        'x': nrm(ks[0], (BATCH, SEQ, D), 1.0),
        'mem': nrm(ks[1], (BATCH, MEM_LEN, D), 1.0),
        'w_in': nrm(ks[2], (DEPTH, D, IN_WIDTH), D ** -0.5),
        'conv_w': nrm(ks[3], (DEPTH, CONV_K, CONV_WIDTH), CONV_K ** -0.5),
        'cmp_pe': nrm(ks[4], (DEPTH, 2, CMP_LEN, HEAD_DIM), 0.02),
        'cmp_w1': nrm(ks[5], (DEPTH, 2, CMP_LEN * HEAD_DIM, CMP_HIDDEN), (CMP_LEN * HEAD_DIM) ** -0.5),
        'cmp_w2': nrm(ks[6], (DEPTH, 2, CMP_HIDDEN, HEAD_DIM), CMP_HIDDEN ** -0.5),
        'hgrn_lb_logits': nrm(ks[7], (DEPTH, HGRN_WIDTH), 1.0),
        'hgrn_norm': gain(ks[8], (DEPTH, HGRN_WIDTH)),
        'w_out': nrm(ks[9], (DEPTH, MIX_WIDTH, D), MIX_WIDTH ** -0.5),
        'cross_wq': nrm(ks[10], (DEPTH, D, CROSS_WIDTH), D ** -0.5),
        'cross_wkv': nrm(ks[11], (DEPTH, D, 2 * CROSS_WIDTH), D ** -0.5),
        'cross_wo': nrm(ks[12], (DEPTH, CROSS_WIDTH, D), CROSS_WIDTH ** -0.5),
        'router_group_w': nrm(ks[13], (DEPTH, D, N_GROUPS), D ** -0.5),
        'router_group_b': nrm(ks[14], (DEPTH, N_GROUPS), 0.01),
        'router_expert_w': nrm(ks[15], (DEPTH, D, N_EXPERTS), D ** -0.5),
        'router_expert_b': nrm(ks[16], (DEPTH, N_EXPERTS), 0.01),
        'expert_w_gate_up': nrm(ks[17], (DEPTH, N_EXPERTS, D, 2 * D_EXPERT), D ** -0.5),
        'expert_w_down': nrm(ks[18], (DEPTH, N_EXPERTS, D_EXPERT, D), D_EXPERT ** -0.5),
        'norm_mix': gain(ks[19], (DEPTH, D)),
        'norm_cross': gain(ks[20], (DEPTH, D)),
        'norm_mem': gain(ks[21], (DEPTH, D)),
        'norm_ffn': gain(ks[22], (DEPTH, D)),
        'norm_final': gain(ks[23], (D,)),
    }

def reference(x, mem, w_in, conv_w, cmp_pe, cmp_w1, cmp_w2, hgrn_lb_logits, hgrn_norm, w_out,
              cross_wq, cross_wkv, cross_wo, router_group_w, router_group_b, router_expert_w,
              router_expert_b, expert_w_gate_up, expert_w_down, norm_mix, norm_cross, norm_mem,
              norm_ffn, norm_final):
    B, T, _ = x.shape
    pos = jnp.arange(T)
    p_lb = jax.nn.softmax(hgrn_lb_logits.astype(jnp.float32), axis=0)
    lower_bounds = jnp.cumsum(p_lb, axis=0) - p_lb[0:1]
    h = x
    for l in range(DEPTH):
        xn = rmsnorm(h, norm_mix[l])
        (q, kc, vc, ksl, vsl, kwn, vwn, gl, cb, cc, ch,
         hq, hf, hi, hg) = jnp.split(jnp.dot(xn, w_in[l]), IN_OFFSETS, axis=-1)
        q = q.reshape(B, T, NSA_KV_HEADS, NSA_GROUP, HEAD_DIM)
        q_rot = rope(q, pos)
        kvh = (B, T, NSA_KV_HEADS, HEAD_DIM)
        kc = nsa_compress(kc.reshape(kvh), cmp_pe[l, 0], cmp_w1[l, 0], cmp_w2[l, 0])
        vc = nsa_compress(vc.reshape(kvh), cmp_pe[l, 1], cmp_w1[l, 1], cmp_w2[l, 1])
        ksl = rope(ksl.reshape(kvh), pos)
        kwn = rope(kwn.reshape(kvh), pos)
        gate = gl.reshape(B, T, NSA_KV_HEADS, NSA_GROUP, 3)
        o_nsa = nsa_attention(q, q_rot, gate, kc, vc, ksl, vsl.reshape(kvh), kwn, vwn.reshape(kvh))
        o_conv = short_conv(cb, cc, ch, conv_w[l])
        hh = (B, T, HGRN_HEADS, HEAD_DIM)
        o_hgrn = hgrn2(hq.reshape(hh), hf.reshape(hh), hi.reshape(hh), hg.reshape(hh),
                       lower_bounds[l].reshape(HGRN_HEADS, HEAD_DIM), hgrn_norm[l].reshape(HGRN_HEADS, HEAD_DIM))
        h = h + jnp.dot(jnp.concatenate([o_nsa, o_conv, o_hgrn], axis=-1), w_out[l])
        h = h + cross_attention(rmsnorm(h, norm_cross[l]), rmsnorm(mem, norm_mem[l]),
                                cross_wq[l], cross_wkv[l], cross_wo[l])
        h = h + hier_moe(rmsnorm(h, norm_ffn[l]), router_group_w[l], router_group_b[l],
                         router_expert_w[l], router_expert_b[l], expert_w_gate_up[l], expert_w_down[l])
    return rmsnorm(h, norm_final)


_drawn_inputs = setup_inputs


def setup_inputs(seed=0):
    import zlib

    import numpy as np

    out = dict(_drawn_inputs(seed))
    spreads = {}
    factors = {'cmp_pe': 2.998, 'router_group_b': 4.522}
    for name, (base, spread) in spreads.items():
        noise = np.random.default_rng([zlib.crc32(name.encode()), seed]).standard_normal(out[name].shape)
        drawn = base * np.exp(spread * noise) if base else spread * noise
        out[name] = jnp.asarray(drawn.astype(out[name].dtype))
    for name, factor in factors.items():
        out[name] = (out[name] * factor).astype(out[name].dtype)
    return out
```

```python
from contextlib import ExitStack

import concourse.bass as bass
from concourse import mybir

F32 = mybir.dt.float32
BF16 = mybir.dt.bfloat16
U8 = mybir.dt.uint8
I32 = mybir.dt.int32
ALU = mybir.AluOpType
ACT = mybir.ActivationFunctionType
AX = mybir.AxisListType.X

P = 128
D = 1024
EPS = 1e-6
LB_FLOOR = 1e-30
HD = 64
KV = 2
GRP = 4
NCMP = 16
TOP_IDX = 1000.0
SLOTS = 64

C_KC, C_KS, C_KW, C_GL = 512, 768, 1024, 1280
C_CB, C_CH, C_HQ, C_HF, C_HG, C_END = 1304, 1816, 2072, 2328, 2840, 3096

HALVES = [1, 2, 4, 8, 16, 32, 64]

PROJECT = (["memk", "memv"] + [f"xT{j}" for j in range(4)] + ["hf", "hi", "hq", "ch", "q0", "q1"]
           + ["dg_0", "dg_1", "rq0", "rq1", "ckv", "ksvs", "lv1_0", "lv1_1", "cmph", "lv2_0", "lv2_1"]
           + ["kwvw", "gl", "cmpo", "lv4_0", "lv4_1", "rk", "cb", "lv8_0", "lv8_1", "cc", "hg", "lv16_0", "lv16_1"]
           + ["lv32_0", "lv32_1", "lv64_0", "lv64_1", "off_0", "off_1"])
GROUPS = [(br, tt, i, n) for br in ("sel", "win") for tt, i, n in ((0, 0, 4), (1, 0, 2), (1, 2, 2))]
NN = len(GROUPS)
GROUPS += [("cross", tt, 0, 2) for tt in range(2)]
NG = len(GROUPS)
USES = {
    0: PROJECT[0::2] + ["s0_0", "av", "s2_0", "s4_0", "wo0", "wo2", "yT0", "yT2", "cq", "s6_0", "co0", "co2",
                        "zT0", "zT2", "rt"],
    1: PROJECT[1::2] + ["s0_1", "s2_1", "hot", "s4_1", "wo1", "wo3", "yT1", "yT3", "s6_1", "co1", "co3",
                        "zT1", "zT3", "pos"],
    2: ["cmp_s_0"] + [f"s{n}_0" for n in range(1, NG, 2)],
    3: ["cmp_s_1"] + [f"s{n}_1" for n in range(1, NG, 2)],
    4: ["cmp_t"] + [f"t{n}_0" for n in range(NG)],
    5: [f"t{n}_1" for n in range(NG)],
    6: ["o6", "cross_o"],
    7: ["o7"],
}
PLACE = {name: (b, n) for b, names in USES.items() for n, name in enumerate(names)}

DVE_STEPS, POOL_STEPS = 165, 21

LAST_USE = ["memv", "hi", "ch", "q1", "ksvs", "cmph", "cmpo", "cc", "hg", "wo1", "wo3", "co3"]
N_SETUP = 5


def flat(ap):
    names = "abc"[:len(ap.shape) - 1]
    return ap if len(names) == 1 else ap.rearrange(f"p {' '.join(names)} -> p ({' '.join(names)})")



def hymba(nc, L, x, mem, w_q, w_in, cmp_w1, cmp_w2, w_out, wq, wkv, wo, w_gu, w_dn, norm_final,
          params, lb_logits, consts, masks, out):
    T = 256
    DEPTH = L
    E = w_gu.shape[1]
    PAIRS = E // 2
    MAXP = T // SLOTS
    NPAR = params.shape[2]

    ctx = ExitStack()
    with ctx:
        def sb(name, shape, dt=F32):
            return ctx.enter_context(nc.sbuf_tensor(name, shape, dt))

        def sem(name):
            return ctx.enter_context(nc.semaphore(name))

        banks = [ctx.enter_context(nc.psum_tensor(f"bank{b}", [P, 512], F32)) for b in range(8)]

        h = sb("h", [P, 2, 1024])
        memT = sb("memT", [P, 8, 256])
        xnT = sb("xnT", [P, 8, 256])
        xhat = sb("xhat", [P, 2, 1024])
        cst = sb("cst", [P, consts.shape[1]])
        cbf = sb("cbf", [P, 288], BF16)
        lvmask = sb("lvmask", [P, 8, 128], U8)
        par = sb("par", [P, DEPTH, NPAR])
        lb_in = sb("lb_in", [P, DEPTH, 2])
        lbf = sb("lbf", [P, DEPTH, 2])
        oml = sb("oml", [P, DEPTH, 2])
        small = sb("small", [P, 254])
        COLS = MAXP * E + 2
        posv = sb("posv", [P, 2, COLS])
        gates = sb("gates", [P, 2, COLS])
        npass_i = sb("npass_i", [1, 2], I32)
        dense = sb("dense", [P, 3, 4096])
        ring = sb("ring", [P, 3, 4096])
        share = sb("share", [P, 12288])
        rest = sb("rest", [P, 4352])

        ident = cst[:, 0:128]
        perm = cst[:, 128:256]
        tri = cst[:, 256:384]
        ones = cst[:, 384:512]
        cos = cst[:, 512:768]
        sin = cst[:, 768:1024]
        iota_slot = cst[:, 1024:1024 + SLOTS]
        iota_g = cst[:, 1088:1092]
        iota_e = cst[:, 1092:1124]
        cmp_ok = cst[:, 1124:1156].rearrange("p (t c) -> p t c", t=2)
        own_block = cst[:, 1156:1164].rearrange("p (i v) -> p i v", v=2)
        ident_b = cbf[:, 0:128]
        causal_b = cbf[:, 128:256]
        cmp_no_b = cbf[:, 256:288].rearrange("p (t c) -> p t c", t=2)

        def pcol(l, a, n):
            return par[:, l, a:a + n]
        G_MIX, G_CROSS, G_MEM, G_FFN, CONVW, PE_C, HNORM, RBIAS, RW = 0, 8, 16, 24, 32, 38, 70, 72, 108

        def cut(t, sizes):
            at, views = 0, []
            for n in sizes:
                views.append(t[:, at:at + n])
                at += n
            assert at <= t.shape[1], at
            return views

        def two(ap):
            return ap.rearrange("p (c t) -> p c t", c=2)

        (f_b, g_b, q_b, k_b, qt0_b, qt1_b, kt0_b, kt1_b, tot, a0_b, a1_b, ao_b, hi_b, hgr_b) = cut(
            share[:, 0:7168], [512] * 14)
        (qraw_b, qrot_b, kraw_b, krot_b, tmp, vv, vblk_b, hgs_b) = cut(
            share[:, 7168:12288], [1024, 1024, 512, 512, 512, 512, 512, 512])
        f_, g_, q_, k_ = two(f_b), two(g_b), two(q_b), two(k_b)
        qt_b, kt_b = [qt0_b, qt1_b], [kt0_b, kt1_b]
        qt, kt = [two(qt0_b), two(qt1_b)], [two(kt0_b), two(kt1_b)]
        a01 = share[:, 4608:5632].rearrange("p (n h t) -> p n h t", n=4, h=2)
        A_ = [t.rearrange("p (h t) -> p h t", h=4) for t in (a0_b, a1_b, ao_b)]
        hi_ = two(hi_b)
        qraw = qraw_b.rearrange("p (i t) -> p i t", i=GRP)
        qrot = qrot_b.rearrange("p (i t) -> p i t", i=GRP)
        kraw, krot = two(kraw_b), two(krot_b)
        v_of = {"sel": two(vv[:, 0:256]), "win": two(vv[:, 256:512])}
        vblk = vblk_b.rearrange("p (i c) -> p i c", i=GRP)
        kcv = hgr_b.rearrange("p (s v u) -> p s v u", s=2, v=KV)
        mask_in = rest[:, 0:1024].rearrange("p (m t) -> p m t", m=8)
        memG = share[:, 8192:10240].rearrange("p (k t) -> p k t", k=8)
        mem_raw = two(share[:, 0:2048])
        mem_sq = two(share[:, 2048:4096])

        (cvb_b, cvc_b, cvh_b, cvy_b) = cut(rest[:, 0:2048], [512] * 4)
        cv_b, cv_c, cv_h, cv_y = two(cvb_b), two(cvc_b), two(cvh_b), two(cvy_b)
        cv_u = two(rest[:, 2048:2048 + 516])
        memk, memv, cq = [two(rest[:, 2564 + 512 * n:3076 + 512 * n]) for n in range(3)]
        coT = cv_b

        flatx = xnT[:, :, :].rearrange("p k t -> p (k t)")
        pT = flatx[:, 1024:2048]

        def probs(n):
            if n % 2 == 1:
                return flatx[:, 0:1024]
            return share[:, 2048:3072] if n < NN else rest[:, 1024:2048]

        cmpP = flatx[:, 0:256]
        mixT = xhat[:, :, :].rearrange("p a b -> p (a b)").rearrange("p (k t) -> p k t", k=8)
        cmp_x = sb("cmp_x", [P, 2, KV, NCMP - 1])
        cmp_e = sb("cmp_e", [P, 2, KV, NCMP - 1])
        cmp_hk = sb("cmp_hk", [P, KV, NCMP])
        cmp_hv = sb("cmp_hv", [P, GRP, KV * NCMP])
        kc = sb("kc", [P, NCMP])
        gate = sb("gate", [P, 2, 24])
        cvw = sb("cvw", [P, 6])
        (ssq, rs, hsum, hrs, pe2, lbt, cmx, csum, crr) = cut(small[:, 0:100], [2, 2, 8, 8, 2, 24, 16, 16, 16])
        att_mx, att_nb, att_sum, att_rr = [
            [small[:, 190 + 16 * n + 8 * b:198 + 16 * n + 8 * b] for b in range(2)] for n in range(4)]
        scratch = small[:, 136:172]
        root_x, root_t = small[:, 172:180], small[:, 180:188]

        (xg_b, yt_b, ys_b, ht_b, pm_b, pg_b, pgt_b) = cut(rest[:, :], [1024, 1024, 1024, 512, 256, 256, 256])
        xg = xg_b.rearrange("p (k s) -> p k s", k=8)
        yt = yt_b.rearrange("p (k s) -> p k s", k=8)
        sgate = ys_b
        ht = ht_b.rearrange("p (e k s) -> p e k s", e=2, k=4)
        pm = pm_b.rearrange("p (t e s) -> p t e s", t=2, e=2)
        pg = pg_b.rearrange("p (t e s) -> p t e s", t=2, e=2)
        pgT = pgt_b
        def rtile(at, n):
            return ys_b[:, at:at + 2 * n].rearrange("p (t c) -> p t c", t=2)
        rl, rlog, r_in, r_out, r_o1, r_o2, chosen = [
            rtile(a, n) for a, n in ((0, 36), (72, 36), (144, 32), (208, 32), (272, 32), (336, 32), (400, 32))]
        rexp = rtile(464, 36)
        r_g1 = rtile(536, 4)
        r_mg, r_me, r_sg, r_e1, r_e2, r_t, r_min = [ys_b[:, 544 + 2 * i:546 + 2 * i] for i in range(7)]
        r_cnt, r_np = ys_b[:, 558:559], ys_b[:, 559:560]
        gain_row = memT[:, :, :].rearrange("p k t -> p (k t)")[:, 0:D]

        def eslot(s):
            return ring[:, s, :] if s < 3 else share[:, (s - 3) * 4096:(s - 2) * 4096]

        filled = [sem(f"bank{b}_filled") for b in range(8)]
        drained = [sem(f"bank{b}_drained") for b in range(8)]
        efilled = [sem(f"ebank{b}_filled") for b in range(8)]
        edrained = [sem(f"ebank{b}_drained") for b in range(8)]
        dloaded = [sem(f"dense{s}_loaded") for s in range(3)]
        eloaded = [sem(f"expert{s}_loaded") for s in range(6)]
        half_read = [sem(f"expert{e}_upper_half_read") for e in range(2)]
        events = {}

        def ev(name):
            if name not in events:
                events[name] = sem(name)
            return events[name]

        s_setup = sem("inputs_loaded")
        s_mem = sem("mem_loaded")
        s_gain = sem("final_gain_loaded")
        s_out = sem("out_stored")
        dve_step, pool_step, setup_step = sem("dve_step"), sem("pool_step"), sem("setup_step")
        onehot_ready, pg_ready, silu_ready = sem("onehot_ready"), sem("gated_onehot_ready"), sem("silu_ready")

        class Chain:

            def __init__(self, eng, semaphore, base, steps, apart=False):
                self.apart = apart
                self.eng, self.sem, self.base, self.n, self.steps = eng, semaphore, base, 0, steps

            def link(self, ins):
                self.n += 1
                ins.then_inc(self.sem, 1)
                self.eng.wait_ge(self.sem, self.base + self.n)
                if self.apart:
                    alone(self.eng)

            def close(self):
                assert self.n == self.steps, (str(self.sem), self.n, self.steps)

        def alone(eng):
            eng.nop(nofuse=True)

        def bank_free(eng, l, use):
            b, n = PLACE[use]
            eng.wait_ge(drained[b], l * len(USES[b]) + (n + 1))
            return banks[b]

        def bank_done(ins, use):
            ins.then_inc(filled[PLACE[use][0]], 1)

        def bank_full(eng, l, use):
            b, n = PLACE[use]
            eng.wait_ge(filled[b], l * len(USES[b]) + (n + 1))
            return banks[b]

        def bank_drained(ins, use):
            ins.then_inc(drained[PLACE[use][0]], 1)

        def wait_drained(eng, l, use):
            b, n = PLACE[use]
            eng.wait_ge(drained[b], l * len(USES[b]) + (n + 2))

        def kt_rows(w, a, b):
            return w.rearrange("(k p) c -> p k c", p=P)[:, :, a:b]

        def unit_view(s, n, c):
            return dense[:, s, 0:n * c].rearrange("p (k c) -> p k c", k=n)

        def unit_dmas(l, u):
            s = u % 3
            win = w_in[l]
            spans = {1: (C_HF, C_HG), 2: (C_CH, C_HF), 4: (C_KC, C_KW),
                     6: (C_KW, C_CB), 7: (C_CB, C_CH), 8: (C_HG, C_END)}
            if u == 0:
                return [(unit_view(s, 8, 512), kt_rows(wkv[l], 0, 512))]
            if u == 3:
                return [(unit_view(s, 8, 512), kt_rows(w_q[l], 0, 512))]
            if u in spans:
                a, b = spans[u]
                dmas = [(unit_view(s, 8, b - a), kt_rows(win, a, b))]
                if u == 6:
                    dmas.append((dense[:, s, 3968:4096], cmp_w2[l]))
                return dmas
            if u == 5:
                return [(dense[:, s, :], cmp_w1[l])]
            if u in (9, 10):
                return [(unit_view(s, 8, 512), kt_rows(w_out[l], (u - 9) * 512, (u - 8) * 512))]
            return [(dense[:, s, 0:2048].rearrange("p (k c) -> p k c", k=8), kt_rows(wq[l], 0, 256)),
                    (dense[:, s, 2048:4096].rearrange("p (k c) -> p k c", k=2), kt_rows(wo[l], 0, 1024))]

        N_DMA = [1, 1, 1, 1, 1, 1, 2, 1, 1, 1, 1, 2]

        def unit_loaded(eng, l, u):
            s = u % 3
            per = sum(N_DMA[s::3])
            upto = sum(N_DMA[i] for i in range(s, u + 1, 3))
            eng.wait_ge(dloaded[s], l * (16 * per) + 16 * upto)

        def expert_dmas(l, e, s):
            part = s % 3
            src = w_dn[l, e] if part == 2 else w_gu[l, e, part * 512:(part + 1) * 512, :]
            return eslot(s).rearrange("p (k c) -> p k c", k=4), src.rearrange("(k p) c -> p k c", p=P)

        block = ctx.enter_context(nc.Block())

        @block.sync
        def _(sp):
            sp.dma_start(mem_raw, mem.rearrange("(t p) d -> p t d", p=P)).then_inc(s_mem, 16)
            sp.dma_start(cst[:, :], consts).then_inc(s_setup, 16)
            sp.dma_start(par[:, :, :], params.rearrange("l p n -> p l n")).then_inc(s_setup, 16)
            sp.dma_start(h[:, :, :], x.rearrange("(t p) d -> p t d", p=P)).then_inc(s_setup, 16)
            sp.dma_start(rest[:, 0:1312], masks).then_inc(s_setup, 16)
            sp.dma_start(lb_in[:, :, :], lb_logits).then_inc(s_setup, 16)
            iters = sp.alloc_register("sp_iters")
            sp.reg_mov(iters, 0)
            with sp.Fori(0, DEPTH) as l:
                base = sp.snap(iters, min_val=0, max_val=DEPTH * MAXP * PAIRS)

                def load_unit(u):
                    s = u % 3
                    if u >= 3:
                        bank_full(sp, l, LAST_USE[u - 3])
                    for dst, src in unit_dmas(l, u):
                        sp.dma_start(dst, src).then_inc(dloaded[s], 16)

                def load_expert(e, s):
                    dst, src = expert_dmas(l, e, s)
                    sp.dma_start(dst, src).then_inc(eloaded[s], 16)

                for u in range(3):
                    load_unit(u)
                for s in range(3):
                    load_unit(3 + s)
                    load_expert(0, s)
                for u in range(6, 12):
                    load_unit(u)
                bank_full(sp, l, "wo0")
                for s in range(3, 6):
                    load_expert(1, s)
                sp.wait_ge(ev("npass_ready"), l + 1)
                alone(sp)
                npass = sp.value_load(npass_i[0:1, 0:1], min_val=1, max_val=MAXP)
                with sp.Fori(1, npass * PAIRS) as t:
                    pair = t % PAIRS
                    before = base + t
                    for e in range(2):
                        sp.wait_ge(half_read[e], before)
                        load_expert(pair * 2 + e, e * 3)
                        sp.wait_ge(efilled[2 + e], before * 2 - 1 if e == 0 else before)
                        load_expert(pair * 2 + e, e * 3 + 1)
                        sp.wait_ge(efilled[4 + e], before * 2 - 1)
                        load_expert(pair * 2 + e, e * 3 + 2)
                sp.reg_add(iters, iters, npass * PAIRS)
            sp.dma_start(gain_row, norm_final.partition_broadcast(P)).then_inc(s_gain, 16)
            sp.wait_ge(ev("out_ready"), 1)
            sp.dma_start(out.rearrange("(t p) d -> p t d", p=P), xhat[:, :, :]).then_inc(s_out, 16)
            sp.wait_ge(s_out, 16)

        @block.tensor
        def _(pe):
            def mm(out_ap, lhsT, rhs, start, stop):
                return pe.matmul(out_ap, lhsT=lhsT, rhs=rhs, start=start, stop=stop, skip_group_check=True)

            pe.wait_ge(s_setup, 16 * N_SETUP)
            pe.wait_ge(ev("mem_hat"), 2)
            for j in range(4):
                for d in range(2):
                    for tt in range(2):
                        ins = pe.transpose(banks[j][:, (d * 2 + tt) * P:(d * 2 + tt + 1) * P],
                                           mem_raw[:, tt, (2 * j + d) * P:(2 * j + d + 1) * P], ident)
            ins.then_inc(ev("mem_turned"), 1)

            iters = pe.alloc_register("pe_iters")
            pe.reg_mov(iters, 0)
            with pe.Fori(0, DEPTH) as l:
                base = pe.snap(iters, min_val=0, max_val=DEPTH * MAXP * PAIRS)

                def wait(name):
                    pe.wait_ge(ev(name), l + 1)

                def settled(*uses):
                    for use in {PLACE[use][0]: use for use in sorted(uses, key=lambda u: PLACE[u][1])}.values():
                        wait_drained(pe, l, use)

                def project_T(out_ap, lhsT_of, src, rhs_cols=slice(0, 256)):
                    for k in range(8):
                        ins = mm(out_ap, lhsT_of(k), src[:, k, rhs_cols], k == 0, k == 7)
                    return ins

                def project_N(out_ap, unit, c0, c1, src, tt):
                    for k in range(8):
                        ins = mm(out_ap, src[:, k, tt * P:(tt + 1) * P], unit[:, k, c0:c1], k == 0, k == 7)
                    return ins

                def two_T(use, unit, c0, src):
                    bk = bank_free(pe, l, use)
                    for c in range(2):
                        ins = project_T(bk[:, c * 256:(c + 1) * 256],
                                        lambda k: unit[:, k, c0 + c * P:c0 + (c + 1) * P], src)
                    bank_done(ins, use)

                def two_N(use, unit, c0, c1, src):
                    bk = bank_free(pe, l, use)
                    n = c1 - c0
                    for tt in range(2):
                        ins = project_N(bk[:, tt * n:(tt + 1) * n], unit, c0, c1, src, tt)
                    bank_done(ins, use)

                def turn(prefix, stage):
                    wait("xhat0_" + stage)
                    wait("xhat1_" + stage)
                    for j in range(4):
                        bk = bank_free(pe, l, f"{prefix}T{j}")
                        for d in range(2):
                            for tt in range(2):
                                ins = pe.transpose(bk[:, (d * 2 + tt) * P:(d * 2 + tt + 1) * P],
                                                   xhat[:, tt, (2 * j + d) * P:(2 * j + d + 1) * P], ident)
                        bank_done(ins, f"{prefix}T{j}")

                wait("memG")
                unit_loaded(pe, l, 0)
                u = unit_view(0, 8, 512)
                two_T("memk", u, 0, memG)
                two_N("memv", u, 256, 512, memG)
                turn("x", "mix")
                settled("xT0", "xT1", "xT2", "xT3")
                unit_loaded(pe, l, 1)
                u = unit_view(1, 8, 512)
                two_T("hf", u, 0, xnT)
                two_N("hi", u, 256, 512, xnT)
                unit_loaded(pe, l, 2)
                u = unit_view(2, 8, 512)
                two_T("hq", u, C_HQ - C_CH, xnT)
                two_T("ch", u, 0, xnT)
                unit_loaded(pe, l, 3)
                u = unit_view(0, 8, 512)
                for use, i0 in (("q0", 0), ("q1", 2)):
                    bk = bank_free(pe, l, use)
                    for i in range(2):
                        ins = project_T(bk[:, i * 256:(i + 1) * 256],
                                        lambda k: u[:, k, (i0 + i) * P:(i0 + i + 1) * P], xnT)
                    bank_done(ins, use)

                def level(name, kk, qq):
                    bks = [bank_free(pe, l, f"{name}_{half}") for half in range(2)]
                    for n in range(4):
                        cols = slice((n // 2) * P, (n // 2 + 1) * P)
                        for half in range(2):
                            ch = slice(half * HD, (half + 1) * HD)
                            ins = mm(bks[half][:, n * P:(n + 1) * P], kk[ch, n % 2, cols], qq[ch, n % 2, cols],
                                     True, True)
                            if n == 3:
                                bank_done(ins, f"{name}_{half}")

                def half_level(L):
                    i = HALVES.index(L)
                    wait(f"qt{L}")
                    if L > 1:
                        wait(f"kt{L}")
                    level(f"lv{L}", k_ if L == 1 else kt[i % 2], qt[i % 2])

                def swap(use, src, c0):
                    bk = bank_free(pe, l, use)
                    bank_done(mm(bk[:, 0:512], perm, src[:, c0:c0 + 512], True, True), use)

                wait("k_ready")
                settled("hq")
                level("dg", k_, q_)
                settled("q0", "q1")
                swap("rq0", qraw_b, 0)
                swap("rq1", qraw_b, 512)

                unit_loaded(pe, l, 4)
                u = unit_view(1, 8, 512)
                xpar = xnT[:, :, :].rearrange("p k (u r) -> p k r u", r=2)
                bk = bank_free(pe, l, "ckv")
                for s in range(2):
                    for v in range(KV):
                        for r in range(2):
                            cols = s * P + v * HD
                            for k in range(8):
                                ins = mm(bk[r * HD:(r + 1) * HD, (s * KV + v) * P:(s * KV + v + 1) * P],
                                         u[:, k, cols:cols + HD], xpar[:, k, r, :], k == 0, k == 7)
                bank_done(ins, "ckv")

                def key_value(use, unit, c0):
                    bk = bank_free(pe, l, use)
                    project_T(bk[:, 0:256], lambda k: unit[:, k, c0:c0 + P], xnT)
                    for tt in range(2):
                        ins = project_N(bk[:, 256 + tt * P:256 + (tt + 1) * P], unit, c0 + P, c0 + 2 * P, xnT, tt)
                    bank_done(ins, use)

                key_value("ksvs", u, C_KS - C_KC)
                half_level(1)

                unit_loaded(pe, l, 5)
                settled("ckv")
                bk = bank_free(pe, l, "cmph")
                for s in range(2):
                    w1 = dense[:, 2, s * 2048:(s + 1) * 2048].rearrange("p (k c) -> p k c", k=16)
                    kpair = kcv[:, s, :, :]
                    for a in range(16):
                        ins = mm(bk[:, s * 32:s * 32 + 30].rearrange("p (v c) -> p v c", v=KV), w1[:, a, :],
                                 kpair[:, :, a:a + 8 * 14 + 1:8], a == 0, a == 15)
                    for a in range(16):
                        c = PE_C + s * 16 + a
                        ins = mm(bk[:, 64 + s:65 + s], w1[:, a, :], pcol(l, c, 1), a == 0, a == 15)
                bank_done(ins, "cmph")
                half_level(2)

                unit_loaded(pe, l, 6)
                u = unit_view(0, 8, C_CB - C_KW)
                key_value("kwvw", u, 0)
                two_N("gl", u, C_GL - C_KW, C_CB - C_KW, xnT)

                wait("cmp_hid")
                w2 = dense[:, 0, 3968:4096].rearrange("p (a d) -> p a d", a=2)
                bk = bank_free(pe, l, "cmpo")
                for v in range(KV):
                    mm(bk[v * HD:(v + 1) * HD, 0:NCMP], w2[:, 0, :], cmp_hk[:, v, :], True, True)
                ins = mm(bk[:, 64:64 + P].rearrange("p (v d) -> p v d", v=KV),
                         cmp_hv[:, :, :].rearrange("p i c -> p (i c)"),
                         w2[:, 1, :].unsqueeze(1).broadcast_to([P, KV, HD]), True, True)
                bank_done(ins, "cmpo")

                half_level(4)
                settled("ksvs", "kwvw")
                swap("rk", kraw_b, 0)
                unit_loaded(pe, l, 7)
                u = unit_view(1, 8, 512)
                two_T("cb", u, 0, xnT)
                half_level(8)
                two_T("cc", u, 256, xnT)
                unit_loaded(pe, l, 8)
                two_N("hg", unit_view(2, 8, 256), 0, 256, xnT)
                for L in (16, 32, 64):
                    half_level(L)

                wait("qt128")
                wait("kt128")
                bks = [bank_free(pe, l, f"off_{half}") for half in range(2)]
                for c in range(2):
                    for half in range(2):
                        ch = slice(half * HD, (half + 1) * HD)
                        ins = mm(bks[half][:, c * P:(c + 1) * P], kt[1][ch, c, 0:P], qt[1][ch, c, P:256], True, True)
                        if c == 1:
                            bank_done(ins, f"off_{half}")

                def scores(n):
                    bks = [bank_free(pe, l, f"s{n}_{v}") for v in range(2)]
                    br, tt, i0, nh = GROUPS[n]
                    nk = 512 // nh
                    for j in range(nh):
                        for v in range(2):
                            ch = slice(v * HD, (v + 1) * HD)
                            o = bks[v][:, j * nk:(j + 1) * nk]
                            if br == "cross":
                                ins = mm(o, cq[ch, j, tt * P:(tt + 1) * P], memk[ch, j, :], True, True)
                                if j == nh - 1:
                                    bank_done(ins, f"s{n}_{v}")
                            else:
                                mm(o, qrot[ch, i0 + j, tt * P:(tt + 1) * P],
                                   krot[ch, 0 if br == "sel" else 1, 0:nk], j == 0, False)
                    if br == "cross":
                        return
                    for v in range(2):
                        for j in range(nh):
                            ins = mm(bks[v][:, (j + 1) * nk - P:(j + 1) * nk], ident_b, causal_b, False, True)
                        bank_done(ins, f"s{n}_{v}")

                def turn_probs(n):
                    pe.wait_ge(ev("p_scaled"), l * NG + (n + 1))
                    for v in range(2):
                        bk = bank_free(pe, l, f"t{n}_{v}")
                        for c in range(4):
                            at = v * 512 + c * P
                            ins = pe.transpose(bk[:, c * P:(c + 1) * P], probs(n)[:, at:at + P], ident)
                        bank_done(ins, f"t{n}_{v}")

                def values(n):
                    wait_drained(pe, l, f"t{n}_0")
                    wait_drained(pe, l, f"t{n}_1")
                    br, tt, i0, nh = GROUPS[n]
                    nkt = 4 // nh
                    for j in range(nh):
                        for v in range(2):
                            for c in range(nkt):
                                at = v * 512 + (j * nkt + c) * P
                                if br == "cross":
                                    o = banks[6][v * HD:(v + 1) * HD, j * 256 + tt * P:j * 256 + (tt + 1) * P]
                                    vals = memv[:, c, (2 * j + v) * HD:(2 * j + v + 1) * HD]
                                    ins = mm(o, vals, pT[:, at:at + P], c == 0, c == 1)
                                else:
                                    i = i0 + j
                                    o = banks[6 + i // 2][v * HD:(v + 1) * HD,
                                                          (i % 2) * 256 + tt * P:(i % 2) * 256 + (tt + 1) * P]
                                    ins = mm(o, v_of[br][:, c, v * HD:(v + 1) * HD], pT[:, at:at + P], False,
                                             c == nkt - 1)
                    if n == NN - 2:
                        bank_done(ins, "o6")
                    if n == NN - 1:
                        bank_done(ins, "o7")
                    if n == NG - 1:
                        bank_done(ins, "cross_o")

                settled("cmpo")
                bks = [bank_free(pe, l, f"cmp_s_{v}") for v in range(KV)]
                for tt in range(2):
                    for i in range(GRP):
                        for v in range(KV):
                            ch = slice(v * HD, (v + 1) * HD)
                            at = (tt * GRP + i) * NCMP
                            mm(bks[v][:, at:at + NCMP], qraw[ch, i, tt * P:(tt + 1) * P], kc[ch, :],
                               tt == i == 0, False)
                for v in range(KV):
                    for tt in range(2):
                        ins = mm(bks[v][:, tt * 64:(tt + 1) * 64].rearrange("p (g c) -> p g c", c=NCMP), ident_b,
                                 cmp_no_b[:, tt, :].unsqueeze(1).broadcast_to([P, GRP, NCMP]), False, tt == 1)
                    bank_done(ins, f"cmp_s_{v}")
                wait("krot")
                wait("qrot")
                scores(0)

                settled("off_0", "off_1", "hi")
                bk = bank_free(pe, l, "av")
                settled("lv64_0", "lv64_1")
                for hd in range(4):
                    e = slice(hd * HD, (hd + 1) * HD)
                    mm(bk[:, hd * HD:(hd + 1) * HD], A_[0][:, hd, :], hi_[:, 0, e], True, True)
                    mm(bk[:, 256 + hd * HD:256 + (hd + 1) * HD], A_[2][:, hd, :], hi_[:, 0, e], True, False)
                    ins = mm(bk[:, 256 + hd * HD:256 + (hd + 1) * HD], A_[1][:, hd, :], hi_[:, 1, e], False, True)
                bank_done(ins, "av")

                wait("cmp_p")
                bk = bank_free(pe, l, "cmp_t")
                for tt in range(2):
                    ins = pe.transpose(bk[:, tt * P:(tt + 1) * P], cmpP[:, tt * P:(tt + 1) * P], ident)
                bank_done(ins, "cmp_t")
                scores(1)
                settled("cmp_t")
                bank_free(pe, l, "o6")
                bank_free(pe, l, "o7")
                for i in range(GRP):
                    mm(banks[6 + i // 2][:, (i % 2) * 256:(i % 2 + 1) * 256], vblk[:, i, :], pT[:, 0:256],
                       i % 2 == 0, False)
                turn_probs(0)
                for n in range(1, NN):
                    if n + 1 < NN:
                        scores(n + 1)
                    if n == 2:
                        wait("hgrn_o")
                        bk = bank_free(pe, l, "hot")
                        for c in range(2):
                            for tt in range(2):
                                ins = pe.transpose(bk[:, (c * 2 + tt) * P:(c * 2 + tt + 1) * P],
                                                   kt1_b[:, tt * 256 + c * P:tt * 256 + (c + 1) * P], ident)
                        bank_done(ins, "hot")
                    values(n - 1)
                    turn_probs(n)
                values(NN - 1)

                def out_proj(prefix, kk, lhs, rhs_of):
                    for n in range(2):
                        for tt in range(2):
                            bk = bank_free(pe, l, f"{prefix}{n * 2 + tt}")
                            for k in range(kk):
                                ins = mm(bk[:, 0:512], lhs[:, k, tt * P:(tt + 1) * P], rhs_of(n, k), k == 0, k == kk - 1)
                            bank_done(ins, f"{prefix}{n * 2 + tt}")

                wait("conv_done")
                settled("hot", "o6", "o7")
                unit_loaded(pe, l, 9)
                unit_loaded(pe, l, 10)
                out_proj("wo", 8, mixT, lambda n, k: unit_view(n, 8, 512)[:, k, :])

                turn("y", "cross")
                settled("yT0", "yT1", "yT2", "yT3")
                unit_loaded(pe, l, 11)
                two_T("cq", dense[:, 2, 0:2048].rearrange("p (k c) -> p k c", k=8), 0, xnT)
                settled("cq")
                bank_free(pe, l, "cross_o")
                for n in range(NN, NG):
                    scores(n)
                for n in range(NN, NG):
                    turn_probs(n)
                    values(n)
                settled("cross_o")
                wo_v = dense[:, 2, 2048:4096].rearrange("p (k c) -> p k c", k=2)
                out_proj("co", 2, coT, lambda n, k: wo_v[:, k, n * 512:(n + 1) * 512])

                turn("z", "ffn")
                settled("zT0", "zT1", "zT2", "zT3")
                bk = bank_free(pe, l, "rt")
                for tt in range(2):
                    for k in range(8):
                        ins = mm(bk[:, tt * 36:(tt + 1) * 36], xnT[:, k, tt * P:(tt + 1) * P],
                                 pcol(l, RW + k * 36, 36), k == 0, k == 7)
                bank_done(ins, "rt")
                wait("chosen")
                bk = bank_free(pe, l, "pos")
                mm(bk[:, 0:E], tri, chosen[:, 0, :], True, True)
                mm(bk[:, E:2 * E], ones, chosen[:, 0, :], True, False)
                mm(bk[:, E:2 * E], tri, chosen[:, 1, :], False, True)
                mm(bk[:, 2 * E:3 * E], ones, chosen[:, 0, :], True, False)
                ins = mm(bk[:, 2 * E:3 * E], ones, chosen[:, 1, :], False, True)
                bank_done(ins, "pos")

                for b in range(8):
                    wait_drained(pe, l, USES[b][-1])
                wait("npass_ready")
                alone(pe)
                npass = pe.value_load(npass_i[0:1, 0:1], min_val=1, max_val=MAXP)
                gbase = base + l

                def gather(n):
                    pe.wait_ge(onehot_ready, gbase + n + 1)
                    for b in range(2):
                        pe.wait_ge(edrained[b], gbase + n + 1)
                    for d in range(8):
                        for tt in range(2):
                            ins = mm(banks[d // 4][:, (d % 4) * P:(d % 4 + 1) * P], xhat[:, tt, d * P:(d + 1) * P],
                                     pm[:, tt, :, :].rearrange("p e s -> p (e s)"), tt == 0, tt == 1)
                        if d % 4 == 3:
                            ins.then_inc(efilled[d // 4], 1)

                gather(0)
                with pe.Fori(0, npass * PAIRS) as t:
                    it = base + t
                    for b in range(2):
                        pe.wait_ge(edrained[b], gbase + t + 2)
                    for e in range(2):
                        bk = banks[2 + e]
                        pe.wait_ge(edrained[2 + e], it * 2 + 1 if e == 0 else it + 1)
                        for k in range(8):
                            s = e * 3 + k // 4
                            if k % 4 == 0:
                                pe.wait_ge(eloaded[s], it * 16 + 16)
                            for m in range(8):
                                w = eslot(s)[:, (k % 4) * 1024 + m * P:(k % 4) * 1024 + (m + 1) * P]
                                ins = mm(bk[:, m * SLOTS:(m + 1) * SLOTS], w, xg[:, k, e * SLOTS:(e + 1) * SLOTS],
                                         k == m == 0, k == 7)
                            if k == 3:
                                ins.then_inc(half_read[e], 1)
                        ins.then_inc(efilled[2 + e], 1)
                    gather(t + 1)
                    for e in range(2):
                        bk = banks[4 + e]
                        pe.wait_ge(edrained[2 + e], it * 2 + 2 if e == 0 else it + 2)
                        pe.wait_ge(edrained[4 + e], it * 2 + 1)
                        s = e * 3 + 2
                        pe.wait_ge(eloaded[s], it * 16 + 16)
                        for k in range(4):
                            for m in range(8):
                                w = eslot(s)[:, k * 1024 + m * P:k * 1024 + (m + 1) * P]
                                ins = mm(bk[:, m * SLOTS:(m + 1) * SLOTS], w, ht[:, e, k, :], k == m == 0, k == 3)
                        ins.then_inc(efilled[4 + e], 1)
                    pe.wait_ge(pg_ready, it + 1)
                    for tt in range(2):
                        ins = pe.transpose(banks[2][:, tt * P:(tt + 1) * P],
                                           pg[:, tt, :, :].rearrange("p e s -> p (e s)"), ident)
                    ins.then_inc(efilled[2], 1)
                    for e in range(2):
                        pe.wait_ge(edrained[4 + e], it * 2 + 2)
                    for n in range(2):
                        pe.wait_ge(edrained[6 + n], it * 2 + 1)
                        for d in range(4):
                            ins = pe.transpose(banks[6 + n][:, d * P:(d + 1) * P], yt[:, n * 4 + d, :], ident)
                        ins.then_inc(efilled[6 + n], 1)
                    pe.wait_ge(edrained[2], it * 2 + 3)
                    for n in range(2):
                        pe.wait_ge(edrained[6 + n], it * 2 + 2)
                    for tt in range(2):
                        for n in range(2):
                            b = (6 if tt == 0 else 4) + n
                            mm(banks[b][:, 0:512], pgT[:, tt * P:(tt + 1) * P], ys_b[:, n * 512:(n + 1) * 512],
                               True, True).then_inc(efilled[b], 1)
                end = base + npass * PAIRS
                for b in (0, 1):
                    pe.wait_ge(edrained[b], end + l + 2)
                for b in (2, 4, 5, 6, 7):
                    pe.wait_ge(edrained[b], end * 2 + 1)
                pe.wait_ge(edrained[3], end + 1)
                pe.reg_add(iters, iters, npass * PAIRS)

        @block.scalar
        def _(act):
            def copy(out_ap, in_ap, scale=1.0):
                return act.activation(out_ap, in_ap, ACT.Copy, scale=scale)

            act.wait_ge(s_mem, 16)
            for tt in range(2):
                ins = act.activation(mem_sq[:, tt, :], mem_raw[:, tt, :], ACT.Square, accum_out=ssq[:, tt:tt + 1])
            ins.then_inc(ev("mem_squares"), 1)
            act.wait_ge(ev("lb_in"), 1)
            act.activation(flat(oml[:, :, :]), flat(lbf[:, :, :]), ACT.Exp).then_inc(ev("lb_exp"), 1)
            iters = act.alloc_register("act_iters")
            act.reg_mov(iters, 0)
            with act.Fori(0, DEPTH) as l:
                base = act.snap(iters, min_val=0, max_val=DEPTH * MAXP * PAIRS)

                def wait(name):
                    act.wait_ge(ev(name), l + 1)

                def drain(use, pairs):
                    bk = bank_full(act, l, use)
                    for out_ap, part, scale in pairs:
                        ins = copy(out_ap, part(bk), scale)
                    return ins

                def squares(stage):
                    wait("h_" + stage)
                    for tt in range(2):
                        ins = act.activation(xhat[:, tt, :], h[:, tt, :], ACT.Square, accum_out=ssq[:, tt:tt + 1])
                    ins.then_inc(ev("squares_" + stage), 1)

                def scale0(stage):
                    wait("rstd_" + stage)
                    act.activation(xhat[:, 0, :], h[:, 0, :], ACT.Identity,
                                   scale=rs[:, 0:1]).then_inc(ev("xhat0_" + stage), 1)

                def turned(prefix, gain):
                    for j in (1, 3):
                        bk = bank_full(act, l, f"{prefix}T{j}")
                        for d in range(2):
                            ins = act.activation(xnT[:, 2 * j + d, :], bk[:, d * 256:(d + 1) * 256], ACT.Identity,
                                                 scale=pcol(l, gain + 2 * j + d, 1))
                        bank_drained(ins, f"{prefix}T{j}")

                def whole(bk):
                    return bk[:, 0:512]

                squares("mix")
                bank_drained(drain("memk", [(flat(memk), whole, 1.0)]), "memk")
                scale0("mix")
                bank_drained(drain("memv", [(flat(memv), whole, 1.0)]), "memv")
                turned("x", G_MIX)

                bk = bank_full(act, l, "hf")
                act.activation(f_b, whole(bk), ACT.Exp, scale=-1.0).then_inc(ev("exp_neg_z"), 1)
                bank_drained(act.activation(k_b, whole(bk), ACT.Exp), "hf")
                bank_drained(drain("hi", [(hi_b, whole, 1.0)]), "hi")
                bank_drained(drain("hq", [(q_b, whole, HD ** -0.5)]), "hq")
                bank_drained(drain("ch", [(cvh_b, whole, 1.0)]), "ch")
                bank_drained(drain("q0", [(qraw_b[:, 0:512], whole, 1.0)]), "q0")
                bank_drained(drain("q1", [(qraw_b[:, 512:1024], whole, 1.0)]), "q1")
                bank_drained(drain("ckv", [(hgr_b, whole, 1.0)]), "ckv")
                bank_drained(drain("ksvs", [(kraw[:, 0, :], lambda b: b[:, 0:256], 1.0),
                                            (vv[:, 0:256], lambda b: b[:, 256:512], 1.0)]), "ksvs")
                wait("cmp_x")
                act.activation(flat(cmp_e[:, :, :, :]), flat(cmp_x[:, :, :, :]), ACT.Exp,
                               scale=-1.0).then_inc(ev("cmp_e"), 1)
                bank_drained(drain("kwvw", [(kraw[:, 1, :], lambda b: b[:, 0:256], 1.0),
                                            (vv[:, 256:512], lambda b: b[:, 256:512], 1.0)]), "kwvw")
                bk = bank_full(act, l, "gl")
                bank_drained(act.activation(flat(gate[:, :, :]), bk[:, 0:48], ACT.Exp, scale=-1.0), "gl")
                bank_drained(drain("cb", [(cvb_b, whole, 1.0)]), "cb")
                bank_drained(drain("cc", [(cvc_b, whole, 1.0)]), "cc")
                bk = bank_full(act, l, "hg")
                act.activation(hgs_b, whole(bk), ACT.Exp, scale=-1.0)
                bank_drained(copy(hgr_b, whole(bk)), "hg")
                for half in range(2):
                    use = f"off_{half}"
                    ao = A_[2].rearrange("p (c h) t -> p c h t", h=2)[:, :, half, :]
                    bank_drained(drain(use, [(ao, lambda b: two(b[:, 0:256]), 1.0)]), use)

                def exps(n):
                    nh = GROUPS[n][3]
                    nk = 512 // nh
                    act.wait_ge(ev("max_ready"), l * NG + (n + 1))
                    for v in range(2):
                        bk = banks[PLACE[f"s{n}_{v}"][0]]
                        for j in range(nh):
                            at = v * 512 + j * nk
                            s = v * nh + j
                            ins = act.activation(probs(n)[:, at:at + nk], bk[:, j * nk:(j + 1) * nk], ACT.Exp,
                                                 bias=att_nb[n % 2][:, s:s + 1], scale=HD ** -0.5,
                                                 accum_out=att_sum[n % 2][:, s:s + 1])
                        bank_drained(ins, f"s{n}_{v}")

                def keep_pT(n):
                    bank_drained(drain(f"t{n}_0", [(pT[:, 0:512], whole, 1.0)]), f"t{n}_0")

                wait("cmp_shifted")
                act.activation(cmpP, cmpP, ACT.Exp,
                               scale=HD ** -0.5).then_inc(ev("cmp_exp"), 1)
                exps(0)
                bk = bank_full(act, l, "av")
                act.activation(kt0_b, whole(bk), ACT.Square).then_inc(ev("o_squares"), 1)
                bank_drained(drain("cmp_t", [(pT[:, 0:256], lambda b: b[:, 0:256], 1.0)]), "cmp_t")
                exps(1)
                keep_pT(0)
                for n in range(1, NN):
                    if n + 1 < NN:
                        exps(n + 1)
                    if n == 2:
                        bk = bank_full(act, l, "hot")
                        for c in range(2):
                            ins = act.activation(mixT[:, 6 + c, :], bk[:, c * 256:(c + 1) * 256], ACT.Identity,
                                                 scale=pcol(l, HNORM + c, 1))
                        bank_drained(ins, "hot")
                    keep_pT(n)
                bank_drained(drain("o6", [(flat(mixT[:, 0:2, :]), whole, 1.0)]), "o6")

                squares("cross")
                scale0("cross")
                turned("y", G_CROSS)
                bank_drained(drain("cq", [(flat(cq), whole, 1.0)]), "cq")
                for n in range(NN, NG):
                    exps(n)
                for n in range(NN, NG):
                    keep_pT(n)
                bank_drained(drain("cross_o", [(flat(coT), whole, 1.0)]), "cross_o")

                squares("ffn")
                scale0("ffn")
                turned("z", G_FFN)
                wait("route_in")
                act.activation(flat(rexp), flat(rlog), ACT.Exp).then_inc(ev("route_exp"), 1)

                wait("npass_ready")
                alone(act)
                npass = act.value_load(npass_i[0:1, 0:1], min_val=1, max_val=MAXP)
                with act.Fori(0, npass * PAIRS) as t:
                    it = base + t
                    for e in range(2):
                        act.wait_ge(efilled[2 + e], it * 2 + 1 if e == 0 else it + 1)
                        act.activation(sgate[:, e * 256:(e + 1) * 256], banks[2 + e][:, 0:256],
                                       ACT.Silu).then_inc(silu_ready, 1)
                    for e in range(2):
                        act.wait_ge(efilled[4 + e], it * 2 + 1)
                        act.activation(yt[:, :, e * SLOTS:(e + 1) * SLOTS],
                                       banks[4 + e][:, 0:512].rearrange("p (m s) -> p m s", m=8),
                                       ACT.Copy).then_inc(edrained[4 + e], 1)
                    for n in range(2):
                        act.wait_ge(efilled[6 + n], it * 2 + 1)
                        act.activation(ys_b[:, n * 512:(n + 1) * 512], banks[6 + n][:, 0:512],
                                       ACT.Copy).then_inc(edrained[6 + n], 1)
                act.reg_add(iters, iters, npass * PAIRS)

            act.wait_ge(ev("h_mix"), DEPTH + 1)
            for tt in range(2):
                ins = act.activation(xhat[:, tt, :], h[:, tt, :], ACT.Square, accum_out=ssq[:, tt:tt + 1])
            ins.then_inc(ev("squares_final"), 1)
            act.wait_ge(ev("rstd_final"), 1)
            act.activation(xhat[:, 0, :], h[:, 0, :], ACT.Identity, scale=rs[:, 0:1]).then_inc(ev("xhat0_final"), 1)

        @block.gpsimd
        def _(pool):
            for b in range(8):
                pool.memset(scratch[:, b:b + 1], 0.0).then_inc(edrained[b], 1)
            for b in range(4, 8):
                pool.memset(scratch[:, 4 + b:5 + b], 0.0).then_inc(drained[b], 1)
            pool.memset(cmp_hk[:, :, :], 0.0)
            pool.memset(cmp_hv[:, :, :], 0.0).then_inc(ev("pads"), 1)
            pool.wait_ge(s_setup, 16 * N_SETUP)
            pool.wait_ge(ev("memT_ready"), 1)
            with pool.Fori(0, DEPTH) as l:
                chain = Chain(pool, pool_step, l * POOL_STEPS, POOL_STEPS, apart=True)

                def wait(name):
                    pool.wait_ge(ev(name), l + 1)
                    alone(pool)

                def tt_(out_ap, a, c, op):
                    return pool.tensor_tensor(out_ap, a, c, op)

                wait("h_mix")
                gain = pcol(l, G_MEM, 8).unsqueeze(2).broadcast_to([P, 8, 256])
                tt_(memG, memT[:, :, :], gain, ALU.mult).then_inc(ev("memG"), 1)
                pool.tensor_copy(cvw[:, :], pcol(l, CONVW, 6)).then_inc(ev("conv_w"), 1)
                chain.link(pool.memset(cv_u[:, :, 0:2], 0.0))
                chain.link(pool.memset(g_b, 1.0))
                chain.link(pool.memset(a0_b, 0.0))
                pool.memset(a1_b, 0.0).then_inc(ev("a_zero"), 1)

                def halves(ap, L):
                    return ap.rearrange("p (n s u) -> p n s u", s=2, u=L)

                def lower(L):
                    return halves(g_b, L)[:, :, 0, :]

                wait("f_ready")
                tot_at = {}
                at = 0
                for L in HALVES[1:]:
                    tot_at[L] = tot[:, at:at + 512 // L]
                    at += 512 // L
                chain.link(pool.tensor_copy(lower(1), halves(f_b, 1)[:, :, 1, :]))
                ff = f_b.rearrange("p (n s) -> p n s", s=2)
                tt_(tot_at[2], ff[:, :, 0], ff[:, :, 1], ALU.mult).then_inc(ev("tot2"), 1)
                wait("tot2")
                wait("k_ready")
                for L in HALVES[1:] + [128]:
                    i = (HALVES + [128]).index(L)
                    if i >= 3:
                        bank_full(pool, l, f"lv{L // 4}_1")
                    tt_(kt_b[i % 2], k_b, g_b, ALU.mult).then_inc(ev(f"kt{L}"), 1)
                    if L == 128:
                        break
                    tv = tot_at[L].rearrange("p (n s) -> p n s", s=2)
                    wait(f"kt{L}")
                    chain.link(tt_(lower(L), lower(L), tv[:, :, 1].unsqueeze(2).broadcast_to([P, 256 // L, L]), ALU.mult))
                    if L < 64:
                        chain.link(tt_(tot_at[2 * L], tv[:, :, 0], tv[:, :, 1], ALU.mult))
                    if L == 4:
                        wait_drained(pool, l, "q0")
                        wait_drained(pool, l, "q1")
                        tt_(qrot, qraw, cos.unsqueeze(1).broadcast_to([P, GRP, 256]), ALU.mult).then_inc(ev("q_cos"), 1)
                    if L == 16:
                        wait_drained(pool, l, "ksvs")
                        wait_drained(pool, l, "kwvw")
                        tt_(krot, kraw, cos.unsqueeze(1).broadcast_to([P, 2, 256]), ALU.mult).then_inc(ev("k_cos"), 1)

                wait_drained(pool, l, "ch")
                wait_drained(pool, l, "cb")
                wait_drained(pool, l, "cc")
                wait("conv_w")
                chain.link(tt_(cv_u[:, :, 2:258], cv_c, cv_h, ALU.mult))
                for c in range(2):
                    ins = pool.tensor_scalar(cv_y[:, c, :], cv_u[:, c, 0:256], cvw[:, c * 3:c * 3 + 1], None, ALU.mult)
                chain.link(ins)
                for tap in (1, 2):
                    for c in range(2):
                        ins = pool.tensor_scalar(cv_h[:, c, :], cv_u[:, c, tap:tap + 256],
                                                 cvw[:, c * 3 + tap:c * 3 + tap + 1], None, ALU.mult)
                    chain.link(ins)
                    chain.link(tt_(cvy_b, cvy_b, cvh_b, ALU.add))
                tt_(flat(mixT[:, 4:6, :]), cvy_b, cvb_b, ALU.mult).then_inc(ev("conv_done"), 1)
                chain.close()

        @block.vector
        def _(dve):
            V = dve
            MUL, ADD, SUB, MAX, MIN, EQ, GT = (ALU.mult, ALU.add, ALU.subtract, ALU.max, ALU.min, ALU.is_equal,
                                               ALU.is_gt)
            setup = Chain(dve, setup_step, 0, None)

            def bc(ap, *shape):
                return ap.broadcast_to([P, *shape])

            def inverse_root(link, y, squares, scale):
                n = y.shape[1]
                x, t = root_x[:, 0:n], root_t[:, 0:n]
                link(V.tensor_scalar(x, squares, scale, EPS, MUL, ADD))
                link(V.tensor_scalar(t.bitcast(I32), x.bitcast(I32), 1, None, ALU.logical_shift_right))
                link(V.tensor_scalar(y.bitcast(I32), t.bitcast(I32), -1.0, float(0x5F3759DF), MUL, ADD))
                for step in range(4):
                    link(V.tensor_tensor(t, y, y, MUL))
                    link(V.tensor_tensor(t, t, x, MUL))
                    link(V.tensor_scalar(t, t, -0.5, 1.5, MUL, ADD))
                    ins = V.tensor_tensor(y, y, t, MUL)
                    if step < 3:
                        link(ins)
                return ins

            dve.wait_ge(s_mem, 16)
            dve.wait_ge(ev("mem_squares"), 1)
            setup.link(inverse_root(setup.link, rs, ssq, 1.0 / D))
            for tt in range(2):
                V.tensor_scalar(mem_raw[:, tt, :], mem_raw[:, tt, :], rs[:, tt:tt + 1], None,
                                MUL).then_inc(ev("mem_hat"), 1)
            dve.wait_ge(s_setup, 16 * N_SETUP)
            V.tensor_copy(lvmask[:, :, :], mask_in).then_inc(ev("masks"), 1)
            V.tensor_copy(cbf[:, :], rest[:, 1024:1312]).then_inc(ev("masks"), 1)

            mx, tot_, run = lbt[:, 0:2], lbt[:, 2:4], lbt[:, 4:6]
            setup.link(V.tensor_reduce(mx, lb_in[:, :, :].rearrange("p l c -> p c l"), AX, MAX))
            V.tensor_tensor(lbf[:, :, :], lb_in[:, :, :], bc(mx.unsqueeze(1), DEPTH, 2), SUB).then_inc(ev("lb_in"), 1)
            V.memset(posv[:, :, MAXP * E:COLS], -1.0)
            V.memset(gates[:, :, MAXP * E:COLS], 0.0)
            dve.wait_ge(ev("lb_exp"), 1)
            setup.link(V.tensor_reduce(tot_, oml[:, :, :].rearrange("p l c -> p c l"), AX, ADD))
            setup.link(V.reciprocal(tot_, tot_))
            setup.link(V.tensor_tensor(oml[:, :, :], oml[:, :, :], bc(tot_.unsqueeze(1), DEPTH, 2), MUL))
            setup.link(V.tensor_copy(lbf[:, 0, :], oml[:, 0, :]))
            for j in range(1, DEPTH):
                setup.link(V.tensor_tensor(lbf[:, j, :], lbf[:, j - 1, :], oml[:, j, :], ADD))
            setup.link(V.tensor_copy(run, oml[:, 0, :]))
            setup.link(V.tensor_tensor(lbf[:, :, :], lbf[:, :, :], bc(run.unsqueeze(1), DEPTH, 2), SUB))
            setup.link(V.tensor_scalar(oml[:, :, :], lbf[:, :, :], -1.0, 1.0, MUL, ADD))
            setup.link(V.tensor_scalar(lbf[:, :, :], lbf[:, :, :], LB_FLOOR, None, MAX))
            dve.wait_ge(ev("mem_turned"), 1)
            for j in range(4):
                V.tensor_copy(flat(memT[:, 2 * j:2 * j + 2, :]), banks[j][:, 0:512]).then_inc(drained[j], 1)
            for j in range(4):
                dve.wait_ge(drained[j], 1)
            dve.wait_ge(ev("pads"), 1)
            dve.wait_ge(ev("masks"), 2)
            V.memset(scratch[:, 24:25], 0.0).then_inc(ev("memT_ready"), 1)

            iters = dve.alloc_register("dve_iters")
            dve.reg_mov(iters, 0)
            with dve.Fori(0, DEPTH) as l:
                base = dve.snap(iters, min_val=0, max_val=DEPTH * MAXP * PAIRS)
                chain = Chain(dve, dve_step, l * DVE_STEPS, DVE_STEPS)
                link = chain.link

                def wait(name):
                    dve.wait_ge(ev(name), l + 1)

                def own(name, ins):
                    ins.then_inc(ev(name), 1)
                    wait(name)

                def rstd(stage):
                    wait("squares_" + stage)
                    own("rstd_" + stage, inverse_root(link, rs, ssq, 1.0 / D))
                    V.tensor_scalar(xhat[:, 1, :], h[:, 1, :], rs[:, 1:2], None, MUL).then_inc(ev("xhat1_" + stage), 1)

                def turned(prefix, gain):
                    for j in (0, 2):
                        bk = bank_full(dve, l, f"{prefix}T{j}")
                        g = bc(pcol(l, gain + 2 * j, 2).unsqueeze(2), 2, 256)
                        bank_drained(V.tensor_tensor(xnT[:, 2 * j:2 * j + 2, :], two(bk[:, 0:512]), g, MUL),
                                     f"{prefix}T{j}")

                def add_out(prefix):
                    for n in range(2):
                        for tt in range(2):
                            bk = bank_full(dve, l, f"{prefix}{n * 2 + tt}")
                            hh = h[:, tt, n * 512:(n + 1) * 512]
                            ins = V.tensor_tensor(hh, hh, bk[:, 0:512], ADD)
                            bank_drained(ins, f"{prefix}{n * 2 + tt}")
                    for n in range(4):
                        wait_drained(dve, l, f"{prefix}{n}")

                def done(name, col):
                    V.memset(scratch[:, col:col + 1], 0.0).then_inc(ev(name), 1)

                done("h_mix", 25)
                rstd("mix")
                turned("x", G_MIX)

                wait("exp_neg_z")
                link(V.tensor_scalar(f_b, f_b, 1.0, None, ADD))
                link(V.reciprocal(f_b, f_b))
                for c in range(2):
                    ins = V.tensor_scalar(f_[:, c, :], f_[:, c, :], oml[:, l, c:c + 1], lbf[:, l, c:c + 1], MUL, ADD)
                own("f_ready", ins)
                wait_drained(dve, l, "hf")
                link(V.tensor_scalar(k_b, k_b, 1.0, None, ADD))
                link(V.reciprocal(k_b, k_b))
                for c in range(2):
                    ins = V.tensor_scalar(k_[:, c, :], k_[:, c, :], oml[:, l, c:c + 1], None, MUL)
                ins.then_inc(ev("k_ready"), 1)

                def level_q(L):
                    i = (HALVES + [128]).index(L)
                    own(f"qt{L}", V.tensor_tensor(qt_b[i % 2], q_b, f_b, MUL))
                    if L == 1:
                        wait("tot2")
                    if L < 128:
                        ff = f_b.rearrange("p (n s u) -> p n s u", s=2, u=L)
                        link(V.tensor_tensor(ff[:, :, 1, :], ff[:, :, 1, :],
                                             bc(ff[:, :, 0, L - 1:L], 256 // L, L), MUL))

                def level_mask(name, m):
                    for half in range(2):
                        use = f"{name}_{half}"
                        bk = bank_full(dve, l, use)
                        if m > 0:
                            wait_drained(dve, l, f"{prev_level[name]}_{half}")
                        alone(dve)
                        bank_drained(V.copy_predicated(a01[:, :, half, :], bc(lvmask[:, m, :].unsqueeze(1), 4, P),
                                                       bk[:, 0:512].rearrange("p (n t) -> p n t", n=4)), use)

                prev_level = {"lv1": "dg"} | {f"lv{2 * L}": f"lv{L}" for L in HALVES[:-1]}
                wait_drained(dve, l, "hq")
                level_q(1)
                wait("a_zero")
                level_mask("dg", 0)

                def rotate(use, raw_x, rot, name, last):
                    bk = bank_full(dve, l, use)
                    s = bc(sin.unsqueeze(1), 2, 256)
                    bank_drained(V.tensor_tensor(two(tmp), two(bk[:, 0:512]), s, MUL), use)
                    wait_drained(dve, l, use)
                    wait(name + "_cos")
                    ins = V.tensor_tensor(rot, rot, tmp, ADD)
                    if last:
                        ins.then_inc(ev(name + "rot"), 1)
                    else:
                        link(ins)

                level_q(2)
                rotate("rq0", None, qrot_b[:, 0:512], "q", False)
                rotate("rq1", None, qrot_b[:, 512:1024], "q", True)
                level_mask("lv1", 1)
                level_q(4)

                bk = bank_full(dve, l, "cmph")
                link(V.tensor_copy(pe2, bk[:, 64:66]))
                for s in range(2):
                    ins = V.tensor_scalar(cmp_x[:, s, :, :], bk[:, s * 32:s * 32 + 30].rearrange("p (v c) -> p v c", v=KV),
                                          pe2[:, s:s + 1], None, ADD)
                bank_drained(ins, "cmph")
                wait_drained(dve, l, "cmph")
                done("cmp_x", 26)
                level_mask("lv2", 2)
                level_q(8)
                wait("cmp_e")
                link(V.tensor_scalar(flat(cmp_e[:, :, :, :]), flat(cmp_e[:, :, :, :]), 1.0, None, ADD))
                link(V.reciprocal(flat(cmp_e[:, :, :, :]), flat(cmp_e[:, :, :, :])))
                V.tensor_tensor(cmp_hk[:, :, 0:15], cmp_x[:, 0, :, :], cmp_e[:, 0, :, :], MUL)
                hv = cmp_hv[:, :, :].rearrange("p i (v c) -> p i v c", v=KV)[:, :, :, 0:15]
                V.tensor_tensor(hv, bc(cmp_x[:, 1, :, :].unsqueeze(1), GRP, KV, 15),
                                bc(cmp_e[:, 1, :, :].unsqueeze(1), GRP, KV, 15), MUL).then_inc(ev("cmp_hid"), 1)
                wait_drained(dve, l, "gl")
                gf = flat(gate[:, :, :])
                link(V.tensor_scalar(gf, gf, 1.0, None, ADD))
                link(V.reciprocal(gf, gf))
                bk = bank_full(dve, l, "cmpo")
                V.tensor_copy(kc[:, :], bk[:, 0:NCMP])
                bank_drained(V.tensor_tensor(
                    vblk.rearrange("p i (v d) -> p i v d", v=KV),
                    bc(bk[:, 64:64 + P].rearrange("p (v d) -> p v d", v=KV).unsqueeze(1), GRP, KV, HD),
                    bc(own_block.unsqueeze(3), GRP, KV, HD), MUL), "cmpo")
                level_mask("lv4", 3)
                level_q(16)
                rotate("rk", None, krot_b, "k", True)
                level_mask("lv8", 4)
                level_q(32)
                wait_drained(dve, l, "hg")
                link(V.tensor_scalar(hgs_b, hgs_b, 1.0, None, ADD))
                link(V.reciprocal(hgs_b, hgs_b))
                link(V.tensor_tensor(hgs_b, hgs_b, hgr_b, MUL))
                level_mask("lv16", 5)
                level_q(64)
                level_mask("lv32", 6)
                level_q(128)
                level_mask("lv64", 7)

                cp = cmpP.rearrange("p (g c) -> p g c", c=NCMP)
                cp4 = cmpP.rearrange("p (g v c) -> p g v c", v=KV, c=NCMP)
                for v in range(KV):
                    bk = bank_full(dve, l, f"cmp_s_{v}")
                    sc = bk[:, 0:128].rearrange("p (g c) -> p g c", c=NCMP)
                    link(V.tensor_reduce(cmx[:, v * 8:(v + 1) * 8], sc, AX, MAX))
                    bank_drained(V.tensor_tensor(cp4[:, :, v, :], sc,
                                                 bc(cmx[:, v * 8:(v + 1) * 8].unsqueeze(2), 8, NCMP), SUB),
                                 f"cmp_s_{v}")
                for v in range(KV):
                    wait_drained(dve, l, f"cmp_s_{v}")
                done("cmp_shifted", 27)

                def maxima(n):
                    nh = GROUPS[n][3]
                    for v in range(2):
                        bk = bank_full(dve, l, f"s{n}_{v}")
                        ins = V.tensor_reduce(att_mx[n % 2][:, v * nh:(v + 1) * nh],
                                              bk[:, 0:512].rearrange("p (h k) -> p h k", h=nh), AX, MAX)
                    link(ins)
                    V.tensor_scalar(att_nb[n % 2][:, 0:2 * nh], att_mx[n % 2][:, 0:2 * nh], -HD ** -0.5, None,
                                    MUL).then_inc(ev("max_ready"), 1)

                def normalise(n):
                    br, tt, i0, nh = GROUPS[n]
                    for v in range(2):
                        wait_drained(dve, l, f"s{n}_{v}")
                    r = att_rr[n % 2][:, 0:2 * nh]
                    link(V.reciprocal(r, att_sum[n % 2][:, 0:2 * nh]))
                    if br != "cross":
                        gv = gate[:, tt, :].rearrange("p (v i b) -> p v i b", v=KV, i=GRP)
                        r2 = r.rearrange("p (v i) -> p v i", v=KV)
                        link(V.tensor_tensor(r2, r2, gv[:, :, i0:i0 + nh, 1 if br == "sel" else 2], MUL))
                    pp = probs(n).rearrange("p (h k) -> p h k", h=2 * nh)
                    V.tensor_tensor(pp, pp, bc(r.unsqueeze(2), 2 * nh, 512 // nh), MUL).then_inc(ev("p_scaled"), 1)

                def keep_pT(n):
                    bk = bank_full(dve, l, f"t{n}_1")
                    bank_drained(V.tensor_copy(pT[:, 512:1024], bk[:, 0:512]), f"t{n}_1")

                maxima(0)
                wait("cmp_exp")
                for tt in range(2):
                    ct = cmpP[:, tt * P:(tt + 1) * P].rearrange("p (g c) -> p g c", c=NCMP)
                    ins = V.tensor_tensor(ct, ct, bc(cmp_ok[:, tt, :].unsqueeze(1), 8, NCMP), MUL)
                link(ins)
                link(V.tensor_reduce(csum, cp, AX, ADD))
                link(V.tensor_scalar(csum, csum, 1e-30, None, MAX))
                link(V.reciprocal(crr, csum))
                g0 = gate[:, :, :].rearrange("p t (v i b) -> p t i v b", v=KV, i=GRP)
                for tt in range(2):
                    c2 = crr[:, tt * 8:(tt + 1) * 8].rearrange("p (i v) -> p i v", v=KV)
                    ins = V.tensor_tensor(c2, c2, g0[:, tt, :, :, 0], MUL)
                link(ins)
                V.tensor_tensor(cp, cp, bc(crr.unsqueeze(2), 16, NCMP), MUL).then_inc(ev("cmp_p"), 1)

                wait("o_squares")
                link(V.tensor_reduce(hsum, kt0_b.rearrange("p (g e) -> p g e", e=HD), AX, ADD))
                link(inverse_root(link, hrs, hsum, 1.0 / HD))
                bk = bank_full(dve, l, "av")
                o_ = kt1_b.rearrange("p (g e) -> p g e", e=HD)
                bank_drained(V.tensor_tensor(o_, bk[:, 0:512].rearrange("p (g e) -> p g e", e=HD),
                                             bc(hrs.unsqueeze(2), 8, HD), MUL), "av")
                wait_drained(dve, l, "av")
                V.tensor_tensor(kt1_b, kt1_b, hgs_b, MUL).then_inc(ev("hgrn_o"), 1)

                maxima(1)
                normalise(0)
                keep_pT(0)
                for n in range(1, NN):
                    if n + 1 < NN:
                        maxima(n + 1)
                    normalise(n)
                    keep_pT(n)
                bk = bank_full(dve, l, "o7")
                bank_drained(V.tensor_copy(flat(mixT[:, 2:4, :]), bk[:, 0:512]), "o7")

                add_out("wo")
                done("h_cross", 28)
                rstd("cross")
                turned("y", G_CROSS)
                for n in range(NN, NG):
                    maxima(n)
                for n in range(NN, NG):
                    normalise(n)
                    keep_pT(n)
                add_out("co")
                done("h_ffn", 29)
                rstd("ffn")
                turned("z", G_FFN)

                bk = bank_full(dve, l, "rt")
                lg = rl[:, :, 0:4]
                le = rl[:, :, 4:36]
                bank_drained(V.tensor_tensor(rl, bk[:, 0:72].rearrange("p (t c) -> p t c", t=2),
                                             bc(pcol(l, RBIAS, 36).unsqueeze(1), 2, 36), ADD), "rt")
                wait_drained(dve, l, "rt")

                def first_of_max(best, vals, iota, n, onehot):
                    link(V.tensor_tensor(onehot, vals, bc(best.unsqueeze(2), 2, n), EQ))
                    link(V.tensor_tensor(onehot, onehot, bc(iota.unsqueeze(1), 2, n), MUL))
                    link(V.tensor_reduce(r_min, onehot, AX, MIN))
                    link(V.tensor_tensor(onehot, bc(iota.unsqueeze(1), 2, n), bc(r_min.unsqueeze(2), 2, n), EQ))

                link(V.tensor_reduce(r_mg, lg, AX, MAX))
                first_of_max(r_mg, lg, iota_g, 4, r_g1)
                link(V.tensor_tensor(rlog[:, :, 0:4], lg, bc(r_mg.unsqueeze(2), 2, 4), SUB))
                for tt in range(2):
                    ins = V.tensor_copy(r_in[:, tt, :].rearrange("p (g e) -> p g e", g=4),
                                        bc(r_g1[:, tt, :].unsqueeze(2), 4, 8))
                link(ins)
                link(V.tensor_scalar(r_out, r_in, -1.0, None, ADD))
                link(V.tensor_tensor(le, le, r_in, MUL))
                link(V.scalar_tensor_tensor(le, r_out, 1e30, le, MUL, ADD))
                link(V.tensor_reduce(r_me, le, AX, MAX))
                link(V.tensor_tensor(rlog[:, :, 4:36], le, bc(r_me.unsqueeze(2), 2, 32), SUB))
                done("route_in", 30)
                wait("route_exp")
                link(V.tensor_reduce(r_sg, rexp[:, :, 0:4], AX, ADD))
                ee = rexp[:, :, 4:36]
                link(V.tensor_tensor(ee, ee, r_out, ADD))
                link(V.tensor_reduce(r_e1, ee, AX, MAX))
                first_of_max(r_e1, ee, iota_e, 32, r_o1)
                link(V.scalar_tensor_tensor(ee, r_o1, -4.0, ee, MUL, ADD))
                link(V.tensor_reduce(r_e2, ee, AX, MAX))
                first_of_max(r_e2, ee, iota_e, 32, r_o2)
                own("chosen", V.tensor_tensor(chosen, r_o1, r_o2, ADD))
                link(V.tensor_tensor(r_t, r_e1, r_e2, ADD))
                link(V.tensor_tensor(r_t, r_t, r_sg, MUL))
                link(V.reciprocal(r_t, r_t))
                link(V.tensor_tensor(r_e1, r_e1, r_t, MUL))
                link(V.tensor_tensor(r_e2, r_e2, r_t, MUL))
                link(V.tensor_tensor(r_o1, r_o1, bc(r_e1.unsqueeze(2), 2, 32), MUL))
                link(V.tensor_tensor(r_o2, r_o2, bc(r_e2.unsqueeze(2), 2, 32), MUL))
                for p_ in range(MAXP):
                    ins = V.tensor_tensor(gates[:, :, p_ * E:(p_ + 1) * E], r_o1, r_o2, ADD)
                link(ins)
                bk = bank_full(dve, l, "pos")
                link(V.tensor_reduce(r_cnt, bk[:, 2 * E:3 * E], AX, MAX))
                pos0 = posv[:, :, 0:E]
                bank_drained(V.scalar_tensor_tensor(pos0, bk[:, 0:2 * E].rearrange("p (t e) -> p t e", t=2), 1.0,
                                                    chosen, ADD, MUL), "pos")
                wait_drained(dve, l, "pos")
                link(V.tensor_scalar(pos0, pos0, -1.0, None, ADD))
                for p_ in range(1, MAXP):
                    ins = V.tensor_scalar(posv[:, :, p_ * E:(p_ + 1) * E], pos0, -float(p_ * SLOTS), None, ADD)
                    link(ins)
                link(V.memset(r_np, 1.0))
                for p_ in range(1, MAXP):
                    link(V.scalar_tensor_tensor(r_np, r_cnt, float(p_ * SLOTS), r_np, GT, ADD))
                own("npass_ready", V.tensor_copy(npass_i[0:1, 0:1], r_np[0:1, :]))
                chain.close()

                alone(dve)
                npass = dve.value_load(npass_i[0:1, 0:1], min_val=1, max_val=MAXP)
                gbase = base + l

                def onehot(col):
                    for tt in range(2):
                        ins = V.tensor_tensor(pm[:, tt, :, :], bc(iota_slot.unsqueeze(1), 2, SLOTS),
                                              bc(posv[:, tt, col].unsqueeze(2), 2, SLOTS), EQ)
                    return ins

                def gathered(n):
                    for b in range(2):
                        dve.wait_ge(efilled[b], gbase + n + 1)
                        g = bc(pcol(l, G_FFN + 4 * b, 4).unsqueeze(2), 4, P)
                        V.tensor_tensor(xg[:, 4 * b:4 * b + 4, :], banks[b][:, 0:512].rearrange("p (d s) -> p d s", d=4),
                                        g, MUL).then_inc(edrained[b], 1)

                onehot(slice(0, 2)).then_inc(onehot_ready, 1)
                gathered(0)
                with dve.Fori(0, npass * PAIRS) as t:
                    it = base + t
                    dve.wait_ge(onehot_ready, gbase + t + 1)
                    for tt in range(2):
                        ins = V.tensor_tensor(pg[:, tt, :, :], pm[:, tt, :, :],
                                              bc(gates[:, tt, bass.ds(t * 2, 2)].unsqueeze(2), 2, SLOTS), MUL)
                    ins.then_inc(pg_ready, 1)
                    dve.wait_ge(pg_ready, it + 1)
                    onehot(bass.ds(t * 2 + 2, 2)).then_inc(onehot_ready, 1)
                    for e in range(2):
                        dve.wait_ge(silu_ready, it * 2 + (e + 1))
                        V.tensor_tensor(flat(ht[:, e, :, :]), sgate[:, e * 256:(e + 1) * 256], banks[2 + e][:, 256:512],
                                        MUL).then_inc(edrained[2 + e], 1)
                    gathered(t + 1)
                    dve.wait_ge(efilled[2], it * 2 + 2)
                    V.tensor_copy(pgT, banks[2][:, 0:256]).then_inc(edrained[2], 1)
                    for tt in range(2):
                        for n in range(2):
                            b = (6 if tt == 0 else 4) + n
                            dve.wait_ge(efilled[b], it * 2 + 2)
                            hh = h[:, tt, n * 512:(n + 1) * 512]
                            V.tensor_tensor(hh, hh, banks[b][:, 0:512], ADD).then_inc(edrained[b], 1)
                    for b in (4, 5, 6, 7):
                        dve.wait_ge(edrained[b], it * 2 + 3)
                dve.reg_add(iters, iters, npass * PAIRS)

            V.memset(scratch[:, 31:32], 0.0).then_inc(ev("h_mix"), 1)
            dve.wait_ge(s_gain, 16)
            dve.wait_ge(ev("squares_final"), 1)
            inverse_root(setup.link, rs, ssq, 1.0 / D).then_inc(ev("rstd_final"), 1)
            dve.wait_ge(ev("rstd_final"), 1)
            setup.link(V.tensor_scalar(xhat[:, 1, :], h[:, 1, :], rs[:, 1:2], None, MUL))
            V.tensor_tensor(xhat[:, 1, :], xhat[:, 1, :], gain_row, MUL)
            dve.wait_ge(ev("xhat0_final"), 1)
            setup.link(V.tensor_tensor(xhat[:, 0, :], xhat[:, 0, :], gain_row, MUL))
            V.memset(scratch[:, 32:33], 0.0).then_inc(ev("out_ready"), 1)


def constants():
    import numpy as np

    p = np.arange(P)
    half = HD // 2
    inv = (10000.0 ** (-np.arange(half, dtype=np.float32) / half)).astype(np.float32)
    ang = (np.arange(256, dtype=np.float32)[None, :] * inv[p % half][:, None]).astype(np.float32)
    sign = np.where(p % HD < half, -1.0, 1.0)[:, None]
    eye = np.eye(P, dtype=np.float32)
    tok = np.arange(2)[None, :, None] * P + p[:, None, None]
    blk = np.arange(NCMP)[None, None, :]
    ok = ((blk * 16 + 31 <= tok) & (blk < NCMP - 1)).astype(np.float32)
    rows = np.arange(P) // NCMP
    own = np.zeros((P, GRP, KV), np.float32)
    own[p, rows // KV, rows % KV] = 1.0
    f = np.concatenate([
        eye, eye[p ^ half], (p[:, None] < p[None, :]).astype(np.float32), np.ones((P, P), np.float32),
        np.cos(ang), np.sin(ang) * sign,
        np.broadcast_to(np.arange(SLOTS, dtype=np.float32), (P, SLOTS)),
        np.broadcast_to(np.arange(4) - TOP_IDX, (P, 4)), np.broadcast_to(np.arange(32) - TOP_IDX, (P, 32)),
        ok.reshape(P, 32), own.reshape(P, 8)], axis=1).astype(np.float32)
    bf = np.concatenate([
        eye, np.where(p[None, :] > p[:, None], -1e30, 0.0), (1.0 - ok.reshape(P, 32)) * -1e30], axis=1)
    s, t = p[:, None], p[None, :]
    masks = [s == t] + [(s // (2 * L) == t // (2 * L)) & (s % (2 * L) < L) & (t % (2 * L) >= L) for L in HALVES]
    return f, np.concatenate([np.stack(masks, 1).reshape(P, -1), bf], axis=1).astype(np.float32)


def kernel(**inputs):
    import numpy as _np
    import concourse.bacc as _bacc
    from concourse import mybir as _mybir
    from concourse.bass_utils import run_bass_kernel_spmd as _run

    a = {k: _np.asarray(v) for k, v in inputs.items()}
    L = a["w_in"].shape[0]

    def cols(w):
        n = w.shape[1] // P
        return _np.moveaxis(w.reshape(L, n, P, -1), 1, 2).reshape(L, P, -1)

    def rows(w):
        return _np.broadcast_to(w[:, None, :], (L, P, w.shape[-1]))

    conv = _np.moveaxis(a["conv_w"].reshape(L, 3, 2, P), 3, 1).transpose(0, 1, 3, 2).reshape(L, P, 6)
    pe = a["cmp_pe"].reshape(L, 2, 16, 2, HD).transpose(0, 3, 4, 1, 2).reshape(L, P, 32)
    router = _np.concatenate([a["router_group_w"], a["router_expert_w"]], axis=2)
    params = _np.concatenate([
        cols(a["norm_mix"]), cols(a["norm_cross"]), cols(a["norm_mem"]), cols(a["norm_ffn"]), conv, pe,
        cols(a["hgrn_norm"]), rows(a["router_group_b"]), rows(a["router_expert_b"]), cols(router)], axis=2)
    w_q = a["w_in"][:, :, 0:512].reshape(L, D, KV, GRP, HD).transpose(0, 1, 3, 2, 4).reshape(L, D, 512)
    heads = a["w_out"][:, 0:512].reshape(L, KV, GRP, HD, D).transpose(0, 2, 1, 3, 4).reshape(L, 512, D)
    w_out = _np.concatenate([heads, a["w_out"][:, 512:]], axis=1)
    cmp_w1 = a["cmp_w1"].reshape(L, 2, 16, P, P).transpose(0, 3, 1, 2, 4).reshape(L, P, 4096)
    cmp_w2 = a["cmp_w2"].transpose(0, 2, 1, 3).reshape(L, P, 2 * HD)
    f, masks = constants()
    feeds = {
        "x": a["x"][0], "mem": a["mem"][0], "w_q": w_q, "w_in": a["w_in"], "cmp_w1": cmp_w1,
        "cmp_w2": cmp_w2, "w_out": w_out, "wq": a["cross_wq"], "wkv": a["cross_wkv"], "wo": a["cross_wo"],
        "w_gu": a["expert_w_gate_up"], "w_dn": a["expert_w_down"], "norm_final": a["norm_final"],
        "params": params, "lb_logits": a["hgrn_lb_logits"].reshape(L, 2, P).transpose(2, 0, 1),
        "consts": f, "masks": masks}
    nc = _bacc.Bacc("TRN2", target_bir_lowering=False, num_devices=1)
    arrays, args = {}, []
    for name, v in feeds.items():
        v = _np.ascontiguousarray(v)
        arrays[f"in_{name}"] = v
        args.append(nc.dram_tensor(f"in_{name}", v.shape, _mybir.dt.from_np(v.dtype), kind="ExternalInput").ap())
    out = nc.dram_tensor("out_y", (256, D), F32, kind="ExternalOutput").ap()
    hymba(nc, L, *args, out)
    r = _run(nc, [arrays], core_ids=[0])
    return r.results[0]["out_y"].reshape(a["x"].shape)
```

```python
from contextlib import ExitStack

import concourse.bass as bass
from concourse import mybir

F32 = mybir.dt.float32
BF16 = mybir.dt.bfloat16
U8 = mybir.dt.uint8
I32 = mybir.dt.int32
ALU = mybir.AluOpType
ACT = mybir.ActivationFunctionType
AX = mybir.AxisListType.X

P = 128
D = 1024
EPS = 1e-6
LB_FLOOR = 1e-30
HD = 64
KV = 2
GRP = 4
NCMP = 16
TOP_IDX = 1000.0
SLOTS = 64

C_KC, C_KS, C_KW, C_GL = 512, 768, 1024, 1280
C_CB, C_CH, C_HQ, C_HF, C_HI, C_HG, C_END = 1304, 1816, 2072, 2328, 2584, 2840, 3096

HALVES = [1, 2, 4, 8, 16, 32, 64]

PROJECT = (["memk"] + [f"xT{j}" for j in range(4)] + ["hf", "hq", "ckv", "dg_0", "dg_1", "q0", "q1", "cmph"]
           + ["lv1_0", "lv1_1", "ksvs", "hidT", "rq0", "rq1", "lv2_0", "lv2_1", "kw", "vwgl", "cmpo", "rk"]
           + ["lv4_0", "lv4_1", "cb", "lv8_0", "lv8_1", "cc", "lv16_0", "lv16_1", "hg"]
           + ["lv32_0", "lv32_1", "ch", "lv64_0", "lv64_1", "hi", "off_0", "off_1", "av", "hot"])
GROUPS = [(br, tt, i, n) for br in ("sel", "win") for tt, i, n in ((0, 0, 4), (1, 0, 2), (1, 2, 2))]
NN = len(GROUPS)
GROUPS += [("cross", tt, 0, 2) for tt in range(2)]
NG = len(GROUPS)
USES = {
    0: PROJECT[0::2] + ["wo0", "wo2", "yT0", "yT2", "cq", "s6_0", "co0", "co2", "zT0", "zT2", "rt"],
    1: PROJECT[1::2] + ["wo1", "wo3", "yT1", "yT3", "s6_1", "co1", "co3", "zT1", "zT3", "pos"],
    2: ["cmp_s_0"] + [f"s{n}_0" for n in range(NG) if n != NN],
    3: ["cmp_s_1"] + [f"s{n}_1" for n in range(NG) if n != NN],
    4: ["cmp_t"] + [f"t{n}_0" for n in range(NG)],
    5: [f"t{n}_1" for n in range(NG)],
    6: ["o6", "cross_o"],
    7: ["o7", "memv"],
}
PLACE = {name: (b, n) for b, names in USES.items() for n, name in enumerate(names)}

DVE_STEPS, POOL_STEPS = 135, 23

LAST_USE = ["memk", "hq", "ksvs", "q1", "cmph", "cmpo", "cc", "hi", "hg", "wo1", "wo3", "co3"]
N_SETUP = 5


def flat(ap):
    names = "abc"[:len(ap.shape) - 1]
    return ap if len(names) == 1 else ap.rearrange(f"p {' '.join(names)} -> p ({' '.join(names)})")



def hymba(nc, L, x, mem, w_q, w_in, cmp_w1, cmp_w2, w_out, wq, wkv, wo, w_gu, w_dn, norm_final,
          params, lb_logits, consts, masks, out):
    T = 256
    DEPTH = L
    E = w_gu.shape[1]
    PAIRS = E // 2
    MAXP = T // SLOTS
    NPAR = params.shape[2]

    ctx = ExitStack()
    with ctx:
        def sb(name, shape, dt=F32):
            return ctx.enter_context(nc.sbuf_tensor(name, shape, dt))

        def sem(name):
            return ctx.enter_context(nc.semaphore(name))

        banks = [ctx.enter_context(nc.psum_tensor(f"bank{b}", [P, 512], F32)) for b in range(8)]

        h = sb("h", [P, 2, 1024])
        memT = sb("memT", [P, 8, 256])
        xnT = sb("xnT", [P, 8, 256])
        xhat = sb("xhat", [P, 2, 1024])
        cst = sb("cst", [P, consts.shape[1]])
        cbf = sb("cbf", [P, 288], BF16)
        lvmask = sb("lvmask", [P, 8, 128], U8)
        par = sb("par", [P, DEPTH, NPAR])
        lb_in = sb("lb_in", [P, DEPTH, 2])
        lbf = sb("lbf", [P, DEPTH, 2])
        oml = sb("oml", [P, DEPTH, 2])
        small = sb("small", [P, 254])
        COLS = MAXP * E + 2
        posv = sb("posv", [P, 2, COLS])
        gates = sb("gates", [P, 2, COLS])
        npass_i = sb("npass_i", [1, 2], I32)
        dense = sb("dense", [P, 3, 4096])
        ring = sb("ring", [P, 3, 4096])
        share = sb("share", [P, 12288])
        rest = sb("rest", [P, 4352])

        ident = cst[:, 0:128]
        perm = cst[:, 128:256]
        tri = cst[:, 256:384]
        ones = cst[:, 384:512]
        cos = cst[:, 512:768]
        sin = cst[:, 768:1024]
        iota_slot = cst[:, 1024:1024 + SLOTS]
        iota_g = cst[:, 1088:1092]
        iota_e = cst[:, 1092:1124]
        cmp_ok = cst[:, 1124:1156].rearrange("p (t c) -> p t c", t=2)
        own_block = cst[:, 1156:1164].rearrange("p (i v) -> p i v", v=2)
        ident_b = cbf[:, 0:128]
        causal_b = cbf[:, 128:256]
        cmp_no_b = cbf[:, 256:288].rearrange("p (t c) -> p t c", t=2)

        def pcol(l, a, n):
            return par[:, l, a:a + n]
        G_MIX, G_CROSS, G_MEM, G_FFN, CONVW, PE_C, HNORM, RBIAS, RW = 0, 8, 16, 24, 32, 38, 70, 72, 108

        def cut(t, sizes):
            at, views = 0, []
            for n in sizes:
                views.append(t[:, at:at + n])
                at += n
            assert at <= t.shape[1], at
            return views

        def two(ap):
            return ap.rearrange("p (c t) -> p c t", c=2)

        (f_b, g_b, q_b, k_b, qt0_b, qt1_b, kt0_b, kt1_b, tot, a0_b, a1_b, ao_b, hi_b, hgr_b) = cut(
            share[:, 0:7168], [512] * 14)
        (qraw_b, qrot_b, kraw_b, krot_b, tmp, vv, vblk_b, hgs_b) = cut(
            share[:, 7168:12288], [1024, 1024, 512, 512, 512, 512, 512, 512])
        f_, g_, q_, k_ = two(f_b), two(g_b), two(q_b), two(k_b)
        qt_b, kt_b = [qt0_b, qt1_b], [kt0_b, kt1_b]
        qt, kt = [two(qt0_b), two(qt1_b)], [two(kt0_b), two(kt1_b)]
        a01 = share[:, 4608:5632].rearrange("p (n h t) -> p n h t", n=4, h=2)
        A_ = [t.rearrange("p (h t) -> p h t", h=4) for t in (a0_b, a1_b, ao_b)]
        hi_ = two(hi_b)
        qraw = qraw_b.rearrange("p (i t) -> p i t", i=GRP)
        qrot = qrot_b.rearrange("p (i t) -> p i t", i=GRP)
        kraw, krot = two(kraw_b), two(krot_b)
        v_of = {"sel": two(vv[:, 0:256]), "win": two(vv[:, 256:512])}
        vblk = vblk_b.rearrange("p (i c) -> p i c", i=GRP)
        mask_in = rest[:, 0:1024].rearrange("p (m t) -> p m t", m=8)
        (memG_b, wkv_v, probs_a, probs_b, pT, cmpPT, cmpP, xe_b, cmp_x, cmp_e) = cut(
            ring[:, :, :].rearrange("p s c -> p (s c)"), [2048, 2048, 1024, 1024, 1024, 256, 256, 1040, 128, 128])
        memG = memG_b.rearrange("p (k t) -> p k t", k=8)
        xe = xe_b[:, 0:1024].rearrange("p (g a c) -> p g a c", g=4, a=16)
        mem_raw = two(share[:, 0:2048])
        mem_sq = two(share[:, 2048:4096])

        (cvb_b, cvc_b, cvh_b, cvy_b) = cut(rest[:, 0:2048], [512] * 4)
        cv_b, cv_c, cv_h, cv_y = two(cvb_b), two(cvc_b), two(cvh_b), two(cvy_b)
        cv_u = two(rest[:, 2048:2048 + 516])
        memk, memv, cq = [two(rest[:, 2564 + 512 * n:3076 + 512 * n]) for n in range(3)]
        coT = cv_b

        flatx = xnT[:, :, :].rearrange("p k t -> p (k t)")

        def probs(n):
            if n < NN:
                return probs_b if n % 2 else probs_a
            return flatx[:, 0:1024] if n % 2 else rest[:, 1024:2048]

        def pT_of(n):
            return pT if n < NN else flatx[:, 1024:2048]

        mixT = xhat[:, :, :].rearrange("p a b -> p (a b)").rearrange("p (k t) -> p k t", k=8)
        cmp_hk = sb("cmp_hk", [P, KV, 32])
        cmp_hv = sb("cmp_hv", [P, GRP, KV * NCMP])
        kc = sb("kc", [P, NCMP])
        gate = sb("gate", [P, 2, 24])
        cvw = sb("cvw", [P, 6])
        (ssq, rs, hsum, hrs, pe2, lbt, cmx, csum, crr) = cut(small[:, 0:100], [2, 2, 8, 8, 2, 24, 16, 16, 16])
        att_mx, att_nb, att_sum, att_rr = [
            [small[:, 190 + 16 * n + 8 * b:198 + 16 * n + 8 * b] for b in range(2)] for n in range(4)]
        scratch = small[:, 136:172]
        root_x, root_t = small[:, 172:180], small[:, 180:188]

        (xg_b, ys_b, sgate, hid, ht_b, pm_b, pg_b, pgt_b) = cut(
            rest[:, :], [1024, 1024, 512, 512, 512, 256, 256, 256])
        xg = xg_b.rearrange("p (k s) -> p k s", k=8)
        ht = ht_b.rearrange("p (k s) -> p k s", k=4)
        pm = pm_b.rearrange("p (t e s) -> p t e s", t=2, e=2)
        pg = pg_b.rearrange("p (t e s) -> p t e s", t=2, e=2)
        pgT = pgt_b
        def rtile(at, n):
            return ys_b[:, at:at + 2 * n].rearrange("p (t c) -> p t c", t=2)
        rl, rlog, r_in, r_out, r_o1, r_o2, chosen = [
            rtile(a, n) for a, n in ((0, 36), (72, 36), (144, 32), (208, 32), (272, 32), (336, 32), (400, 32))]
        rexp = rtile(464, 36)
        r_g1 = rtile(536, 4)
        r_mg, r_me, r_sg, r_e1, r_e2, r_t, r_min = [ys_b[:, 544 + 2 * i:546 + 2 * i] for i in range(7)]
        r_cnt, r_np = ys_b[:, 558:559], ys_b[:, 559:560]
        gain_row = memT[:, :, :].rearrange("p k t -> p (k t)")[:, 0:D]

        def eslot(s):
            return ring[:, s, :] if s < 3 else share[:, (s - 3) * 4096:(s - 2) * 4096]

        filled = [sem(f"bank{b}_filled") for b in range(8)]
        drained = [sem(f"bank{b}_drained") for b in range(8)]
        efilled = [sem(f"ebank{b}_filled") for b in range(8)]
        edrained = [sem(f"ebank{b}_drained") for b in range(8)]
        dloaded = [sem(f"dense{s}_loaded") for s in range(3)]
        eloaded = [sem(f"expert{s}_loaded") for s in range(6)]
        vloaded = sem("memory_value_weights_loaded")
        half_read = sem("gate_up_first_rows_read")
        events = {}

        def ev(name):
            if name not in events:
                events[name] = sem(name)
            return events[name]

        s_setup = sem("inputs_loaded")
        s_mem = sem("mem_loaded")
        s_gain = sem("final_gain_loaded")
        s_out = sem("out_stored")
        dve_step, pool_step, setup_step = sem("dve_step"), sem("pool_step"), sem("setup_step")
        onehot_ready, pg_ready = sem("onehot_ready"), sem("gated_onehot_ready")

        class Chain:

            def __init__(self, eng, semaphore, base, steps, apart=False):
                self.apart = apart
                self.eng, self.sem, self.base, self.n, self.steps = eng, semaphore, base, 0, steps

            def link(self, ins):
                self.n += 1
                ins.then_inc(self.sem, 1)
                self.eng.wait_ge(self.sem, self.base + self.n)
                if self.apart:
                    alone(self.eng)

            def close(self):
                assert self.n == self.steps, (str(self.sem), self.n, self.steps)

        def alone(eng):
            eng.nop(nofuse=True)

        def bank_free(eng, l, use):
            b, n = PLACE[use]
            eng.wait_ge(drained[b], l * len(USES[b]) + (n + 1))
            return banks[b]

        def bank_done(ins, use):
            ins.then_inc(filled[PLACE[use][0]], 1)

        def bank_full(eng, l, use):
            b, n = PLACE[use]
            eng.wait_ge(filled[b], l * len(USES[b]) + (n + 1))
            return banks[b]

        def bank_drained(ins, use):
            ins.then_inc(drained[PLACE[use][0]], 1)

        def wait_drained(eng, l, use):
            b, n = PLACE[use]
            eng.wait_ge(drained[b], l * len(USES[b]) + (n + 2))

        def kt_rows(w, a, b):
            return w.rearrange("(k p) c -> p k c", p=P)[:, :, a:b]

        def unit_view(s, n, c):
            return dense[:, s, 0:n * c].rearrange("p (k c) -> p k c", k=n)

        def unit_dmas(l, u):
            s = u % 3
            win = w_in[l]
            spans = {1: (C_HQ, C_HI), 2: (C_KC, C_KW), 5: (C_KW, C_CB), 6: (C_CB, C_CH), 8: (C_HG, C_END)}
            if u == 0:
                return [(unit_view(s, 8, 256), kt_rows(wkv[l], 0, 256))]
            if u == 3:
                return [(unit_view(s, 8, 512), kt_rows(w_q[l], 0, 512))]
            if u in spans:
                a, b = spans[u]
                dmas = [(unit_view(s, 8, b - a), kt_rows(win, a, b))]
                if u == 5:
                    dmas.append((dense[:, s, 3968:4096], cmp_w2[l]))
                return dmas
            if u == 4:
                return [(dense[:, s, :], cmp_w1[l])]
            if u == 7:
                return [(dense[:, s, n * 2048:(n + 1) * 2048].rearrange("p (k c) -> p k c", k=8),
                         kt_rows(win, a, a + 256)) for n, a in enumerate((C_CH, C_HI))]
            if u in (9, 10):
                return [(unit_view(s, 8, 512), kt_rows(w_out[l], (u - 9) * 512, (u - 8) * 512))]
            return [(dense[:, s, 0:2048].rearrange("p (k c) -> p k c", k=8), kt_rows(wq[l], 0, 256)),
                    (dense[:, s, 2048:4096].rearrange("p (k c) -> p k c", k=2), kt_rows(wo[l], 0, 1024))]

        N_DMA = [1, 1, 1, 1, 1, 2, 1, 2, 1, 1, 1, 2]

        def unit_loaded(eng, l, u):
            s = u % 3
            per = sum(N_DMA[s::3])
            upto = sum(N_DMA[i] for i in range(s, u + 1, 3))
            eng.wait_ge(dloaded[s], l * (16 * per) + 16 * upto)

        def expert_dmas(l, pair, s):
            part, e = s // 2, pair * 2 + s % 2
            src = w_dn[l, e] if part == 2 else w_gu[l, e, part * 512:(part + 1) * 512, :]
            return eslot(s).rearrange("p (k c) -> p k c", k=4), src.rearrange("(k p) c -> p k c", p=P)

        block = ctx.enter_context(nc.Block())

        @block.sync
        def _(sp):
            sp.dma_start(mem_raw, mem.rearrange("(t p) d -> p t d", p=P)).then_inc(s_mem, 16)
            sp.dma_start(cst[:, :], consts).then_inc(s_setup, 16)
            sp.dma_start(par[:, :, :], params.rearrange("l p n -> p l n")).then_inc(s_setup, 16)
            sp.dma_start(h[:, :, :], x.rearrange("(t p) d -> p t d", p=P)).then_inc(s_setup, 16)
            sp.dma_start(rest[:, 0:1312], masks).then_inc(s_setup, 16)
            sp.dma_start(lb_in[:, :, :], lb_logits).then_inc(s_setup, 16)
            iters = sp.alloc_register("sp_iters")
            sp.reg_mov(iters, 0)
            with sp.Fori(0, DEPTH) as l:
                base = sp.snap(iters, min_val=0, max_val=DEPTH * MAXP * PAIRS)

                def load_unit(u):
                    s = u % 3
                    if u >= 3:
                        bank_full(sp, l, LAST_USE[u - 3])
                    for dst, src in unit_dmas(l, u):
                        sp.dma_start(dst, src).then_inc(dloaded[s], 16)

                def load_expert(pair, s):
                    dst, src = expert_dmas(l, pair, s)
                    sp.dma_start(dst, src).then_inc(eloaded[s], 16)

                for u in range(3):
                    load_unit(u)
                sp.wait_ge(ev("h_mix"), l + 1)
                alone(sp)
                sp.dma_start(wkv_v.rearrange("p (k c) -> p k c", k=8),
                             kt_rows(wkv[l], 256, 512)).then_inc(vloaded, 16)
                for u in range(3, 12):
                    load_unit(u)
                bank_full(sp, l, "wo0")
                for s in range(1, 6):
                    load_expert(0, s)
                bank_full(sp, l, "memv")
                alone(sp)
                load_expert(0, 0)
                sp.wait_ge(ev("npass_ready"), l + 1)
                alone(sp)
                npass = sp.value_load(npass_i[0:1, 0:1], min_val=1, max_val=MAXP)
                with sp.Fori(1, npass * PAIRS) as t:
                    pair = t % PAIRS
                    before = base + t
                    sp.wait_ge(half_read, before)
                    load_expert(pair, 0)
                    load_expert(pair, 1)
                    sp.wait_ge(efilled[3], before)
                    load_expert(pair, 2)
                    load_expert(pair, 3)
                    sp.wait_ge(efilled[5], before * 2 - 1)
                    load_expert(pair, 4)
                    load_expert(pair, 5)
                sp.reg_add(iters, iters, npass * PAIRS)
            sp.dma_start(gain_row, norm_final.partition_broadcast(P)).then_inc(s_gain, 16)
            sp.wait_ge(ev("out_ready"), 1)
            sp.dma_start(out.rearrange("(t p) d -> p t d", p=P), xhat[:, :, :]).then_inc(s_out, 16)
            sp.wait_ge(s_out, 16)

        @block.tensor
        def _(pe):
            def mm(out_ap, lhsT, rhs, start, stop):
                return pe.matmul(out_ap, lhsT=lhsT, rhs=rhs, start=start, stop=stop, skip_group_check=True)

            pe.wait_ge(s_setup, 16 * N_SETUP)
            pe.wait_ge(ev("mem_hat"), 2)
            for j in range(4):
                for d in range(2):
                    for tt in range(2):
                        ins = pe.transpose(banks[j][:, (d * 2 + tt) * P:(d * 2 + tt + 1) * P],
                                           mem_raw[:, tt, (2 * j + d) * P:(2 * j + d + 1) * P], ident)
            ins.then_inc(ev("mem_turned"), 1)

            iters = pe.alloc_register("pe_iters")
            pe.reg_mov(iters, 0)
            with pe.Fori(0, DEPTH) as l:
                base = pe.snap(iters, min_val=0, max_val=DEPTH * MAXP * PAIRS)

                def wait(name):
                    pe.wait_ge(ev(name), l + 1)

                def settled(*uses):
                    for use in {PLACE[use][0]: use for use in sorted(uses, key=lambda u: PLACE[u][1])}.values():
                        wait_drained(pe, l, use)

                def project_T(out_ap, lhsT_of, src, rhs_cols=slice(0, 256)):
                    for k in range(8):
                        ins = mm(out_ap, lhsT_of(k), src[:, k, rhs_cols], k == 0, k == 7)
                    return ins

                def project_N(out_ap, unit, c0, c1, src, tt):
                    for k in range(8):
                        ins = mm(out_ap, src[:, k, tt * P:(tt + 1) * P], unit[:, k, c0:c1], k == 0, k == 7)
                    return ins

                def two_T(use, unit, c0, src):
                    bk = bank_free(pe, l, use)
                    for c in range(2):
                        ins = project_T(bk[:, c * 256:(c + 1) * 256],
                                        lambda k: unit[:, k, c0 + c * P:c0 + (c + 1) * P], src)
                    bank_done(ins, use)

                def two_N(use, unit, c0, c1, src):
                    bk = bank_free(pe, l, use)
                    n = c1 - c0
                    for tt in range(2):
                        ins = project_N(bk[:, tt * n:(tt + 1) * n], unit, c0, c1, src, tt)
                    bank_done(ins, use)

                def turn(prefix, stage):
                    wait("xhat0_" + stage)
                    wait("xhat1_" + stage)
                    for j in range(4):
                        bk = bank_free(pe, l, f"{prefix}T{j}")
                        for d in range(2):
                            for tt in range(2):
                                ins = pe.transpose(bk[:, (d * 2 + tt) * P:(d * 2 + tt + 1) * P],
                                                   xhat[:, tt, (2 * j + d) * P:(2 * j + d + 1) * P], ident)
                        bank_done(ins, f"{prefix}T{j}")

                wait("memG")
                unit_loaded(pe, l, 0)
                two_T("memk", unit_view(0, 8, 256), 0, memG)
                turn("x", "mix")
                settled("xT0", "xT1", "xT2", "xT3")
                unit_loaded(pe, l, 1)
                u = unit_view(1, 8, 512)
                two_T("hf", u, C_HF - C_HQ, xnT)
                two_T("hq", u, 0, xnT)

                def level(name, kk, qq):
                    bks = [bank_free(pe, l, f"{name}_{half}") for half in range(2)]
                    for n in range(4):
                        cols = slice((n // 2) * P, (n // 2 + 1) * P)
                        for half in range(2):
                            ch = slice(half * HD, (half + 1) * HD)
                            ins = mm(bks[half][:, n * P:(n + 1) * P], kk[ch, n % 2, cols], qq[ch, n % 2, cols],
                                     True, True)
                            if n == 3:
                                bank_done(ins, f"{name}_{half}")

                def half_level(L):
                    i = HALVES.index(L)
                    wait(f"qt{L}")
                    if L > 1:
                        wait(f"kt{L}")
                    level(f"lv{L}", k_ if L == 1 else kt[i % 2], qt[i % 2])

                def swap(use, src, c0):
                    bk = bank_free(pe, l, use)
                    bank_done(mm(bk[:, 0:512], perm, src[:, c0:c0 + 512], True, True), use)

                unit_loaded(pe, l, 2)
                u = unit_view(2, 8, 512)
                xpar = xnT[:, :, :].rearrange("p k (u r) -> p k r u", r=2)
                bk = bank_free(pe, l, "ckv")
                for s in range(2):
                    for v in range(KV):
                        cols = s * P + v * HD
                        for k in range(8):
                            for r in range(2):
                                ins = mm(bk[r * HD:(r + 1) * HD, (s * KV + v) * P:(s * KV + v + 1) * P],
                                         u[:, k, cols:cols + HD], xpar[:, k, r, :], k == 0, k == 7)
                bank_done(ins, "ckv")
                wait("k_ready")
                settled("hq")
                level("dg", k_, q_)

                unit_loaded(pe, l, 3)
                u = unit_view(0, 8, 512)
                for use, i0 in (("q0", 0), ("q1", 2)):
                    bk = bank_free(pe, l, use)
                    for i in range(2):
                        ins = project_T(bk[:, i * 256:(i + 1) * 256],
                                        lambda k: u[:, k, (i0 + i) * P:(i0 + i + 1) * P], xnT)
                    bank_done(ins, use)

                unit_loaded(pe, l, 4)
                settled("ckv")
                bk = bank_free(pe, l, "cmph")
                for a in range(16):
                    for g in range(4):
                        w1 = dense[:, 1, (g // KV) * 2048 + a * P:(g // KV) * 2048 + (a + 1) * P]
                        ins = mm(bk[g * 32:(g + 1) * 32, 0:P], xe_b[:, g * 256 + a * 16:g * 256 + a * 16 + 32], w1,
                                 a == 0, a == 15)
                bank_done(ins, "cmph")
                half_level(1)

                def key_T(bk, unit, c0):
                    return project_T(bk[:, 0:256], lambda k: unit[:, k, c0:c0 + P], xnT)

                def columns_N(bk, unit, c0, n, at):
                    for tt in range(2):
                        ins = project_N(bk[:, at + tt * n:at + (tt + 1) * n], unit, c0, c0 + n, xnT, tt)
                    return ins

                u = unit_view(2, 8, 512)
                bk = bank_free(pe, l, "ksvs")
                key_T(bk, u, C_KS - C_KC)
                bank_done(columns_N(bk, u, C_KS - C_KC + P, P, 256), "ksvs")

                wait("cmp_hid")
                bk = bank_free(pe, l, "hidT")
                bank_done(pe.transpose(bk[:, 0:P], cmp_x, ident), "hidT")

                settled("q0", "q1")
                swap("rq0", qraw_b, 0)
                swap("rq1", qraw_b, 512)
                half_level(2)

                unit_loaded(pe, l, 5)
                u = unit_view(2, 8, C_CB - C_KW)
                bk = bank_free(pe, l, "kw")
                bank_done(key_T(bk, u, 0), "kw")
                bk = bank_free(pe, l, "vwgl")
                bank_done(columns_N(bk, u, P, C_CB - C_KW - P, 0), "vwgl")

                settled("hidT")
                w2 = dense[:, 2, 3968:4096].rearrange("p (a d) -> p a d", a=2)
                bk = bank_free(pe, l, "cmpo")
                for v in range(KV):
                    mm(bk[v * HD:(v + 1) * HD, 0:NCMP], w2[:, 0, :], cmp_hk[:, v, 0:NCMP], True, True)
                ins = mm(bk[:, 64:64 + P].rearrange("p (v d) -> p v d", v=KV),
                         cmp_hv[:, :, :].rearrange("p i c -> p (i c)"),
                         w2[:, 1, :].unsqueeze(1).broadcast_to([P, KV, HD]), True, True)
                bank_done(ins, "cmpo")
                settled("ksvs", "kw")
                swap("rk", kraw_b, 0)
                half_level(4)
                def scores(n):
                    bks = [bank_free(pe, l, f"s{n}_{v}") for v in range(2)]
                    br, tt, i0, nh = GROUPS[n]
                    nk = 512 // nh
                    for j in range(nh):
                        for v in range(2):
                            ch = slice(v * HD, (v + 1) * HD)
                            o = bks[v][:, j * nk:(j + 1) * nk]
                            if br == "cross":
                                ins = mm(o, cq[ch, j, tt * P:(tt + 1) * P], memk[ch, j, :], True, True)
                                if j == nh - 1:
                                    bank_done(ins, f"s{n}_{v}")
                            else:
                                mm(o, qrot[ch, i0 + j, tt * P:(tt + 1) * P],
                                   krot[ch, 0 if br == "sel" else 1, 0:nk], j == 0, False)
                    if br == "cross":
                        return
                    for v in range(2):
                        for j in range(nh):
                            ins = mm(bks[v][:, (j + 1) * nk - P:(j + 1) * nk], ident_b, causal_b, False, True)
                        bank_done(ins, f"s{n}_{v}")

                def turn_probs(n):
                    pe.wait_ge(ev("p_scaled"), l * NG + (n + 1))
                    for v in range(2):
                        bk = bank_free(pe, l, f"t{n}_{v}")
                        for c in range(4):
                            at = v * 512 + c * P
                            ins = pe.transpose(bk[:, c * P:(c + 1) * P], probs(n)[:, at:at + P], ident)
                        bank_done(ins, f"t{n}_{v}")

                def values(n):
                    wait_drained(pe, l, f"t{n}_0")
                    wait_drained(pe, l, f"t{n}_1")
                    br, tt, i0, nh = GROUPS[n]
                    nkt = 4 // nh
                    for j in range(nh):
                        for c in range(nkt):
                            for v in range(2):
                                at = v * 512 + (j * nkt + c) * P
                                if br == "cross":
                                    o = banks[6][v * HD:(v + 1) * HD, j * 256 + tt * P:j * 256 + (tt + 1) * P]
                                    vals = memv[:, c, (2 * j + v) * HD:(2 * j + v + 1) * HD]
                                    ins = mm(o, vals, pT_of(n)[:, at:at + P], c == 0, c == 1)
                                else:
                                    i = i0 + j
                                    o = banks[6 + i // 2][v * HD:(v + 1) * HD,
                                                          (i % 2) * 256 + tt * P:(i % 2) * 256 + (tt + 1) * P]
                                    ins = mm(o, v_of[br][:, c, v * HD:(v + 1) * HD], pT_of(n)[:, at:at + P], False,
                                             c == nkt - 1)
                    if n == NN - 2:
                        bank_done(ins, "o6")
                    if n == NN - 1:
                        bank_done(ins, "o7")
                    if n == NG - 1:
                        bank_done(ins, "cross_o")

                settled("cmpo")
                bks = [bank_free(pe, l, f"cmp_s_{v}") for v in range(KV)]
                for tt in range(2):
                    for i in range(GRP):
                        for v in range(KV):
                            ch = slice(v * HD, (v + 1) * HD)
                            at = (tt * GRP + i) * NCMP
                            mm(bks[v][:, at:at + NCMP], qraw[ch, i, tt * P:(tt + 1) * P], kc[ch, :],
                               tt == i == 0, False)
                for v in range(KV):
                    for tt in range(2):
                        ins = mm(bks[v][:, tt * 64:(tt + 1) * 64].rearrange("p (g c) -> p g c", c=NCMP), ident_b,
                                 cmp_no_b[:, tt, :].unsqueeze(1).broadcast_to([P, GRP, NCMP]), False, tt == 1)
                    bank_done(ins, f"cmp_s_{v}")
                wait("krot")
                wait("qrot")
                scores(0)
                unit_loaded(pe, l, 6)
                u6 = unit_view(0, 8, 512)
                two_T("cb", u6, 0, xnT)
                half_level(8)
                wait("cmp_p")
                bk = bank_free(pe, l, "cmp_t")
                for tt in range(2):
                    ins = pe.transpose(bk[:, tt * P:(tt + 1) * P], cmpP[:, tt * P:(tt + 1) * P], ident)
                bank_done(ins, "cmp_t")
                settled("cmp_t")
                bank_free(pe, l, "o6")
                bank_free(pe, l, "o7")
                for i in range(GRP):
                    mm(banks[6 + i // 2][:, (i % 2) * 256:(i % 2 + 1) * 256], vblk[:, i, :], cmpPT,
                       i % 2 == 0, False)

                scores(1)
                turn_probs(0)
                two_T("cc", u6, 256, xnT)
                values(0)
                half_level(16)
                scores(2)
                turn_probs(1)
                unit_loaded(pe, l, 8)
                two_N("hg", unit_view(2, 8, 256), 0, 256, xnT)
                values(1)
                half_level(32)
                scores(3)
                turn_probs(2)
                unit_loaded(pe, l, 7)
                two_T("ch", dense[:, 1, 0:2048].rearrange("p (k c) -> p k c", k=8), 0, xnT)
                values(2)
                half_level(64)
                scores(4)
                turn_probs(3)
                two_N("hi", dense[:, 1, 2048:4096].rearrange("p (k c) -> p k c", k=8), 0, 256, xnT)
                values(3)

                wait("qt128")
                wait("kt128")
                bks = [bank_free(pe, l, f"off_{half}") for half in range(2)]
                for c in range(2):
                    for half in range(2):
                        ch = slice(half * HD, (half + 1) * HD)
                        ins = mm(bks[half][:, c * P:(c + 1) * P], kt[1][ch, c, 0:P], qt[1][ch, c, P:256], True, True)
                        if c == 1:
                            bank_done(ins, f"off_{half}")
                scores(5)
                turn_probs(4)
                values(4)

                settled("off_0", "off_1")
                bk = bank_free(pe, l, "av")
                for hd in range(4):
                    e = slice(hd * HD, (hd + 1) * HD)
                    mm(bk[:, hd * HD:(hd + 1) * HD], A_[0][:, hd, :], hi_[:, 0, e], True, True)
                    mm(bk[:, 256 + hd * HD:256 + (hd + 1) * HD], A_[2][:, hd, :], hi_[:, 0, e], True, False)
                    ins = mm(bk[:, 256 + hd * HD:256 + (hd + 1) * HD], A_[1][:, hd, :], hi_[:, 1, e], False, True)
                bank_done(ins, "av")
                turn_probs(5)
                values(5)
                wait("hgrn_o")
                bk = bank_free(pe, l, "hot")
                for c in range(2):
                    for tt in range(2):
                        ins = pe.transpose(bk[:, (c * 2 + tt) * P:(c * 2 + tt + 1) * P],
                                           kt1_b[:, tt * 256 + c * P:tt * 256 + (c + 1) * P], ident)
                bank_done(ins, "hot")

                def out_proj(prefix, kk, lhs, rhs_of):
                    for n in range(2):
                        for tt in range(2):
                            bk = bank_free(pe, l, f"{prefix}{n * 2 + tt}")
                            for k in range(kk):
                                ins = mm(bk[:, 0:512], lhs[:, k, tt * P:(tt + 1) * P], rhs_of(n, k), k == 0, k == kk - 1)
                            bank_done(ins, f"{prefix}{n * 2 + tt}")

                wait("conv_done")
                settled("hot", "o6", "o7")
                unit_loaded(pe, l, 9)
                unit_loaded(pe, l, 10)
                out_proj("wo", 8, mixT, lambda n, k: unit_view(n, 8, 512)[:, k, :])

                pe.wait_ge(vloaded, l * 16 + 16)
                bk = bank_free(pe, l, "memv")
                w = wkv_v.rearrange("p (k c) -> p k c", k=8)
                for tt in range(2):
                    ins = project_N(bk[:, tt * 256:(tt + 1) * 256], w, 0, 256, memG, tt)
                bank_done(ins, "memv")
                turn("y", "cross")
                settled("yT0", "yT1", "yT2", "yT3")
                unit_loaded(pe, l, 11)
                two_T("cq", dense[:, 2, 0:2048].rearrange("p (k c) -> p k c", k=8), 0, xnT)
                settled("cq", "memv")
                bank_free(pe, l, "cross_o")
                for n in range(NN, NG):
                    scores(n)
                for n in range(NN, NG):
                    turn_probs(n)
                    values(n)
                settled("cross_o")
                wo_v = dense[:, 2, 2048:4096].rearrange("p (k c) -> p k c", k=2)
                out_proj("co", 2, coT, lambda n, k: wo_v[:, k, n * 512:(n + 1) * 512])

                turn("z", "ffn")
                settled("zT0", "zT1", "zT2", "zT3")
                bk = bank_free(pe, l, "rt")
                for tt in range(2):
                    for k in range(8):
                        ins = mm(bk[:, tt * 36:(tt + 1) * 36], xnT[:, k, tt * P:(tt + 1) * P],
                                 pcol(l, RW + k * 36, 36), k == 0, k == 7)
                bank_done(ins, "rt")
                wait("chosen")
                bk = bank_free(pe, l, "pos")
                mm(bk[:, 0:E], tri, chosen[:, 0, :], True, True)
                mm(bk[:, E:2 * E], ones, chosen[:, 0, :], True, False)
                mm(bk[:, E:2 * E], tri, chosen[:, 1, :], False, True)
                mm(bk[:, 2 * E:3 * E], ones, chosen[:, 0, :], True, False)
                ins = mm(bk[:, 2 * E:3 * E], ones, chosen[:, 1, :], False, True)
                bank_done(ins, "pos")

                for b in range(8):
                    wait_drained(pe, l, USES[b][-1])
                wait("npass_ready")
                alone(pe)
                npass = pe.value_load(npass_i[0:1, 0:1], min_val=1, max_val=MAXP)
                gbase = base + l

                def gather(n):
                    pe.wait_ge(onehot_ready, gbase + n + 1)
                    for b in range(2):
                        pe.wait_ge(edrained[b], gbase + n + 1)
                    for d in range(8):
                        for tt in range(2):
                            ins = mm(banks[d // 4][:, (d % 4) * P:(d % 4 + 1) * P], xhat[:, tt, d * P:(d + 1) * P],
                                     pm[:, tt, :, :].rearrange("p e s -> p (e s)"), tt == 0, tt == 1)
                        if d % 4 == 3:
                            ins.then_inc(efilled[d // 4], 1)

                gather(0)
                with pe.Fori(0, npass * PAIRS) as t:
                    it = base + t
                    for b in range(2):
                        pe.wait_ge(edrained[b], gbase + t + 2)
                        pe.wait_ge(edrained[2 + b], it + 1)
                    for k in range(8):
                        for n in range(2):
                            for e in range(2):
                                s = k // 4 * 2 + e
                                if k % 4 == n == 0:
                                    pe.wait_ge(eloaded[s], it * 16 + 16)
                                w = eslot(s)[:, (k % 4) * 1024 + n * 512:(k % 4) * 1024 + (n + 1) * 512]
                                half = slice(e * SLOTS, (e + 1) * SLOTS)
                                ins = mm(banks[2 + n][half, 0:512], xg[:, k, half], w, k == 0, k == 7)
                            if k == 7:
                                ins.then_inc(efilled[2 + n], 1)
                        if k == 3:
                            ins.then_inc(half_read, 1)
                    gather(t + 1)
                    pe.wait_ge(pg_ready, it + 1)
                    pe.wait_ge(edrained[7], it * 2 + 1)
                    for tt in range(2):
                        ins = pe.transpose(banks[7][:, tt * P:(tt + 1) * P],
                                           pg[:, tt, :, :].rearrange("p e s -> p (e s)"), ident)
                    ins.then_inc(efilled[7], 1)
                    pe.wait_ge(edrained[3], it + 2)
                    pe.wait_ge(edrained[6], it * 2 + 1)
                    for k in range(4):
                        ins = pe.transpose(banks[6][:, k * P:(k + 1) * P], hid[:, k * P:(k + 1) * P], ident)
                    ins.then_inc(efilled[6], 1)
                    pe.wait_ge(edrained[6], it * 2 + 2)
                    for b in (4, 5):
                        pe.wait_ge(edrained[b], it * 2 + 1)
                    for k in range(4):
                        for n in range(2):
                            for e in range(2):
                                if k == n == 0:
                                    pe.wait_ge(eloaded[4 + e], it * 16 + 16)
                                w = eslot(4 + e)[:, k * 1024 + n * 512:k * 1024 + (n + 1) * 512]
                                half = slice(e * SLOTS, (e + 1) * SLOTS)
                                ins = mm(banks[4 + n][half, 0:512], ht[:, k, half], w, k == 0, k == 3)
                            if k == 3:
                                ins.then_inc(efilled[4 + n], 1)
                    pe.wait_ge(edrained[7], it * 2 + 2)
                    for n in range(2):
                        pe.wait_ge(edrained[4 + n], it * 2 + 2)
                    for tt in range(2):
                        for n in range(2):
                            b = (6 if tt == 0 else 4) + n
                            mm(banks[b][:, 0:512], pgT[:, tt * P:(tt + 1) * P], ys_b[:, n * 512:(n + 1) * 512],
                               True, True).then_inc(efilled[b], 1)
                end = base + npass * PAIRS
                for b in (0, 1):
                    pe.wait_ge(edrained[b], end + l + 2)
                for b in (2, 3):
                    pe.wait_ge(edrained[b], end + 1)
                for b in (4, 5, 6, 7):
                    pe.wait_ge(edrained[b], end * 2 + 1)
                pe.reg_add(iters, iters, npass * PAIRS)

        @block.scalar
        def _(act):
            def copy(out_ap, in_ap, scale=1.0):
                return act.activation(out_ap, in_ap, ACT.Copy, scale=scale)

            act.wait_ge(s_mem, 16)
            for tt in range(2):
                ins = act.activation(mem_sq[:, tt, :], mem_raw[:, tt, :], ACT.Square, accum_out=ssq[:, tt:tt + 1])
            ins.then_inc(ev("mem_squares"), 1)
            act.wait_ge(ev("lb_in"), 1)
            act.activation(flat(oml[:, :, :]), flat(lbf[:, :, :]), ACT.Exp).then_inc(ev("lb_exp"), 1)
            iters = act.alloc_register("act_iters")
            act.reg_mov(iters, 0)
            with act.Fori(0, DEPTH) as l:
                base = act.snap(iters, min_val=0, max_val=DEPTH * MAXP * PAIRS)

                def wait(name):
                    act.wait_ge(ev(name), l + 1)

                def drain(use, pairs):
                    bk = bank_full(act, l, use)
                    for out_ap, part, scale in pairs:
                        ins = copy(out_ap, part(bk), scale)
                    return ins

                def squares(stage):
                    wait("h_" + stage)
                    for tt in range(2):
                        ins = act.activation(xhat[:, tt, :], h[:, tt, :], ACT.Square, accum_out=ssq[:, tt:tt + 1])
                    ins.then_inc(ev("squares_" + stage), 1)

                def scale0(stage):
                    wait("rstd_" + stage)
                    act.activation(xhat[:, 0, :], h[:, 0, :], ACT.Identity,
                                   scale=rs[:, 0:1]).then_inc(ev("xhat0_" + stage), 1)

                def turned(prefix, gain):
                    for j in (1, 3):
                        bk = bank_full(act, l, f"{prefix}T{j}")
                        for d in range(2):
                            ins = act.activation(xnT[:, 2 * j + d, :], bk[:, d * 256:(d + 1) * 256], ACT.Identity,
                                                 scale=pcol(l, gain + 2 * j + d, 1))
                        bank_drained(ins, f"{prefix}T{j}")

                def whole(bk):
                    return bk[:, 0:512]

                squares("mix")
                bank_drained(drain("memk", [(flat(memk), whole, 1.0)]), "memk")
                scale0("mix")
                turned("x", G_MIX)

                bk = bank_full(act, l, "hf")
                bank_drained(act.activation(f_b, whole(bk), ACT.Exp, scale=-1.0), "hf")
                bank_drained(drain("hq", [(q_b, whole, HD ** -0.5)]), "hq")
                bank_drained(drain("q0", [(qraw_b[:, 0:512], whole, 1.0)]), "q0")
                bank_drained(drain("q1", [(qraw_b[:, 512:1024], whole, 1.0)]), "q1")
                bk = bank_full(act, l, "cmph")
                act.activation(cmp_e, bk[:, 0:P], ACT.Exp, scale=-1.0).then_inc(ev("cmp_e"), 1)
                bank_drained(drain("ksvs", [(kraw[:, 0, :], lambda b: b[:, 0:256], 1.0),
                                            (vv[:, 0:256], lambda b: b[:, 256:512], 1.0)]), "ksvs")
                bk = bank_full(act, l, "hidT")
                copy(flat(cmp_hk[:, :, :]), bk[:, 0:64])
                hid_v = bk[:, 64:128].rearrange("p (v c) -> p v c", v=KV)[:, :, 0:NCMP]
                for i in range(GRP):
                    ins = copy(cmp_hv[:, i, :].rearrange("p (v c) -> p v c", v=KV), hid_v)
                bank_drained(ins, "hidT")
                bank_drained(drain("kw", [(kraw[:, 1, :], lambda b: b[:, 0:256], 1.0)]), "kw")
                bk = bank_full(act, l, "vwgl")
                b3 = bk[:, 0:304].rearrange("p (t c) -> p t c", t=2)
                copy(v_of["win"], b3[:, :, 0:P])
                bank_drained(act.activation(gate[:, :, :], b3[:, :, P:152], ACT.Exp, scale=-1.0), "vwgl")

                def exps(n):
                    nh = GROUPS[n][3]
                    nk = 512 // nh
                    act.wait_ge(ev("max_ready"), l * NG + (n + 1))
                    for v in range(2):
                        bk = banks[PLACE[f"s{n}_{v}"][0]]
                        for j in range(nh):
                            at = v * 512 + j * nk
                            s = v * nh + j
                            ins = act.activation(probs(n)[:, at:at + nk], bk[:, j * nk:(j + 1) * nk], ACT.Exp,
                                                 bias=att_nb[n % 2][:, s:s + 1], scale=HD ** -0.5,
                                                 accum_out=att_sum[n % 2][:, s:s + 1])
                        bank_drained(ins, f"s{n}_{v}")

                def keep_pT(n):
                    bank_drained(drain(f"t{n}_0", [(pT_of(n)[:, 0:512], whole, 1.0)]), f"t{n}_0")

                wait("cmp_shifted")
                act.activation(cmpP, cmpP, ACT.Exp,
                               scale=HD ** -0.5).then_inc(ev("cmp_exp"), 1)
                exps(0)
                bank_drained(drain("cb", [(cvb_b, whole, 1.0)]), "cb")
                bank_drained(drain("cmp_t", [(cmpPT, lambda b: b[:, 0:256], 1.0)]), "cmp_t")
                exps(1)
                keep_pT(0)
                bank_drained(drain("cc", [(cvc_b, whole, 1.0)]), "cc")
                exps(2)
                keep_pT(1)
                bk = bank_full(act, l, "hg")
                act.activation(hgs_b, whole(bk), ACT.Exp, scale=-1.0)
                bank_drained(copy(hgr_b, whole(bk)), "hg")
                exps(3)
                keep_pT(2)
                bank_drained(drain("ch", [(cvh_b, whole, 1.0)]), "ch")
                exps(4)
                keep_pT(3)
                bank_drained(drain("hi", [(hi_b, whole, 1.0)]), "hi")
                for half in range(2):
                    use = f"off_{half}"
                    ao = A_[2].rearrange("p (c h) t -> p c h t", h=2)[:, :, half, :]
                    bank_drained(drain(use, [(ao, lambda b: two(b[:, 0:256]), 1.0)]), use)
                exps(5)
                keep_pT(4)
                bk = bank_full(act, l, "av")
                act.activation(kt0_b, whole(bk), ACT.Square).then_inc(ev("o_squares"), 1)
                keep_pT(5)
                bank_drained(drain("o6", [(flat(mixT[:, 0:2, :]), whole, 1.0)]), "o6")
                bk = bank_full(act, l, "hot")
                for c in range(2):
                    ins = act.activation(mixT[:, 6 + c, :], bk[:, c * 256:(c + 1) * 256], ACT.Identity,
                                         scale=pcol(l, HNORM + c, 1))
                bank_drained(ins, "hot")

                squares("cross")
                scale0("cross")
                bank_drained(drain("memv", [(flat(memv), whole, 1.0)]), "memv")
                turned("y", G_CROSS)
                bank_drained(drain("cq", [(flat(cq), whole, 1.0)]), "cq")
                for n in range(NN, NG):
                    exps(n)
                for n in range(NN, NG):
                    keep_pT(n)
                bank_drained(drain("cross_o", [(flat(coT), whole, 1.0)]), "cross_o")

                squares("ffn")
                scale0("ffn")
                turned("z", G_FFN)
                wait("route_in")
                act.activation(flat(rexp), flat(rlog), ACT.Exp).then_inc(ev("route_exp"), 1)

                wait("npass_ready")
                alone(act)
                npass = act.value_load(npass_i[0:1, 0:1], min_val=1, max_val=MAXP)
                with act.Fori(0, npass * PAIRS) as t:
                    it = base + t
                    act.wait_ge(efilled[2], it + 1)
                    act.activation(sgate, banks[2][:, 0:512], ACT.Silu).then_inc(edrained[2], 1)
                    act.wait_ge(efilled[6], it * 2 + 1)
                    act.activation(ht_b, banks[6][:, 0:512], ACT.Copy).then_inc(edrained[6], 1)
                    act.wait_ge(efilled[4], it * 2 + 1)
                    act.activation(ys_b[:, 0:512], banks[4][:, 0:512], ACT.Copy).then_inc(edrained[4], 1)
                act.reg_add(iters, iters, npass * PAIRS)

            act.wait_ge(ev("h_mix"), DEPTH + 1)
            for tt in range(2):
                ins = act.activation(xhat[:, tt, :], h[:, tt, :], ACT.Square, accum_out=ssq[:, tt:tt + 1])
            ins.then_inc(ev("squares_final"), 1)
            act.wait_ge(ev("rstd_final"), 1)
            act.activation(xhat[:, 0, :], h[:, 0, :], ACT.Identity, scale=rs[:, 0:1]).then_inc(ev("xhat0_final"), 1)

        @block.gpsimd
        def _(pool):
            for b in range(8):
                pool.memset(scratch[:, b:b + 1], 0.0).then_inc(edrained[b], 1)
            for b in range(4, 8):
                pool.memset(scratch[:, 4 + b:5 + b], 0.0).then_inc(drained[b], 1)
            pool.wait_ge(s_setup, 16 * N_SETUP)
            pool.wait_ge(ev("memT_ready"), 1)
            with pool.Fori(0, DEPTH) as l:
                chain = Chain(pool, pool_step, l * POOL_STEPS, POOL_STEPS, apart=True)

                def wait(name):
                    pool.wait_ge(ev(name), l + 1)
                    alone(pool)

                def tt_(out_ap, a, c, op):
                    return pool.tensor_tensor(out_ap, a, c, op)

                wait("h_mix")
                gain = pcol(l, G_MEM, 8).unsqueeze(2).broadcast_to([P, 8, 256])
                tt_(memG, memT[:, :, :], gain, ALU.mult).then_inc(ev("memG"), 1)
                pool.tensor_copy(cvw[:, :], pcol(l, CONVW, 6)).then_inc(ev("conv_w"), 1)
                chain.link(pool.memset(cv_u[:, :, 0:2], 0.0))
                chain.link(pool.memset(g_b, 1.0))
                chain.link(pool.memset(a0_b, 0.0))
                chain.link(pool.memset(xe[:, :, :, NCMP - 1], 0.0))
                chain.link(pool.memset(xe_b[:, 1024:1040], 0.0))
                pool.memset(a1_b, 0.0).then_inc(ev("a_zero"), 1)

                def halves(ap, L):
                    return ap.rearrange("p (n s u) -> p n s u", s=2, u=L)

                def lower(L):
                    return halves(g_b, L)[:, :, 0, :]

                wait("f_ready")
                tot_at = {}
                at = 0
                for L in HALVES[1:]:
                    tot_at[L] = tot[:, at:at + 512 // L]
                    at += 512 // L
                chain.link(pool.tensor_copy(lower(1), halves(f_b, 1)[:, :, 1, :]))
                ff = f_b.rearrange("p (n s) -> p n s", s=2)
                tt_(tot_at[2], ff[:, :, 0], ff[:, :, 1], ALU.mult).then_inc(ev("tot2"), 1)
                wait("tot2")
                wait("k_ready")
                for L in HALVES[1:] + [128]:
                    i = (HALVES + [128]).index(L)
                    if i >= 3:
                        bank_full(pool, l, f"lv{L // 4}_1")
                    tt_(kt_b[i % 2], k_b, g_b, ALU.mult).then_inc(ev(f"kt{L}"), 1)
                    if L == 128:
                        break
                    tv = tot_at[L].rearrange("p (n s) -> p n s", s=2)
                    wait(f"kt{L}")
                    chain.link(tt_(lower(L), lower(L), tv[:, :, 1].unsqueeze(2).broadcast_to([P, 256 // L, L]), ALU.mult))
                    if L < 64:
                        chain.link(tt_(tot_at[2 * L], tv[:, :, 0], tv[:, :, 1], ALU.mult))
                    if L == 4:
                        wait_drained(pool, l, "q0")
                        wait_drained(pool, l, "q1")
                        tt_(qrot, qraw, cos.unsqueeze(1).broadcast_to([P, GRP, 256]), ALU.mult).then_inc(ev("q_cos"), 1)
                    if L == 8:
                        wait_drained(pool, l, "ksvs")
                        wait_drained(pool, l, "kw")
                        tt_(krot, kraw, cos.unsqueeze(1).broadcast_to([P, 2, 256]), ALU.mult).then_inc(ev("k_cos"), 1)

                wait_drained(pool, l, "ch")
                wait_drained(pool, l, "cb")
                wait_drained(pool, l, "cc")
                wait("conv_w")
                chain.link(tt_(cv_u[:, :, 2:258], cv_c, cv_h, ALU.mult))
                for c in range(2):
                    ins = pool.tensor_scalar(cv_y[:, c, :], cv_u[:, c, 0:256], cvw[:, c * 3:c * 3 + 1], None, ALU.mult)
                chain.link(ins)
                for tap in (1, 2):
                    for c in range(2):
                        ins = pool.tensor_scalar(cv_h[:, c, :], cv_u[:, c, tap:tap + 256],
                                                 cvw[:, c * 3 + tap:c * 3 + tap + 1], None, ALU.mult)
                    chain.link(ins)
                    chain.link(tt_(cvy_b, cvy_b, cvh_b, ALU.add))
                tt_(flat(mixT[:, 4:6, :]), cvy_b, cvb_b, ALU.mult).then_inc(ev("conv_done"), 1)
                chain.close()

        @block.vector
        def _(dve):
            V = dve
            MUL, ADD, SUB, MAX, MIN, EQ, GT = (ALU.mult, ALU.add, ALU.subtract, ALU.max, ALU.min, ALU.is_equal,
                                               ALU.is_gt)
            setup = Chain(dve, setup_step, 0, None)

            def bc(ap, *shape):
                return ap.broadcast_to([P, *shape])

            def inverse_root(link, y, squares, scale):
                n = y.shape[1]
                x, t = root_x[:, 0:n], root_t[:, 0:n]
                link(V.tensor_scalar(x, squares, scale, EPS, MUL, ADD))
                link(V.tensor_scalar(t.bitcast(I32), x.bitcast(I32), 1, None, ALU.logical_shift_right))
                link(V.tensor_scalar(y.bitcast(I32), t.bitcast(I32), -1.0, float(0x5F3759DF), MUL, ADD))
                for step in range(3):
                    link(V.tensor_tensor(t, y, y, MUL))
                    link(V.scalar_tensor_tensor(t, t, -0.5, x, MUL, MUL))
                    ins = V.scalar_tensor_tensor(y, t, 1.5, y, ADD, MUL)
                    if step < 2:
                        link(ins)
                return ins

            dve.wait_ge(s_mem, 16)
            dve.wait_ge(ev("mem_squares"), 1)
            setup.link(inverse_root(setup.link, rs, ssq, 1.0 / D))
            for tt in range(2):
                V.tensor_scalar(mem_raw[:, tt, :], mem_raw[:, tt, :], rs[:, tt:tt + 1], None,
                                MUL).then_inc(ev("mem_hat"), 1)
            dve.wait_ge(s_setup, 16 * N_SETUP)
            V.tensor_copy(lvmask[:, :, :], mask_in).then_inc(ev("masks"), 1)
            V.tensor_copy(cbf[:, :], rest[:, 1024:1312]).then_inc(ev("masks"), 1)

            mx, tot_, run = lbt[:, 0:2], lbt[:, 2:4], lbt[:, 4:6]
            setup.link(V.tensor_reduce(mx, lb_in[:, :, :].rearrange("p l c -> p c l"), AX, MAX))
            V.tensor_tensor(lbf[:, :, :], lb_in[:, :, :], bc(mx.unsqueeze(1), DEPTH, 2), SUB).then_inc(ev("lb_in"), 1)
            V.memset(posv[:, :, MAXP * E:COLS], -1.0)
            V.memset(gates[:, :, MAXP * E:COLS], 0.0)
            dve.wait_ge(ev("lb_exp"), 1)
            setup.link(V.tensor_reduce(tot_, oml[:, :, :].rearrange("p l c -> p c l"), AX, ADD))
            setup.link(V.reciprocal(tot_, tot_))
            setup.link(V.tensor_tensor(oml[:, :, :], oml[:, :, :], bc(tot_.unsqueeze(1), DEPTH, 2), MUL))
            setup.link(V.tensor_copy(lbf[:, 0, :], oml[:, 0, :]))
            for j in range(1, DEPTH):
                setup.link(V.tensor_tensor(lbf[:, j, :], lbf[:, j - 1, :], oml[:, j, :], ADD))
            setup.link(V.tensor_copy(run, oml[:, 0, :]))
            setup.link(V.tensor_tensor(lbf[:, :, :], lbf[:, :, :], bc(run.unsqueeze(1), DEPTH, 2), SUB))
            setup.link(V.tensor_scalar(oml[:, :, :], lbf[:, :, :], -1.0, 1.0, MUL, ADD))
            setup.link(V.tensor_scalar(lbf[:, :, :], lbf[:, :, :], LB_FLOOR, None, MAX))
            dve.wait_ge(ev("mem_turned"), 1)
            for j in range(4):
                V.tensor_copy(flat(memT[:, 2 * j:2 * j + 2, :]), banks[j][:, 0:512]).then_inc(drained[j], 1)
            for j in range(4):
                dve.wait_ge(drained[j], 1)
            dve.wait_ge(ev("masks"), 2)
            V.memset(scratch[:, 24:25], 0.0).then_inc(ev("memT_ready"), 1)

            iters = dve.alloc_register("dve_iters")
            dve.reg_mov(iters, 0)
            with dve.Fori(0, DEPTH) as l:
                base = dve.snap(iters, min_val=0, max_val=DEPTH * MAXP * PAIRS)
                chain = Chain(dve, dve_step, l * DVE_STEPS, DVE_STEPS)
                link = chain.link

                def wait(name):
                    dve.wait_ge(ev(name), l + 1)

                def own(name, ins):
                    ins.then_inc(ev(name), 1)
                    wait(name)

                def rstd(stage):
                    wait("squares_" + stage)
                    own("rstd_" + stage, inverse_root(link, rs, ssq, 1.0 / D))
                    V.tensor_scalar(xhat[:, 1, :], h[:, 1, :], rs[:, 1:2], None, MUL).then_inc(ev("xhat1_" + stage), 1)

                def turned(prefix, gain):
                    for j in (0, 2):
                        bk = bank_full(dve, l, f"{prefix}T{j}")
                        g = bc(pcol(l, gain + 2 * j, 2).unsqueeze(2), 2, 256)
                        bank_drained(V.tensor_tensor(xnT[:, 2 * j:2 * j + 2, :], two(bk[:, 0:512]), g, MUL),
                                     f"{prefix}T{j}")

                def add_out(prefix):
                    for n in range(2):
                        for tt in range(2):
                            bk = bank_full(dve, l, f"{prefix}{n * 2 + tt}")
                            hh = h[:, tt, n * 512:(n + 1) * 512]
                            ins = V.tensor_tensor(hh, hh, bk[:, 0:512], ADD)
                            bank_drained(ins, f"{prefix}{n * 2 + tt}")
                    for n in range(4):
                        wait_drained(dve, l, f"{prefix}{n}")

                def done(name, col):
                    V.memset(scratch[:, col:col + 1], 0.0).then_inc(ev(name), 1)

                done("h_mix", 25)
                rstd("mix")
                turned("x", G_MIX)

                wait_drained(dve, l, "hf")
                link(V.tensor_scalar(tmp, f_b, 1e37, 1.0, MIN, ADD))
                link(V.reciprocal(tmp, tmp))
                link(V.scalar_tensor_tensor(k_b, f_b, 1e37, tmp, MIN, MUL))
                for c in range(2):
                    ins = V.tensor_scalar(f_[:, c, :], two(tmp)[:, c, :], oml[:, l, c:c + 1], lbf[:, l, c:c + 1],
                                          MUL, ADD)
                own("f_ready", ins)
                for c in range(2):
                    ins = V.tensor_scalar(k_[:, c, :], k_[:, c, :], oml[:, l, c:c + 1], None, MUL)
                ins.then_inc(ev("k_ready"), 1)

                def level_q(L):
                    i = (HALVES + [128]).index(L)
                    own(f"qt{L}", V.tensor_tensor(qt_b[i % 2], q_b, f_b, MUL))
                    if L == 1:
                        wait("tot2")
                    if L < 128:
                        ff = f_b.rearrange("p (n s u) -> p n s u", s=2, u=L)
                        link(V.tensor_tensor(ff[:, :, 1, :], ff[:, :, 1, :],
                                             bc(ff[:, :, 0, L - 1:L], 256 // L, L), MUL))

                def level_mask(name, m):
                    for half in range(2):
                        use = f"{name}_{half}"
                        bk = bank_full(dve, l, use)
                        if m > 0:
                            wait_drained(dve, l, f"{prev_level[name]}_{half}")
                        alone(dve)
                        bank_drained(V.copy_predicated(a01[:, :, half, :], bc(lvmask[:, m, :].unsqueeze(1), 4, P),
                                                       bk[:, 0:512].rearrange("p (n t) -> p n t", n=4)), use)

                prev_level = {"lv1": "dg"} | {f"lv{2 * L}": f"lv{L}" for L in HALVES[:-1]}
                def rotate(use, rot, name, last):
                    bk = bank_full(dve, l, use)
                    s = bc(sin.unsqueeze(1), 2, 256)
                    bank_drained(V.tensor_tensor(two(tmp), two(bk[:, 0:512]), s, MUL), use)
                    wait_drained(dve, l, use)
                    wait(name + "_cos")
                    ins = V.tensor_tensor(rot, rot, tmp, ADD)
                    if last:
                        ins.then_inc(ev(name + "rot"), 1)
                    else:
                        link(ins)

                def maxima(n):
                    nh = GROUPS[n][3]
                    for v in range(2):
                        bk = bank_full(dve, l, f"s{n}_{v}")
                        ins = V.tensor_reduce(att_mx[n % 2][:, v * nh:(v + 1) * nh],
                                              bk[:, 0:512].rearrange("p (h k) -> p h k", h=nh), AX, MAX)
                    link(ins)
                    V.tensor_scalar(att_nb[n % 2][:, 0:2 * nh], att_mx[n % 2][:, 0:2 * nh], -HD ** -0.5, None,
                                    MUL).then_inc(ev("max_ready"), 1)

                def normalise(n):
                    br, tt, i0, nh = GROUPS[n]
                    for v in range(2):
                        wait_drained(dve, l, f"s{n}_{v}")
                    r = att_rr[n % 2][:, 0:2 * nh]
                    link(V.reciprocal(r, att_sum[n % 2][:, 0:2 * nh]))
                    if br != "cross":
                        gv = gate[:, tt, :].rearrange("p (v i b) -> p v i b", v=KV, i=GRP)
                        r2 = r.rearrange("p (v i) -> p v i", v=KV)
                        link(V.tensor_tensor(r2, r2, gv[:, :, i0:i0 + nh, 1 if br == "sel" else 2], MUL))
                    pp = probs(n).rearrange("p (h k) -> p h k", h=2 * nh)
                    V.tensor_tensor(pp, pp, bc(r.unsqueeze(2), 2 * nh, 512 // nh), MUL).then_inc(ev("p_scaled"), 1)

                def keep_pT(n):
                    bk = bank_full(dve, l, f"t{n}_1")
                    bank_drained(V.tensor_copy(pT_of(n)[:, 512:1024], bk[:, 0:512]), f"t{n}_1")

                wait_drained(dve, l, "hq")
                level_q(1)
                bk = bank_full(dve, l, "ckv")
                b3 = bk[:, 0:512].rearrange("p (g u) -> p g u", g=4)
                for s in range(2):
                    for a in (0, 8):
                        pe_ = pcol(l, PE_C + s * 16 + a, 8).unsqueeze(1).unsqueeze(3)
                        ins = V.tensor_tensor(
                            xe[:, s * 2:s * 2 + 2, a:a + 8, 0:15],
                            b3[:, s * 2:s * 2 + 2, a:a + 120].rearrange("p g (c a) -> p g a c", a=8),
                            bc(pe_, 2, 8, 15), ADD)
                wait("a_zero")
                bank_drained(ins, "ckv")
                level_mask("dg", 0)
                level_q(2)
                bk = bank_full(dve, l, "cmph")
                wait("cmp_e")
                link(V.tensor_scalar(cmp_e, cmp_e, 1.0, None, ADD))
                link(V.reciprocal(cmp_e, cmp_e))
                own("cmp_hid", V.tensor_tensor(cmp_x, cmp_e, bk[:, 0:P], MUL))
                bank_drained(V.memset(scratch[:, 26:27], 0.0), "cmph")
                level_mask("lv1", 1)
                level_q(4)
                rotate("rq0", qrot_b[:, 0:512], "q", False)
                rotate("rq1", qrot_b[:, 512:1024], "q", True)
                level_mask("lv2", 2)
                level_q(8)
                wait_drained(dve, l, "vwgl")
                gf = flat(gate[:, :, :])
                link(V.tensor_scalar(gf, gf, 1.0, None, ADD))
                link(V.reciprocal(gf, gf))
                bk = bank_full(dve, l, "cmpo")
                V.tensor_copy(kc[:, :], bk[:, 0:NCMP])
                bank_drained(V.tensor_tensor(
                    vblk.rearrange("p i (v d) -> p i v d", v=KV),
                    bc(bk[:, 64:64 + P].rearrange("p (v d) -> p v d", v=KV).unsqueeze(1), GRP, KV, HD),
                    bc(own_block.unsqueeze(3), GRP, KV, HD), MUL), "cmpo")
                rotate("rk", krot_b, "k", True)
                level_mask("lv4", 3)
                level_q(16)

                cp = cmpP.rearrange("p (g c) -> p g c", c=NCMP)
                cp4 = cmpP.rearrange("p (g v c) -> p g v c", v=KV, c=NCMP)
                for v in range(KV):
                    bk = bank_full(dve, l, f"cmp_s_{v}")
                    sc = bk[:, 0:128].rearrange("p (g c) -> p g c", c=NCMP)
                    link(V.tensor_reduce(cmx[:, v * 8:(v + 1) * 8], sc, AX, MAX))
                    bank_drained(V.tensor_tensor(cp4[:, :, v, :], sc,
                                                 bc(cmx[:, v * 8:(v + 1) * 8].unsqueeze(2), 8, NCMP), SUB),
                                 f"cmp_s_{v}")
                for v in range(KV):
                    wait_drained(dve, l, f"cmp_s_{v}")
                done("cmp_shifted", 27)
                maxima(0)
                wait("cmp_exp")
                for tt in range(2):
                    ct = cmpP[:, tt * P:(tt + 1) * P].rearrange("p (g c) -> p g c", c=NCMP)
                    ins = V.tensor_tensor(ct, ct, bc(cmp_ok[:, tt, :].unsqueeze(1), 8, NCMP), MUL)
                link(ins)
                link(V.tensor_reduce(csum, cp, AX, ADD))
                link(V.tensor_scalar(csum, csum, 1e-30, None, MAX))
                link(V.reciprocal(crr, csum))
                g0 = gate[:, :, :].rearrange("p t (v i b) -> p t i v b", v=KV, i=GRP)
                for tt in range(2):
                    c2 = crr[:, tt * 8:(tt + 1) * 8].rearrange("p (i v) -> p i v", v=KV)
                    ins = V.tensor_tensor(c2, c2, g0[:, tt, :, :, 0], MUL)
                link(ins)
                V.tensor_tensor(cp, cp, bc(crr.unsqueeze(2), 16, NCMP), MUL).then_inc(ev("cmp_p"), 1)

                level_mask("lv8", 4)
                level_q(32)
                normalise(0)
                maxima(1)
                keep_pT(0)
                level_mask("lv16", 5)
                level_q(64)
                normalise(1)
                maxima(2)
                keep_pT(1)
                level_mask("lv32", 6)
                level_q(128)
                normalise(2)
                maxima(3)
                keep_pT(2)
                wait_drained(dve, l, "hg")
                link(V.tensor_scalar(hgs_b, hgs_b, 1.0, None, ADD))
                link(V.reciprocal(hgs_b, hgs_b))
                link(V.tensor_tensor(hgs_b, hgs_b, hgr_b, MUL))
                level_mask("lv64", 7)
                normalise(3)
                maxima(4)
                keep_pT(3)
                normalise(4)
                maxima(5)
                keep_pT(4)
                normalise(5)
                wait("o_squares")
                link(V.tensor_reduce(hsum, kt0_b.rearrange("p (g e) -> p g e", e=HD), AX, ADD))
                link(inverse_root(link, hrs, hsum, 1.0 / HD))
                bk = bank_full(dve, l, "av")
                o_ = kt1_b.rearrange("p (g e) -> p g e", e=HD)
                bank_drained(V.tensor_tensor(o_, bk[:, 0:512].rearrange("p (g e) -> p g e", e=HD),
                                             bc(hrs.unsqueeze(2), 8, HD), MUL), "av")
                wait_drained(dve, l, "av")
                V.tensor_tensor(kt1_b, kt1_b, hgs_b, MUL).then_inc(ev("hgrn_o"), 1)
                keep_pT(5)
                bk = bank_full(dve, l, "o7")
                bank_drained(V.tensor_copy(flat(mixT[:, 2:4, :]), bk[:, 0:512]), "o7")

                add_out("wo")
                done("h_cross", 28)
                rstd("cross")
                turned("y", G_CROSS)
                for n in range(NN, NG):
                    maxima(n)
                for n in range(NN, NG):
                    normalise(n)
                    keep_pT(n)
                add_out("co")
                done("h_ffn", 29)
                rstd("ffn")
                turned("z", G_FFN)

                bk = bank_full(dve, l, "rt")
                lg = rl[:, :, 0:4]
                le = rl[:, :, 4:36]
                bank_drained(V.tensor_tensor(rl, bk[:, 0:72].rearrange("p (t c) -> p t c", t=2),
                                             bc(pcol(l, RBIAS, 36).unsqueeze(1), 2, 36), ADD), "rt")
                wait_drained(dve, l, "rt")

                def first_of_max(best, vals, iota, n, onehot):
                    link(V.tensor_tensor(onehot, vals, bc(best.unsqueeze(2), 2, n), EQ))
                    link(V.tensor_tensor(onehot, onehot, bc(iota.unsqueeze(1), 2, n), MUL))
                    link(V.tensor_reduce(r_min, onehot, AX, MIN))
                    link(V.tensor_tensor(onehot, bc(iota.unsqueeze(1), 2, n), bc(r_min.unsqueeze(2), 2, n), EQ))

                link(V.tensor_reduce(r_mg, lg, AX, MAX))
                first_of_max(r_mg, lg, iota_g, 4, r_g1)
                link(V.tensor_tensor(rlog[:, :, 0:4], lg, bc(r_mg.unsqueeze(2), 2, 4), SUB))
                for tt in range(2):
                    ins = V.tensor_copy(r_in[:, tt, :].rearrange("p (g e) -> p g e", g=4),
                                        bc(r_g1[:, tt, :].unsqueeze(2), 4, 8))
                link(ins)
                link(V.tensor_scalar(r_out, r_in, -1.0, None, ADD))
                link(V.tensor_tensor(le, le, r_in, MUL))
                link(V.scalar_tensor_tensor(le, r_out, 1e30, le, MUL, ADD))
                link(V.tensor_reduce(r_me, le, AX, MAX))
                link(V.tensor_tensor(rlog[:, :, 4:36], le, bc(r_me.unsqueeze(2), 2, 32), SUB))
                done("route_in", 30)
                wait("route_exp")
                link(V.tensor_reduce(r_sg, rexp[:, :, 0:4], AX, ADD))
                ee = rexp[:, :, 4:36]
                link(V.tensor_tensor(ee, ee, r_out, ADD))
                link(V.tensor_reduce(r_e1, ee, AX, MAX))
                first_of_max(r_e1, ee, iota_e, 32, r_o1)
                link(V.scalar_tensor_tensor(ee, r_o1, -4.0, ee, MUL, ADD))
                link(V.tensor_reduce(r_e2, ee, AX, MAX))
                first_of_max(r_e2, ee, iota_e, 32, r_o2)
                own("chosen", V.tensor_tensor(chosen, r_o1, r_o2, ADD))
                link(V.tensor_tensor(r_t, r_e1, r_e2, ADD))
                link(V.tensor_tensor(r_t, r_t, r_sg, MUL))
                link(V.reciprocal(r_t, r_t))
                link(V.tensor_tensor(r_e1, r_e1, r_t, MUL))
                link(V.tensor_tensor(r_e2, r_e2, r_t, MUL))
                link(V.tensor_tensor(r_o1, r_o1, bc(r_e1.unsqueeze(2), 2, 32), MUL))
                link(V.tensor_tensor(r_o2, r_o2, bc(r_e2.unsqueeze(2), 2, 32), MUL))
                for p_ in range(MAXP):
                    ins = V.tensor_tensor(gates[:, :, p_ * E:(p_ + 1) * E], r_o1, r_o2, ADD)
                link(ins)
                bk = bank_full(dve, l, "pos")
                link(V.tensor_reduce(r_cnt, bk[:, 2 * E:3 * E], AX, MAX))
                pos0 = posv[:, :, 0:E]
                bank_drained(V.scalar_tensor_tensor(pos0, bk[:, 0:2 * E].rearrange("p (t e) -> p t e", t=2), 1.0,
                                                    chosen, ADD, MUL), "pos")
                wait_drained(dve, l, "pos")
                link(V.tensor_scalar(pos0, pos0, -1.0, None, ADD))
                for p_ in range(1, MAXP):
                    ins = V.tensor_scalar(posv[:, :, p_ * E:(p_ + 1) * E], pos0, -float(p_ * SLOTS), None, ADD)
                    link(ins)
                link(V.memset(r_np, 1.0))
                for p_ in range(1, MAXP):
                    link(V.scalar_tensor_tensor(r_np, r_cnt, float(p_ * SLOTS), r_np, GT, ADD))
                own("npass_ready", V.tensor_copy(npass_i[0:1, 0:1], r_np[0:1, :]))
                chain.close()

                alone(dve)
                npass = dve.value_load(npass_i[0:1, 0:1], min_val=1, max_val=MAXP)
                gbase = base + l

                def onehot(col):
                    for tt in range(2):
                        ins = V.tensor_tensor(pm[:, tt, :, :], bc(iota_slot.unsqueeze(1), 2, SLOTS),
                                              bc(posv[:, tt, col].unsqueeze(2), 2, SLOTS), EQ)
                    return ins

                def gathered(n):
                    for b in range(2):
                        dve.wait_ge(efilled[b], gbase + n + 1)
                        g = bc(pcol(l, G_FFN + 4 * b, 4).unsqueeze(2), 4, P)
                        V.tensor_tensor(xg[:, 4 * b:4 * b + 4, :], banks[b][:, 0:512].rearrange("p (d s) -> p d s", d=4),
                                        g, MUL).then_inc(edrained[b], 1)

                onehot(slice(0, 2)).then_inc(onehot_ready, 1)
                gathered(0)
                with dve.Fori(0, npass * PAIRS) as t:
                    it = base + t
                    dve.wait_ge(onehot_ready, gbase + t + 1)
                    for tt in range(2):
                        ins = V.tensor_tensor(pg[:, tt, :, :], pm[:, tt, :, :],
                                              bc(gates[:, tt, bass.ds(t * 2, 2)].unsqueeze(2), 2, SLOTS), MUL)
                    ins.then_inc(pg_ready, 1)
                    dve.wait_ge(pg_ready, it + 1)
                    onehot(bass.ds(t * 2 + 2, 2)).then_inc(onehot_ready, 1)
                    dve.wait_ge(efilled[3], it + 1)
                    dve.wait_ge(edrained[2], it + 2)
                    V.tensor_tensor(hid, sgate, banks[3][:, 0:512], MUL).then_inc(edrained[3], 1)
                    gathered(t + 1)
                    dve.wait_ge(efilled[7], it * 2 + 1)
                    V.tensor_copy(pgT, banks[7][:, 0:256]).then_inc(edrained[7], 1)
                    dve.wait_ge(efilled[5], it * 2 + 1)
                    V.tensor_copy(ys_b[:, 512:1024], banks[5][:, 0:512]).then_inc(edrained[5], 1)
                    for tt in range(2):
                        for n in range(2):
                            b = (6 if tt == 0 else 4) + n
                            dve.wait_ge(efilled[b], it * 2 + 2)
                            hh = h[:, tt, n * 512:(n + 1) * 512]
                            V.tensor_tensor(hh, hh, banks[b][:, 0:512], ADD).then_inc(edrained[b], 1)
                    for b in (4, 5, 6, 7):
                        dve.wait_ge(edrained[b], it * 2 + 3)
                dve.reg_add(iters, iters, npass * PAIRS)

            V.memset(scratch[:, 31:32], 0.0).then_inc(ev("h_mix"), 1)
            dve.wait_ge(s_gain, 16)
            dve.wait_ge(ev("squares_final"), 1)
            inverse_root(setup.link, rs, ssq, 1.0 / D).then_inc(ev("rstd_final"), 1)
            dve.wait_ge(ev("rstd_final"), 1)
            setup.link(V.tensor_scalar(xhat[:, 1, :], h[:, 1, :], rs[:, 1:2], None, MUL))
            V.tensor_tensor(xhat[:, 1, :], xhat[:, 1, :], gain_row, MUL)
            dve.wait_ge(ev("xhat0_final"), 1)
            setup.link(V.tensor_tensor(xhat[:, 0, :], xhat[:, 0, :], gain_row, MUL))
            V.memset(scratch[:, 32:33], 0.0).then_inc(ev("out_ready"), 1)


def constants():
    import numpy as np

    p = np.arange(P)
    half = HD // 2
    inv = (10000.0 ** (-np.arange(half, dtype=np.float32) / half)).astype(np.float32)
    ang = (np.arange(256, dtype=np.float32)[None, :] * inv[p % half][:, None]).astype(np.float32)
    sign = np.where(p % HD < half, -1.0, 1.0)[:, None]
    eye = np.eye(P, dtype=np.float32)
    tok = np.arange(2)[None, :, None] * P + p[:, None, None]
    blk = np.arange(NCMP)[None, None, :]
    ok = ((blk * 16 + 31 <= tok) & (blk < NCMP - 1)).astype(np.float32)
    rows = np.arange(P) // NCMP
    own = np.zeros((P, GRP, KV), np.float32)
    own[p, rows // KV, rows % KV] = 1.0
    f = np.concatenate([
        eye, eye[p ^ half], (p[:, None] < p[None, :]).astype(np.float32), np.ones((P, P), np.float32),
        np.cos(ang), np.sin(ang) * sign,
        np.broadcast_to(np.arange(SLOTS, dtype=np.float32), (P, SLOTS)),
        np.broadcast_to(np.arange(4) - TOP_IDX, (P, 4)), np.broadcast_to(np.arange(32) - TOP_IDX, (P, 32)),
        ok.reshape(P, 32), own.reshape(P, 8)], axis=1).astype(np.float32)
    bf = np.concatenate([
        eye, np.where(p[None, :] > p[:, None], -1e30, 0.0), (1.0 - ok.reshape(P, 32)) * -1e30], axis=1)
    s, t = p[:, None], p[None, :]
    masks = [s == t] + [(s // (2 * L) == t // (2 * L)) & (s % (2 * L) < L) & (t % (2 * L) >= L) for L in HALVES]
    return f, np.concatenate([np.stack(masks, 1).reshape(P, -1), bf], axis=1).astype(np.float32)


def kernel(**inputs):
    import numpy as _np
    import concourse.bacc as _bacc
    from concourse import mybir as _mybir
    from concourse.bass_utils import run_bass_kernel_spmd as _run

    a = {k: _np.asarray(v) for k, v in inputs.items()}
    L = a["w_in"].shape[0]

    def cols(w):
        n = w.shape[1] // P
        return _np.moveaxis(w.reshape(L, n, P, -1), 1, 2).reshape(L, P, -1)

    def rows(w):
        return _np.broadcast_to(w[:, None, :], (L, P, w.shape[-1]))

    conv = _np.moveaxis(a["conv_w"].reshape(L, 3, 2, P), 3, 1).transpose(0, 1, 3, 2).reshape(L, P, 6)
    pe = a["cmp_pe"].reshape(L, 2, 16, 2, HD).transpose(0, 3, 4, 1, 2).reshape(L, P, 32)
    router = _np.concatenate([a["router_group_w"], a["router_expert_w"]], axis=2)
    params = _np.concatenate([
        cols(a["norm_mix"]), cols(a["norm_cross"]), cols(a["norm_mem"]), cols(a["norm_ffn"]), conv, pe,
        cols(a["hgrn_norm"]), rows(a["router_group_b"]), rows(a["router_expert_b"]), cols(router)], axis=2)
    w_q = a["w_in"][:, :, 0:512].reshape(L, D, KV, GRP, HD).transpose(0, 1, 3, 2, 4).reshape(L, D, 512)
    heads = a["w_out"][:, 0:512].reshape(L, KV, GRP, HD, D).transpose(0, 2, 1, 3, 4).reshape(L, 512, D)
    w_out = _np.concatenate([heads, a["w_out"][:, 512:]], axis=1)
    cmp_w1 = a["cmp_w1"].reshape(L, 2, 16, P, P).transpose(0, 3, 1, 2, 4).reshape(L, P, 4096)
    cmp_w2 = a["cmp_w2"].transpose(0, 2, 1, 3).reshape(L, P, 2 * HD)
    f, masks = constants()
    feeds = {
        "x": a["x"][0], "mem": a["mem"][0], "w_q": w_q, "w_in": a["w_in"], "cmp_w1": cmp_w1,
        "cmp_w2": cmp_w2, "w_out": w_out, "wq": a["cross_wq"], "wkv": a["cross_wkv"], "wo": a["cross_wo"],
        "w_gu": a["expert_w_gate_up"], "w_dn": a["expert_w_down"], "norm_final": a["norm_final"],
        "params": params, "lb_logits": a["hgrn_lb_logits"].reshape(L, 2, P).transpose(2, 0, 1),
        "consts": f, "masks": masks}
    nc = _bacc.Bacc("TRN2", target_bir_lowering=False, num_devices=1)
    arrays, args = {}, []
    for name, v in feeds.items():
        v = _np.ascontiguousarray(v)
        arrays[f"in_{name}"] = v
        args.append(nc.dram_tensor(f"in_{name}", v.shape, _mybir.dt.from_np(v.dtype), kind="ExternalInput").ap())
    out = nc.dram_tensor("out_y", (256, D), F32, kind="ExternalOutput").ap()
    hymba(nc, L, *args, out)
    r = _run(nc, [arrays], core_ids=[0])
    return r.results[0]["out_y"].reshape(a["x"].shape)
```

```python
from contextlib import ExitStack

import concourse.bass as bass
from concourse import mybir

F32 = mybir.dt.float32
BF16 = mybir.dt.bfloat16
U8 = mybir.dt.uint8
I32 = mybir.dt.int32
ALU = mybir.AluOpType
ACT = mybir.ActivationFunctionType
AX = mybir.AxisListType.X

P = 128
D = 1024
EPS = 1e-6
LB_FLOOR = 1e-30
HD = 64
KV = 2
GRP = 4
NCMP = 16
TOP_IDX = 1000.0
SLOTS = 64

C_KC, C_KS, C_KW, C_GL = 512, 768, 1024, 1280
C_CB, C_CH, C_HQ, C_HF, C_HI, C_HG, C_END = 1304, 1816, 2072, 2328, 2584, 2840, 3096

HALVES = [1, 2, 4, 8, 16, 32, 64]


GROUPS = [(br, tt, i, n) for tt, heads in enumerate((((0, 4),), ((0, 2), (2, 2)))) for br in ("sel", "win")
          for i, n in heads]
NN = len(GROUPS)
GROUPS += [("cross", tt, 0, 2) for tt in range(2)]
NG = len(GROUPS)
USES = {
    0: ["xT1", "dg_0", "lv1_0", "lv2_0", "lv4_0", "lv8_0", "cc", "lv16_0", "lv32_0", "ch", "lv64_0", "off_0",
        "wo0", "wo2", "yT0", "cq0", "yT2", "co0", "co2", "zT0", "zT2"],
    1: ["xT2", "dg_1", "lv1_1", "lv2_1", "lv4_1", "cb", "lv8_1", "lv16_1", "hg", "lv32_1", "lv64_1", "off_1", "hi",
        "wo1", "wo3", "yT1", "yT3", "cq1", "co1", "co3", "zT1", "zT3", "pos"],
    2: ["memk", "xT3", "cmph", "vwgl", "cmp_s_0"] + [f"s{n}_0" for n in range(NN)] + ["av"]
       + [f"s{n}_0" for n in range(NN, NG)],
    3: ["xT0", "hf", "ksvs", "cmpo", "cmp_s_1"] + [f"s{n}_1" for n in range(NG)],
    4: ["hq", "hidT", "rk", "cmp_t"] + [f"t{n}_0" for n in range(NG)],
    5: ["ckv", "rq0"] + [f"t{n}_1" for n in range(NN)] + ["hot"] + [f"t{n}_1" for n in range(NN, NG)],
    6: ["q0", "rq1", "o6", "xo0", "rt"],
    7: ["q1", "kw", "o7", "memv", "xo1"],
}
PLACE = {name: (b, n) for b, names in USES.items() for n, name in enumerate(names)}

DVE_STEPS, POOL_STEPS = 149, 23

LAST_USE = ["memk", "hq", "ksvs", "q1", "cmph", "cmpo", "cc", "hi", "hg", "wo2", "wo3", "co3"]
N_SETUP = 4
STEPS_AHEAD = 4


def flat(ap):
    names = "abc"[:len(ap.shape) - 1]
    return ap if len(names) == 1 else ap.rearrange(f"p {' '.join(names)} -> p ({' '.join(names)})")



def hymba(nc, L, x, mem, w_q, w_in, cmp_w1, cmp_w2, w_out, wq, wkv, wo, w_gu, w_dn, norm_final,
          params, lb_logits, consts, masks, out):
    T = 256
    DEPTH = L
    E = w_gu.shape[1]
    PAIRS = E // 2
    MAXP = T // SLOTS
    NPAR = params.shape[2]

    ctx = ExitStack()
    with ctx:
        def sb(name, shape, dt=F32):
            return ctx.enter_context(nc.sbuf_tensor(name, shape, dt))

        def sem(name):
            return ctx.enter_context(nc.semaphore(name))

        banks = [ctx.enter_context(nc.psum_tensor(f"bank{b}", [P, 512], F32)) for b in range(8)]

        h = sb("h", [P, 2, 1024])
        memT = sb("memT", [P, 8, 256])
        xnT = sb("xnT", [P, 8, 256])
        xhat = sb("xhat", [P, 2, 1024])
        cst = sb("cst", [P, consts.shape[1]])
        cbf = sb("cbf", [P, 288], BF16)
        lvmask = sb("lvmask", [P, 8, 128], U8)
        par = sb("par", [P, DEPTH, NPAR])
        lb_in = sb("lb_in", [P, DEPTH, 2])
        lbf = sb("lbf", [P, DEPTH, 2])
        oml = sb("oml", [P, DEPTH, 2])
        small = sb("small", [P, 254])
        COLS = MAXP * E + 2
        posv = sb("posv", [P, 2, COLS])
        gates = sb("gates", [P, 2, COLS])
        npass_i = sb("npass_i", [1, 2], I32)
        dense = sb("dense", [P, 3, 4096])
        ring = sb("ring", [P, 3, 4096])
        share = sb("share", [P, 12288])
        rest = sb("rest", [P, 4352])

        ident = cst[:, 0:128]
        perm = cst[:, 128:256]
        tri = cst[:, 256:384]
        ones = cst[:, 384:512]
        cos = cst[:, 512:768]
        sin = cst[:, 768:1024]
        iota_slot = cst[:, 1024:1024 + SLOTS]
        iota_g = cst[:, 1088:1092]
        iota_e = cst[:, 1092:1124]
        cmp_ok = cst[:, 1124:1156].rearrange("p (t c) -> p t c", t=2)
        own_block = cst[:, 1156:1164].rearrange("p (i v) -> p i v", v=2)
        ident_b = cbf[:, 0:128]
        causal_b = cbf[:, 128:256]
        cmp_no_b = cbf[:, 256:288].rearrange("p (t c) -> p t c", t=2)

        def pcol(l, a, n):
            return par[:, l, a:a + n]
        G_MIX, G_CROSS, G_MEM, G_FFN, CONVW, PE_C, HNORM, RBIAS, RW = 0, 8, 16, 24, 32, 38, 70, 72, 108

        def cut(t, sizes):
            at, views = 0, []
            for n in sizes:
                views.append(t[:, at:at + n])
                at += n
            assert at <= t.shape[1], at
            return views

        def two(ap):
            return ap.rearrange("p (c t) -> p c t", c=2)

        (f_b, g_b, q_b, k_b, qt0_b, qt1_b, kt0_b, kt1_b, tot, a0_b, a1_b, ao_b, hi_b, hgr_b) = cut(
            share[:, 0:7168], [512] * 14)
        (qraw_b, qrot_b, kraw_b, krot_b, tmp, vv, vblk_b, hgs_b) = cut(
            share[:, 7168:12288], [1024, 1024, 512, 512, 512, 512, 512, 512])
        f_, q_, k_ = two(f_b), two(q_b), two(k_b)
        qt_b, kt_b = [qt0_b, qt1_b], [kt0_b, kt1_b]
        qt, kt = [two(qt0_b), two(qt1_b)], [two(kt0_b), two(kt1_b)]
        a01 = share[:, 4608:5632].rearrange("p (n h t) -> p n h t", n=4, h=2)
        A_ = [t.rearrange("p (h t) -> p h t", h=4) for t in (a0_b, a1_b, ao_b)]
        hi_ = two(hi_b)
        qraw = qraw_b.rearrange("p (i t) -> p i t", i=GRP)
        qrot = qrot_b.rearrange("p (i t) -> p i t", i=GRP)
        kraw, krot = two(kraw_b), two(krot_b)
        v_of = {"sel": two(vv[:, 0:256]), "win": two(vv[:, 256:512])}
        vblk = vblk_b.rearrange("p (i c) -> p i c", i=GRP)
        mask_in = rest[:, 0:1024].rearrange("p (m t) -> p m t", m=8)
        (memG_b, wkv_v, probs_a, probs_b, pT, cmpPT, cmpP, xe_b, cmp_x, cmp_e, mixT_b) = cut(
            ring[:, :, :].rearrange("p s c -> p (s c)"),
            [2048, 2048, 1024, 1024, 1024, 256, 256, 1040, 128, 128, 2048])
        mixT = mixT_b.rearrange("p (k t) -> p k t", k=8)
        memG_ring = memG_b.rearrange("p (k t) -> p k t", k=8)
        xe = xe_b[:, 0:1024].rearrange("p (g a c) -> p g a c", g=4, a=16)
        mem_raw = two(share[:, 0:2048])
        mem_sq = two(share[:, 2048:4096])

        (cvb_b, cvc_b, cvh_b, cvy_b) = cut(rest[:, 0:2048], [512] * 4)
        cv_b, cv_c, cv_h, cv_y = two(cvb_b), two(cvc_b), two(cvh_b), two(cvy_b)
        cv_u = two(rest[:, 2048:2048 + 516])
        memk, memv, cq = [two(rest[:, 2564 + 512 * n:3076 + 512 * n]) for n in range(3)]
        coT = cv_b

        flatx = xnT[:, :, :].rearrange("p k t -> p (k t)")

        def probs(n):
            if n < NN:
                return probs_b if n % 2 else probs_a
            return flatx[:, 0:1024] if n % 2 else rest[:, 1024:2048]

        def pT_of(n):
            return pT if n < NN else flatx[:, 1024:2048]

        cmp_hk = sb("cmp_hk", [P, KV, 32])
        cmp_hv = sb("cmp_hv", [P, GRP, KV * NCMP])
        kc = sb("kc", [P, NCMP])
        gate = sb("gate", [P, 2, 24])
        cvw = sb("cvw", [P, 6])
        (ssq, rs, hsum, hrs, lbt, cmx, csum, crr) = cut(small[:, 0:92], [2, 2, 8, 8, 24, 16, 16, 16])
        att_mx, att_nb, att_sum, att_rr = [
            [small[:, 190 + 16 * n + 8 * b:198 + 16 * n + 8 * b] for b in range(2)] for n in range(4)]
        scratch = small[:, 136:172]
        root_x, root_t = small[:, 172:180], small[:, 180:188]

        (xg_b, ys_b, sgate, hid, ht_b, pm_b, pg_b, pgt_b) = cut(
            rest[:, :], [1024, 1024, 512, 512, 512, 256, 256, 256])
        xg = xg_b.rearrange("p (k s) -> p k s", k=8)
        ht = ht_b.rearrange("p (k s) -> p k s", k=4)
        pm = pm_b.rearrange("p (t e s) -> p t e s", t=2, e=2)
        pg = pg_b.rearrange("p (t e s) -> p t e s", t=2, e=2)
        pgT = pgt_b
        def rtile(at, n):
            return ys_b[:, at:at + 2 * n].rearrange("p (t c) -> p t c", t=2)
        rl, rlog, r_in, r_o1, r_o2, chosen = [
            rtile(a, n) for a, n in ((0, 36), (72, 36), (144, 32), (272, 32), (336, 32), (400, 32))]
        rexp = rtile(464, 36)
        r_g1 = rtile(536, 4)
        r_mg, r_sg, r_e1, r_e2, r_t, r_min = [ys_b[:, 544 + 2 * i:546 + 2 * i] for i in range(6)]
        r_cnt, r_np = ys_b[:, 558:559], ys_b[:, 559:560]
        gain_row = memT[:, :, :].rearrange("p k t -> p (k t)")[:, 0:D]

        def eslot(s):
            return ring[:, s, :] if s < 3 else share[:, (s - 3) * 4096:(s - 2) * 4096]

        def odd_slot(s):
            return dense[:, s, :] if s < 3 else eslot(s)

        filled = [sem(f"bank{b}_filled") for b in range(8)]
        drained = [sem(f"bank{b}_drained") for b in range(8)]
        efilled = [sem(f"ebank{b}_filled") for b in range(8)]
        edrained = [sem(f"ebank{b}_drained") for b in range(8)]
        dloaded = [sem(f"dense{s}_loaded") for s in range(3)]
        eloaded = [sem(f"expert{s}_loaded") for s in range(6)]
        odd_loaded = [sem(f"odd_expert{s}_loaded") for s in range(3)]
        vloaded = sem("memory_value_weights_loaded")
        half_read = sem("gate_up_first_rows_read")
        events = {}

        def ev(name):
            if name not in events:
                events[name] = sem(name)
            return events[name]

        s_consts = sem("constants_loaded")
        s_setup = sem("inputs_loaded")
        s_mem = sem("mem_loaded")
        s_gain = sem("final_gain_loaded")
        s_out = sem("out_stored")
        dve_step, pool_step, setup_step = sem("dve_step"), sem("pool_step"), sem("setup_step")
        onehot_ready, pg_ready = sem("onehot_ready"), sem("gated_onehot_ready")

        class Chain:

            def __init__(self, eng, semaphore, base, steps, apart=False):
                self.apart = apart
                self.eng, self.sem, self.base, self.n, self.steps = eng, semaphore, base, 0, steps

            def link(self, ins):
                self.n += 1
                ins.then_inc(self.sem, 1)
                self.eng.wait_ge(self.sem, self.base + self.n)
                if self.apart:
                    alone(self.eng)

            def close(self):
                assert self.n == self.steps, (str(self.sem), self.n, self.steps)

        def alone(eng):
            eng.nop(nofuse=True)

        def bank_free(eng, l, use):
            b, n = PLACE[use]
            eng.wait_ge(drained[b], l * len(USES[b]) + (n + 1))
            return banks[b]

        def bank_done(ins, use):
            ins.then_inc(filled[PLACE[use][0]], 1)

        def bank_full(eng, l, use):
            b, n = PLACE[use]
            eng.wait_ge(filled[b], l * len(USES[b]) + (n + 1))
            return banks[b]

        def bank_drained(ins, use):
            ins.then_inc(drained[PLACE[use][0]], 1)

        def wait_drained(eng, l, use):
            b, n = PLACE[use]
            eng.wait_ge(drained[b], l * len(USES[b]) + (n + 2))

        def kt_rows(w, a, b):
            return w.rearrange("(k p) c -> p k c", p=P)[:, :, a:b]

        def unit_view(s, n, c):
            return dense[:, s, 0:n * c].rearrange("p (k c) -> p k c", k=n)

        def unit_dmas(l, u):
            s = u % 3
            win = w_in[l]
            spans = {1: (C_HQ, C_HI), 2: (C_KC, C_KW), 5: (C_KW, C_CB), 6: (C_CB, C_CH), 8: (C_HG, C_END)}
            if u == 0:
                return [(unit_view(s, 8, 256), kt_rows(wkv[l], 0, 256))]
            if u == 3:
                return [(unit_view(s, 8, 512), kt_rows(w_q[l], 0, 512))]
            if u in spans:
                a, b = spans[u]
                dmas = [(unit_view(s, 8, b - a), kt_rows(win, a, b))]
                if u == 5:
                    dmas.append((dense[:, s, 3968:4096], cmp_w2[l]))
                return dmas
            if u == 4:
                return [(dense[:, s, :], cmp_w1[l])]
            if u == 7:
                return [(dense[:, s, n * 2048:(n + 1) * 2048].rearrange("p (k c) -> p k c", k=8),
                         kt_rows(win, a, a + 256)) for n, a in enumerate((C_CH, C_HI))]
            if u in (9, 10):
                return [(unit_view(s, 8, 512), kt_rows(w_out[l], (u - 9) * 512, (u - 8) * 512))]
            return [(dense[:, s, 0:2048].rearrange("p (k c) -> p k c", k=8), kt_rows(wq[l], 0, 256)),
                    (dense[:, s, 2048:4096].rearrange("p (k c) -> p k c", k=2), kt_rows(wo[l], 0, 1024))]

        N_DMA = [1, 1, 1, 1, 1, 2, 1, 2, 1, 1, 1, 2]

        def unit_loaded(eng, l, u):
            s = u % 3
            per = sum(N_DMA[s::3])
            upto = sum(N_DMA[i] for i in range(s, u + 1, 3))
            eng.wait_ge(dloaded[s], l * (16 * per) + 16 * upto)

        def expert_loaded(eng, it, odd, s):
            if s >= 3:
                eng.wait_ge(eloaded[s], it * 16 + 16)
            elif odd:
                eng.wait_ge(odd_loaded[s], it * 8 + 8)
            else:
                eng.wait_ge(eloaded[s], it * 8 + 16)

        def expert_dmas(l, pair, s, slot_of=eslot):
            part, e = s // 2, pair * 2 + s % 2
            src = w_dn[l, e] if part == 2 else w_gu[l, e, part * 512:(part + 1) * 512, :]
            return slot_of(s).rearrange("p (k c) -> p k c", k=4), src.rearrange("(k p) c -> p k c", p=P)

        block = ctx.enter_context(nc.Block())

        @block.sync
        def _(sp):
            sp.dma_start(mem_raw, mem.rearrange("(t p) d -> p t d", p=P)).then_inc(s_mem, 16)
            sp.dma_start(cst[:, :], consts).then_inc(s_consts, 16)
            sp.dma_start(par[:, :, :], params.rearrange("l p n -> p l n")).then_inc(s_setup, 16)
            sp.dma_start(h[:, :, :], x.rearrange("(t p) d -> p t d", p=P)).then_inc(s_setup, 16)
            sp.dma_start(rest[:, 0:1312], masks).then_inc(s_setup, 16)
            sp.dma_start(lb_in[:, :, :], lb_logits).then_inc(s_setup, 16)
            iters = sp.alloc_register("sp_iters")
            sp.reg_mov(iters, 0)
            odd_reg = sp.alloc_register("sp_odd_pair")
            sp.reg_mov(odd_reg, 1)
            with sp.Fori(0, DEPTH) as l:
                base = sp.snap(iters, min_val=0, max_val=DEPTH * MAXP * PAIRS)

                def load_unit(u):
                    s = u % 3
                    if u >= 3:
                        bank_full(sp, l, LAST_USE[u - 3])
                    for dst, src in unit_dmas(l, u):
                        sp.dma_start(dst, src).then_inc(dloaded[s], 16)

                def load_expert(pair, s, odd=False):
                    dst, src = expert_dmas(l, pair, s, odd_slot if odd else eslot)
                    sp.dma_start(dst, src).then_inc(odd_loaded[s] if odd and s < 3 else eloaded[s], 16)

                for u in range(3):
                    load_unit(u)
                sp.wait_ge(ev("h_mix"), l + 1)
                alone(sp)
                sp.dma_start(wkv_v.rearrange("p (k c) -> p k c", k=8),
                             kt_rows(wkv[l], 256, 512)).then_inc(vloaded, 16)
                for u in range(3, 12):
                    load_unit(u)
                bank_full(sp, l, "wo3")
                alone(sp)
                for s in range(1, 6):
                    load_expert(0, s)
                bank_full(sp, l, "memv")
                alone(sp)
                load_expert(0, 0)
                load_expert(1, 0, True)
                load_expert(1, 1, True)
                bank_full(sp, l, LAST_USE[11])
                alone(sp)
                load_expert(1, 2, True)
                sp.wait_ge(ev("npass_ready"), l + 1)
                alone(sp)
                npass = sp.value_load(npass_i[0:1, 0:1], min_val=1, max_val=MAXP)

                def first_rows(t, odd, it):
                    sp.wait_ge(half_read, it)
                    alone(sp)
                    load_expert((t + 1) % PAIRS, 0, not odd)
                    load_expert((t + 1) % PAIRS, 1, not odd)

                def other_rows(t, odd, it):
                    sp.wait_ge(efilled[3], it)
                    alone(sp)
                    load_expert(t % PAIRS, 3, odd)

                def down(t, odd, it):
                    sp.wait_ge(efilled[5], it * 2 - 1)
                    alone(sp)
                    load_expert(t % PAIRS, 4, odd)
                    load_expert(t % PAIRS, 5, odd)

                def pairs_before():
                    return sp.snap(odd_reg, min_val=1, max_val=DEPTH * MAXP * PAIRS + 1)

                for t in range(1, 1 + STEPS_AHEAD):
                    odd = t % 2 == 1
                    it = pairs_before() if odd else pairs_before() + 1
                    first_rows(t, odd, it)
                    other_rows(t, odd, it)
                    load_expert(t + 1, 2, not odd)
                    down(t, odd, it)
                    if not odd:
                        sp.reg_add(odd_reg, odd_reg, 2)
                with sp.Fori(STEPS_AHEAD // 2, npass * (PAIRS // 2) - 1) as i:
                    for step in (1, 2):
                        t, odd = i * 2 + step, step == 1
                        it = pairs_before() if odd else pairs_before() + 1
                        other_rows(t, odd, it)
                        down(t, odd, it)
                        first_rows(t, odd, it)
                        load_expert((t + 1) % PAIRS, 2, not odd)
                    sp.reg_add(odd_reg, odd_reg, 2)
                it = pairs_before()
                other_rows(PAIRS - 1, True, it)
                down(PAIRS - 1, True, it)
                sp.wait_ge(efilled[3], it + 1)
                alone(sp)
                sp.reg_add(odd_reg, odd_reg, 2)
                sp.reg_add(iters, iters, npass * PAIRS)
            sp.wait_ge(ev("memG"), DEPTH + 1)
            sp.dma_start(gain_row, norm_final.partition_broadcast(P)).then_inc(s_gain, 16)
            sp.wait_ge(ev("out_ready"), 1)
            sp.dma_start(out.rearrange("(t p) d -> p t d", p=P), xhat[:, :, :]).then_inc(s_out, 16)
            sp.wait_ge(s_out, 16)

        @block.tensor
        def _(pe):
            def mm(out_ap, lhsT, rhs, start, stop):
                return pe.matmul(out_ap, lhsT=lhsT, rhs=rhs, start=start, stop=stop, skip_group_check=True)

            pe.wait_ge(s_consts, 16)
            pe.wait_ge(ev("mem_hat"), 2)
            for j in range(4):
                for d in range(2):
                    for tt in range(2):
                        ins = pe.transpose(banks[j][:, (d * 2 + tt) * P:(d * 2 + tt + 1) * P],
                                           mem_raw[:, tt, (2 * j + d) * P:(2 * j + d + 1) * P], ident)
            ins.then_inc(ev("mem_turned"), 1)

            iters = pe.alloc_register("pe_iters")
            pe.reg_mov(iters, 0)
            with pe.Fori(0, DEPTH) as l:
                base = pe.snap(iters, min_val=0, max_val=DEPTH * MAXP * PAIRS)

                def wait(name):
                    pe.wait_ge(ev(name), l + 1)

                def settled(*uses):
                    for use in {PLACE[use][0]: use for use in sorted(uses, key=lambda u: PLACE[u][1])}.values():
                        wait_drained(pe, l, use)

                def project_T(out_ap, lhsT_of, src, rhs_cols=slice(0, 256)):
                    for k in range(8):
                        ins = mm(out_ap, lhsT_of(k), src[:, k, rhs_cols], k == 0, k == 7)
                    return ins

                def project_N(out_ap, unit, c0, c1, src, tt):
                    for k in range(8):
                        ins = mm(out_ap, src[:, k, tt * P:(tt + 1) * P], unit[:, k, c0:c1], k == 0, k == 7)
                    return ins

                def two_T(use, unit, c0, src):
                    bk = bank_free(pe, l, use)
                    for c in range(2):
                        ins = project_T(bk[:, c * 256:(c + 1) * 256],
                                        lambda k: unit[:, k, c0 + c * P:c0 + (c + 1) * P], src)
                    bank_done(ins, use)

                def two_N(use, unit, c0, c1, src):
                    bk = bank_free(pe, l, use)
                    n = c1 - c0
                    for tt in range(2):
                        ins = project_N(bk[:, tt * n:(tt + 1) * n], unit, c0, c1, src, tt)
                    bank_done(ins, use)

                def turn(prefix, stage, tt):
                    wait(f"xhat{tt}_{stage}")
                    for j in range(2):
                        bk = bank_free(pe, l, f"{prefix}T{tt * 2 + j}")
                        for d in range(4):
                            k = 4 * j + d
                            ins = pe.transpose(bk[:, d * P:(d + 1) * P], xhat[:, tt, k * P:(k + 1) * P], ident)
                        bank_done(ins, f"{prefix}T{tt * 2 + j}")

                for b in (0, 1):
                    pe.wait_ge(edrained[b], base + l + 1)
                for b in (2, 3):
                    pe.wait_ge(edrained[b], base + 1)
                wait("memG")
                unit_loaded(pe, l, 0)
                two_T("memk", unit_view(0, 8, 256), 0, xnT)
                turn("x", "mix", 0)
                turn("x", "mix", 1)
                for b in (4, 5, 6, 7):
                    pe.wait_ge(edrained[b], base * 2 + 1)
                settled("xT0", "xT1", "xT2", "xT3")
                unit_loaded(pe, l, 1)
                u = unit_view(1, 8, 512)
                two_T("hf", u, C_HF - C_HQ, xnT)
                two_T("hq", u, 0, xnT)

                def level(name, kk, qq):
                    bks = [bank_free(pe, l, f"{name}_{half}") for half in range(2)]
                    for n in range(4):
                        cols = slice((n // 2) * P, (n // 2 + 1) * P)
                        for half in range(2):
                            ch = slice(half * HD, (half + 1) * HD)
                            ins = mm(bks[half][:, n * P:(n + 1) * P], kk[ch, n % 2, cols], qq[ch, n % 2, cols],
                                     True, True)
                            if n == 3:
                                bank_done(ins, f"{name}_{half}")

                def half_level(L):
                    i = HALVES.index(L)
                    wait(f"qt{L}")
                    if L > 1:
                        wait(f"kt{L}")
                    level(f"lv{L}", k_ if L == 1 else kt[i % 2], qt[i % 2])

                def swap(use, src, c0):
                    bk = bank_free(pe, l, use)
                    bank_done(mm(bk[:, 0:512], perm, src[:, c0:c0 + 512], True, True), use)

                unit_loaded(pe, l, 2)
                u = unit_view(2, 8, 512)
                xpar = xnT[:, :, :].rearrange("p k (u r) -> p k r u", r=2)
                bk = bank_free(pe, l, "ckv")
                for s in range(2):
                    for v in range(KV):
                        cols = s * P + v * HD
                        for k in range(8):
                            for r in range(2):
                                ins = mm(bk[r * HD:(r + 1) * HD, (s * KV + v) * P:(s * KV + v + 1) * P],
                                         u[:, k, cols:cols + HD], xpar[:, k, r, :], k == 0, k == 7)
                bank_done(ins, "ckv")
                def key_T(bk, unit, c0):
                    return project_T(bk[:, 0:256], lambda k: unit[:, k, c0:c0 + P], xnT)

                def columns_N(bk, unit, c0, n, at):
                    for tt in range(2):
                        ins = project_N(bk[:, at + tt * n:at + (tt + 1) * n], unit, c0, c0 + n, xnT, tt)
                    return ins

                bk = bank_free(pe, l, "ksvs")
                key_T(bk, u, C_KS - C_KC)
                bank_done(columns_N(bk, u, C_KS - C_KC + P, P, 256), "ksvs")

                unit_loaded(pe, l, 3)
                u = unit_view(0, 8, 512)
                for use, i0 in (("q0", 0), ("q1", 2)):
                    bk = bank_free(pe, l, use)
                    for i in range(2):
                        ins = project_T(bk[:, i * 256:(i + 1) * 256],
                                        lambda k: u[:, k, (i0 + i) * P:(i0 + i + 1) * P], xnT)
                    bank_done(ins, use)
                    if use == "q0":
                        wait("k_ready")
                        settled("hq")
                        level("dg", k_, q_)

                unit_loaded(pe, l, 4)
                settled("ckv")
                bk = bank_free(pe, l, "cmph")
                for a in range(16):
                    for g in range(4):
                        w1 = dense[:, 1, (g // KV) * 2048 + a * P:(g // KV) * 2048 + (a + 1) * P]
                        ins = mm(bk[g * 32:(g + 1) * 32, 0:P], xe_b[:, g * 256 + a * 16:g * 256 + a * 16 + 32], w1,
                                 a == 0, a == 15)
                bank_done(ins, "cmph")
                half_level(1)

                wait("cmp_hid")
                bk = bank_free(pe, l, "hidT")
                bank_done(pe.transpose(bk[:, 0:P], cmp_x, ident), "hidT")

                settled("q0", "q1")
                swap("rq0", qraw_b, 0)
                swap("rq1", qraw_b, 512)
                half_level(2)

                unit_loaded(pe, l, 5)
                u = unit_view(2, 8, C_CB - C_KW)
                bk = bank_free(pe, l, "kw")
                bank_done(key_T(bk, u, 0), "kw")
                bk = bank_free(pe, l, "vwgl")
                bank_done(columns_N(bk, u, P, C_CB - C_KW - P, 0), "vwgl")

                settled("hidT")
                w2 = dense[:, 2, 3968:4096].rearrange("p (a d) -> p a d", a=2)
                bk = bank_free(pe, l, "cmpo")
                for v in range(KV):
                    mm(bk[v * HD:(v + 1) * HD, 0:NCMP], w2[:, 0, :], cmp_hk[:, v, 0:NCMP], True, True)
                ins = mm(bk[:, 64:64 + P].rearrange("p (v d) -> p v d", v=KV),
                         cmp_hv[:, :, :].rearrange("p i c -> p (i c)"),
                         w2[:, 1, :].unsqueeze(1).broadcast_to([P, KV, HD]), True, True)
                bank_done(ins, "cmpo")
                settled("ksvs", "kw")
                swap("rk", kraw_b, 0)
                half_level(4)
                def scores(n):
                    bks = [bank_free(pe, l, f"s{n}_{v}") for v in range(2)]
                    br, tt, i0, nh = GROUPS[n]
                    nk = 512 // nh
                    for j in range(nh):
                        for v in range(2):
                            ch = slice(v * HD, (v + 1) * HD)
                            o = bks[v][:, j * nk:(j + 1) * nk]
                            if br == "cross":
                                ins = mm(o, cq[ch, j, tt * P:(tt + 1) * P], memk[ch, j, :], True, True)
                                if j == nh - 1:
                                    bank_done(ins, f"s{n}_{v}")
                            else:
                                mm(o, qrot[ch, i0 + j, tt * P:(tt + 1) * P],
                                   krot[ch, 0 if br == "sel" else 1, 0:nk], j == 0, False)
                    if br == "cross":
                        return
                    for v in range(2):
                        for j in range(nh):
                            ins = mm(bks[v][:, (j + 1) * nk - P:(j + 1) * nk], ident_b, causal_b, False, True)
                        bank_done(ins, f"s{n}_{v}")

                def turn_probs(n):
                    pe.wait_ge(ev("p_scaled"), l * NG + (n + 1))
                    for v in range(2):
                        bk = bank_free(pe, l, f"t{n}_{v}")
                        for c in range(4):
                            at = v * 512 + c * P
                            ins = pe.transpose(bk[:, c * P:(c + 1) * P], probs(n)[:, at:at + P], ident)
                        bank_done(ins, f"t{n}_{v}")

                def values(n):
                    wait_drained(pe, l, f"t{n}_0")
                    wait_drained(pe, l, f"t{n}_1")
                    br, tt, i0, nh = GROUPS[n]
                    nkt = 4 // nh
                    for j in range(nh):
                        for c in range(nkt):
                            for v in range(2):
                                at = v * 512 + (j * nkt + c) * P
                                if br == "cross":
                                    o = banks[6 + tt][v * HD:(v + 1) * HD, j * P:(j + 1) * P]
                                    vals = memv[:, c, (2 * j + v) * HD:(2 * j + v + 1) * HD]
                                    ins = mm(o, vals, pT_of(n)[:, at:at + P], c == 0, c == 1)
                                else:
                                    i = i0 + j
                                    o = banks[6 + i // 2][v * HD:(v + 1) * HD,
                                                          (i % 2) * 256 + tt * P:(i % 2) * 256 + (tt + 1) * P]
                                    ins = mm(o, v_of[br][:, c, v * HD:(v + 1) * HD], pT_of(n)[:, at:at + P], False,
                                             c == nkt - 1)
                    if n == 1:
                        ins.then_inc(ev("o_tile0"), 1)
                    if n == NN - 2:
                        bank_done(ins, "o6")
                    if n == NN - 1:
                        bank_done(ins, "o7")
                    if br == "cross":
                        bank_done(ins, f"xo{tt}")

                settled("cmpo")
                bks = [bank_free(pe, l, f"cmp_s_{v}") for v in range(KV)]
                for tt in range(2):
                    for i in range(GRP):
                        for v in range(KV):
                            ch = slice(v * HD, (v + 1) * HD)
                            at = (tt * GRP + i) * NCMP
                            mm(bks[v][:, at:at + NCMP], qraw[ch, i, tt * P:(tt + 1) * P], kc[ch, :],
                               tt == i == 0, False)
                for v in range(KV):
                    for tt in range(2):
                        ins = mm(bks[v][:, tt * 64:(tt + 1) * 64].rearrange("p (g c) -> p g c", c=NCMP), ident_b,
                                 cmp_no_b[:, tt, :].unsqueeze(1).broadcast_to([P, GRP, NCMP]), False, tt == 1)
                    bank_done(ins, f"cmp_s_{v}")
                wait("krot")
                wait("qrot")
                scores(0)
                unit_loaded(pe, l, 6)
                u6 = unit_view(0, 8, 512)
                two_T("cb", u6, 0, xnT)
                half_level(8)
                wait("cmp_p")
                bk = bank_free(pe, l, "cmp_t")
                for tt in range(2):
                    ins = pe.transpose(bk[:, tt * P:(tt + 1) * P], cmpP[:, tt * P:(tt + 1) * P], ident)
                bank_done(ins, "cmp_t")
                settled("cmp_t")
                bank_free(pe, l, "o6")
                bank_free(pe, l, "o7")
                for i in range(GRP):
                    mm(banks[6 + i // 2][:, (i % 2) * 256:(i % 2 + 1) * 256], vblk[:, i, :], cmpPT,
                       i % 2 == 0, False)

                scores(1)
                turn_probs(0)
                two_T("cc", u6, 256, xnT)
                values(0)
                scores(2)
                half_level(16)
                turn_probs(1)
                unit_loaded(pe, l, 8)
                two_N("hg", unit_view(2, 8, 256), 0, 256, xnT)
                values(1)
                scores(3)
                half_level(32)
                turn_probs(2)
                unit_loaded(pe, l, 7)
                two_T("ch", dense[:, 1, 0:2048].rearrange("p (k c) -> p k c", k=8), 0, xnT)
                values(2)
                scores(4)
                half_level(64)
                turn_probs(3)
                wait("qt128")
                wait("kt128")
                bks = [bank_free(pe, l, f"off_{half}") for half in range(2)]
                for c in range(2):
                    for half in range(2):
                        ch = slice(half * HD, (half + 1) * HD)
                        ins = mm(bks[half][:, c * P:(c + 1) * P], kt[1][ch, c, 0:P], qt[1][ch, c, P:256], True, True)
                        if c == 1:
                            bank_done(ins, f"off_{half}")
                two_N("hi", dense[:, 1, 2048:4096].rearrange("p (k c) -> p k c", k=8), 0, 256, xnT)
                values(3)

                scores(5)
                turn_probs(4)

                settled("off_0", "hi")
                bk = bank_free(pe, l, "av")
                for hd in range(4):
                    e = slice(hd * HD, (hd + 1) * HD)
                    mm(bk[:, hd * HD:(hd + 1) * HD], A_[0][:, hd, :], hi_[:, 0, e], True, True)
                    mm(bk[:, 256 + hd * HD:256 + (hd + 1) * HD], A_[2][:, hd, :], hi_[:, 0, e], True, False)
                    ins = mm(bk[:, 256 + hd * HD:256 + (hd + 1) * HD], A_[1][:, hd, :], hi_[:, 1, e], False, True)
                bank_done(ins, "av")
                values(4)
                turn_probs(5)

                def out_proj(use, k0, k1, last, lhs, tt, w):
                    for k in range(k0, k1):
                        ins = mm(banks[PLACE[use][0]][:, 0:512], lhs[:, k, tt * P:(tt + 1) * P], w(k), k == 0,
                                 k == last)
                    if k1 > last:
                        bank_done(ins, use)

                def w_mix(n):
                    return lambda k: unit_view(n, 8, 512)[:, k, :]

                wait("conv_done")
                wait("mix0_heads01")
                wait("mix0_heads23")
                unit_loaded(pe, l, 9)
                bank_free(pe, l, "wo0")
                out_proj("wo0", 0, 6, 7, mixT, 0, w_mix(0))
                values(5)
                wait("hgrn_o")
                bk = bank_free(pe, l, "hot")
                for c in range(2):
                    for tt in range(2):
                        ins = pe.transpose(bk[:, (c * 2 + tt) * P:(c * 2 + tt + 1) * P],
                                           kt1_b[:, tt * 256 + c * P:tt * 256 + (c + 1) * P], ident)
                bank_done(ins, "hot")
                unit_loaded(pe, l, 10)
                bank_free(pe, l, "wo1")
                out_proj("wo1", 0, 6, 7, mixT, 0, w_mix(1))
                settled("hot")
                out_proj("wo0", 6, 8, 7, mixT, 0, w_mix(0))
                out_proj("wo1", 6, 8, 7, mixT, 0, w_mix(1))
                settled("o6", "o7")
                for n in range(2):
                    bank_free(pe, l, f"wo{2 + n}")
                    out_proj(f"wo{2 + n}", 0, 8, 7, mixT, 1, w_mix(n))

                def cross_query(tt):
                    settled(f"yT{2 * tt}", f"yT{2 * tt + 1}")
                    wq_v = dense[:, 2, 0:2048].rearrange("p (k c) -> p k c", k=8)
                    bk = bank_free(pe, l, f"cq{tt}")
                    for c in range(2):
                        ins = project_T(bk[:, c * P:(c + 1) * P], lambda k: wq_v[:, k, c * P:(c + 1) * P], xnT,
                                        slice(tt * P, (tt + 1) * P))
                    bank_done(ins, f"cq{tt}")

                def memory_values(tt):
                    w = wkv_v.rearrange("p (k c) -> p k c", k=8)
                    return project_N(banks[7][:, tt * 256:(tt + 1) * 256], w, 0, 256, memG_ring, tt)

                def cross_out(tt):
                    settled(f"xo{tt}")
                    for n in range(2):
                        use = f"co{2 * tt + n}"
                        bank_free(pe, l, use)
                        out_proj(use, 0, 2, 1, coT, tt, lambda k: wo_v[:, k, n * 512:(n + 1) * 512])

                wo_v = dense[:, 2, 2048:4096].rearrange("p (k c) -> p k c", k=2)
                turn("y", "cross", 0)
                pe.wait_ge(vloaded, l * 16 + 16)
                wait("memG_ring")
                bank_free(pe, l, "memv")
                memory_values(0)
                unit_loaded(pe, l, 11)
                cross_query(0)
                bank_done(memory_values(1), "memv")
                settled("cq0")
                scores(NN)
                turn("y", "cross", 1)
                cross_query(1)
                turn_probs(NN)
                settled("cq1", "memv")
                scores(NN + 1)
                bank_free(pe, l, "xo0")
                values(NN)
                cross_out(0)
                turn_probs(NN + 1)
                bank_free(pe, l, "xo1")
                values(NN + 1)
                cross_out(1)

                bk = bank_free(pe, l, "rt")
                for tt in range(2):
                    turn("z", "ffn", tt)
                    settled(f"zT{2 * tt}", f"zT{2 * tt + 1}")
                    for k in range(8):
                        ins = mm(bk[:, tt * 36:(tt + 1) * 36], xnT[:, k, tt * P:(tt + 1) * P],
                                 pcol(l, RW + k * 36, 36), k == 0, k == 7)
                bank_done(ins, "rt")
                wait("chosen")
                bk = bank_free(pe, l, "pos")
                mm(bk[:, 0:E], tri, chosen[:, 0, :], True, True)
                mm(bk[:, E:2 * E], ones, chosen[:, 0, :], True, False)
                mm(bk[:, E:2 * E], tri, chosen[:, 1, :], False, True)
                mm(bk[:, 2 * E:3 * E], ones, chosen[:, 0, :], True, False)
                ins = mm(bk[:, 2 * E:3 * E], ones, chosen[:, 1, :], False, True)
                bank_done(ins, "pos")

                for b in range(8):
                    wait_drained(pe, l, USES[b][-1])
                gbase = base + l

                def gather(n, b):
                    if b == 0:
                        pe.wait_ge(onehot_ready, gbase + n + 1)
                    pe.wait_ge(edrained[b], gbase + n + 1)
                    for d in range(4 * b, 4 * b + 4):
                        for tt in range(2):
                            ins = mm(banks[d // 4][:, (d % 4) * P:(d % 4 + 1) * P], xhat[:, tt, d * P:(d + 1) * P],
                                     pm[:, tt, :, :].rearrange("p e s -> p (e s)"), tt == 0, tt == 1)
                        if d % 4 == 3:
                            ins.then_inc(efilled[d // 4], 1)

                gather(0, 0)
                gather(0, 1)
                wait("npass_ready")
                alone(pe)
                npass = pe.value_load(npass_i[0:1, 0:1], min_val=1, max_val=MAXP)
                def pair(t, odd, slot_of):
                    it = base + t
                    for b in range(2):
                        pe.wait_ge(edrained[b], gbase + t + 2)
                        pe.wait_ge(edrained[2 + b], it + 1)
                    for k in range(8):
                        for n in range(2):
                            for e in range(2):
                                s = k // 4 * 2 + e
                                if k % 4 == n == 0:
                                    expert_loaded(pe, it, odd, s)
                                w = slot_of(s)[:, (k % 4) * 1024 + n * 512:(k % 4) * 1024 + (n + 1) * 512]
                                half = slice(e * SLOTS, (e + 1) * SLOTS)
                                ins = mm(banks[2 + n][half, 0:512], xg[:, k, half], w, k == 0, k == 7)
                            if k == 7:
                                ins.then_inc(efilled[2 + n], 1)
                        if k == 3:
                            ins.then_inc(half_read, 1)
                    gather(t + 1, 0)
                    pe.wait_ge(pg_ready, it + 1)
                    pe.wait_ge(edrained[7], it * 2 + 1)
                    for tt in range(2):
                        ins = pe.transpose(banks[7][:, tt * P:(tt + 1) * P],
                                           pg[:, tt, :, :].rearrange("p e s -> p (e s)"), ident)
                    ins.then_inc(efilled[7], 1)
                    pe.wait_ge(edrained[3], it + 2)
                    pe.wait_ge(edrained[6], it * 2 + 1)
                    for k in range(4):
                        ins = pe.transpose(banks[6][:, k * P:(k + 1) * P], hid[:, k * P:(k + 1) * P], ident)
                    ins.then_inc(efilled[6], 1)
                    gather(t + 1, 1)
                    pe.wait_ge(edrained[6], it * 2 + 2)
                    for b in (4, 5):
                        pe.wait_ge(edrained[b], it * 2 + 1)
                    for k in range(4):
                        for n in range(2):
                            for e in range(2):
                                if k == n == 0:
                                    expert_loaded(pe, it, odd, 4 + e)
                                w = slot_of(4 + e)[:, k * 1024 + n * 512:k * 1024 + (n + 1) * 512]
                                half = slice(e * SLOTS, (e + 1) * SLOTS)
                                ins = mm(banks[4 + n][half, 0:512], ht[:, k, half], w, k == 0, k == 3)
                            if k == 3:
                                ins.then_inc(efilled[4 + n], 1)
                    pe.wait_ge(edrained[7], it * 2 + 2)
                    for n in range(2):
                        pe.wait_ge(edrained[4 + n], it * 2 + 2)
                    for tt in range(2):
                        for n in range(2):
                            b = (6 if tt == 0 else 4) + n
                            mm(banks[b][:, 0:512], pgT[:, tt * P:(tt + 1) * P], ys_b[:, n * 512:(n + 1) * 512],
                               True, True).then_inc(efilled[b], 1)

                with pe.Fori(0, npass * (PAIRS // 2)) as i:
                    pair(i * 2, False, eslot)
                    pair(i * 2 + 1, True, odd_slot)
                pe.reg_add(iters, iters, npass * PAIRS)

        @block.scalar
        def _(act):
            def copy(out_ap, in_ap, scale=1.0):
                return act.activation(out_ap, in_ap, ACT.Copy, scale=scale)

            act.wait_ge(s_mem, 16)
            for tt in range(2):
                ins = act.activation(mem_sq[:, tt, :], mem_raw[:, tt, :], ACT.Square, accum_out=ssq[:, tt:tt + 1])
            ins.then_inc(ev("mem_squares"), 1)
            act.wait_ge(s_consts, 16)
            act.wait_ge(s_setup, 16 * N_SETUP)
            act.wait_ge(ev("lb_in"), 1)
            act.activation(flat(oml[:, :, :]), flat(lbf[:, :, :]), ACT.Exp).then_inc(ev("lb_exp"), 1)
            iters = act.alloc_register("act_iters")
            act.reg_mov(iters, 0)
            with act.Fori(0, DEPTH) as l:
                base = act.snap(iters, min_val=0, max_val=DEPTH * MAXP * PAIRS)

                def wait(name):
                    act.wait_ge(ev(name), l + 1)

                def drain(use, pairs):
                    bk = bank_full(act, l, use)
                    for out_ap, part, scale in pairs:
                        ins = copy(out_ap, part(bk), scale)
                    return ins

                def squares(stage, tt):
                    return act.activation(xhat[:, tt, :], h[:, tt, :], ACT.Square, accum_out=ssq[:, tt:tt + 1])

                def scale(stage):
                    act.activation(xhat[:, 0, :], h[:, 0, :], ACT.Identity,
                                   scale=rs[:, 0:1]).then_inc(ev("xhat0_" + stage), 1)

                def norm(stage, tt):
                    wait(f"h{tt}_{stage}")
                    squares(stage, tt).then_inc(ev(f"squares{tt}_{stage}"), 1)
                    if tt == 0:
                        wait("rstd0_" + stage)
                        scale(stage)

                def turned(prefix, gain, tt):
                    bk = bank_full(act, l, f"{prefix}T{2 * tt + 1}")
                    alone(act)
                    for d in range(4):
                        ins = act.activation(xnT[:, 4 + d, tt * P:(tt + 1) * P], bk[:, d * P:(d + 1) * P],
                                             ACT.Identity, scale=pcol(l, gain + 4 + d, 1))
                    bank_drained(ins, f"{prefix}T{2 * tt + 1}")

                def whole(bk):
                    return bk[:, 0:512]

                act.activation(scratch[:, 33:34], ident[:, 0:1], ACT.Exp)
                for b in (6, 7):
                    act.wait_ge(edrained[b], base * 2 + 1)
                squares("mix", 0)
                wait("h_mix")
                squares("mix", 1).then_inc(ev("squares_mix"), 1)
                bank_drained(drain("memk", [(flat(memk), whole, 1.0)]), "memk")
                wait("rstd_mix")
                scale("mix")
                turned("x", G_MIX, 0)
                turned("x", G_MIX, 1)

                bk = bank_full(act, l, "hf")
                bank_drained(act.activation(f_b, whole(bk), ACT.Exp, scale=-1.0), "hf")
                bank_drained(drain("hq", [(q_b, whole, HD ** -0.5)]), "hq")
                bank_drained(drain("ksvs", [(kraw[:, 0, :], lambda b: b[:, 0:256], 1.0),
                                            (vv[:, 0:256], lambda b: b[:, 256:512], 1.0)]), "ksvs")
                bank_drained(drain("q0", [(qraw_b[:, 0:512], whole, 1.0)]), "q0")
                bank_drained(drain("q1", [(qraw_b[:, 512:1024], whole, 1.0)]), "q1")
                bk = bank_full(act, l, "cmph")
                act.activation(cmp_e, bk[:, 0:P], ACT.Exp, scale=-1.0).then_inc(ev("cmp_e"), 1)
                bk = bank_full(act, l, "hidT")
                copy(flat(cmp_hk[:, :, :]), bk[:, 0:64])
                hid_v = bk[:, 64:128].rearrange("p (v c) -> p v c", v=KV)[:, :, 0:NCMP]
                for i in range(GRP):
                    ins = copy(cmp_hv[:, i, :].rearrange("p (v c) -> p v c", v=KV), hid_v)
                bank_drained(ins, "hidT")
                bank_drained(drain("kw", [(kraw[:, 1, :], lambda b: b[:, 0:256], 1.0)]), "kw")
                bk = bank_full(act, l, "vwgl")
                b3 = bk[:, 0:304].rearrange("p (t c) -> p t c", t=2)
                copy(v_of["win"], b3[:, :, 0:P])
                bank_drained(act.activation(gate[:, :, :], b3[:, :, P:152], ACT.Exp, scale=-1.0), "vwgl")

                def exps(n):
                    nh = GROUPS[n][3]
                    nk = 512 // nh
                    act.wait_ge(ev("max_ready"), l * NG + (n + 1))
                    for v in range(2):
                        bk = banks[PLACE[f"s{n}_{v}"][0]]
                        for j in range(nh):
                            at = v * 512 + j * nk
                            s = v * nh + j
                            ins = act.activation(probs(n)[:, at:at + nk], bk[:, j * nk:(j + 1) * nk], ACT.Exp,
                                                 bias=att_nb[n % 2][:, s:s + 1], scale=HD ** -0.5,
                                                 accum_out=att_sum[n % 2][:, s:s + 1])
                        bank_drained(ins, f"s{n}_{v}")

                def keep_pT(n):
                    bank_drained(drain(f"t{n}_0", [(pT_of(n)[:, 0:512], whole, 1.0)]), f"t{n}_0")

                wait("cmp_shifted")
                act.activation(cmpP, cmpP, ACT.Exp,
                               scale=HD ** -0.5).then_inc(ev("cmp_exp"), 1)
                exps(0)
                bank_drained(drain("cb", [(cvb_b, whole, 1.0)]), "cb")
                bank_drained(drain("cmp_t", [(cmpPT, lambda b: b[:, 0:256], 1.0)]), "cmp_t")
                exps(1)
                keep_pT(0)
                bank_drained(drain("cc", [(cvc_b, whole, 1.0)]), "cc")
                exps(2)
                keep_pT(1)
                bk = bank_full(act, l, "hg")
                act.activation(hgs_b, whole(bk), ACT.Exp, scale=-1.0)
                bank_drained(copy(hgr_b, whole(bk)), "hg")
                wait("o_tile0")
                copy(mixT[:, 0:2, 0:P], two(banks[6][:, 0:512])[:, :, 0:P]).then_inc(ev("mix0_heads01"), 1)
                exps(3)
                keep_pT(2)
                bank_drained(drain("ch", [(cvh_b, whole, 1.0)]), "ch")
                exps(4)
                keep_pT(3)
                for half in range(2):
                    use = f"off_{half}"
                    ao = A_[2].rearrange("p (c h) t -> p c h t", h=2)[:, :, half, :]
                    bank_drained(drain(use, [(ao, lambda b: two(b[:, 0:256]), 1.0)]), use)
                bank_drained(drain("hi", [(hi_b, whole, 1.0)]), "hi")
                exps(5)
                keep_pT(4)
                bk = bank_full(act, l, "av")
                act.activation(kt0_b, whole(bk), ACT.Square).then_inc(ev("o_squares"), 1)
                keep_pT(5)
                bank_drained(drain("o6", [(mixT[:, 0:2, P:256], lambda b: two(b[:, 0:512])[:, :, P:256], 1.0)]), "o6")
                bk = bank_full(act, l, "hot")
                for c in range(2):
                    ins = act.activation(mixT[:, 6 + c, :], bk[:, c * 256:(c + 1) * 256], ACT.Identity,
                                         scale=pcol(l, HNORM + c, 1))
                bank_drained(ins, "hot")

                def keep_queries(tt):
                    bank_drained(drain(f"cq{tt}", [(cq[:, :, tt * P:(tt + 1) * P], lambda b: two(b[:, 0:256]), 1.0)]),
                                 f"cq{tt}")

                norm("cross", 0)
                norm("cross", 1)
                turned("y", G_CROSS, 0)
                keep_queries(0)
                bank_drained(drain("memv", [(flat(memv), whole, 1.0)]), "memv")
                turned("y", G_CROSS, 1)
                exps(NN)
                keep_queries(1)
                keep_pT(NN)
                exps(NN + 1)
                keep_pT(NN + 1)
                bank_drained(drain("xo1", [(coT[:, :, P:256], lambda b: two(b[:, 0:256]), 1.0)]), "xo1")
                norm("ffn", 0)
                norm("ffn", 1)
                turned("z", G_FFN, 0)
                turned("z", G_FFN, 1)
                wait("route_in")
                act.activation(rexp[:, :, 0:5], rlog[:, :, 0:5], ACT.Exp).then_inc(ev("route_exp"), 1)

                wait("npass_ready")
                alone(act)
                npass = act.value_load(npass_i[0:1, 0:1], min_val=1, max_val=MAXP)
                with act.Fori(0, npass * PAIRS) as t:
                    it = base + t
                    act.wait_ge(efilled[2], it + 1)
                    act.activation(sgate, banks[2][:, 0:512], ACT.Silu).then_inc(edrained[2], 1)
                    act.wait_ge(efilled[6], it * 2 + 1)
                    act.activation(ht_b, banks[6][:, 0:512], ACT.Copy).then_inc(edrained[6], 1)
                    act.wait_ge(efilled[4], it * 2 + 1)
                    act.activation(ys_b[:, 0:512], banks[4][:, 0:512], ACT.Copy).then_inc(edrained[4], 1)
                act.reg_add(iters, iters, npass * PAIRS)

            act.wait_ge(ev("h_mix"), DEPTH + 1)
            for tt in range(2):
                ins = act.activation(xhat[:, tt, :], h[:, tt, :], ACT.Square, accum_out=ssq[:, tt:tt + 1])
            ins.then_inc(ev("squares_final"), 1)
            act.wait_ge(ev("rstd_final"), 1)
            act.activation(xhat[:, 0, :], h[:, 0, :], ACT.Identity, scale=rs[:, 0:1]).then_inc(ev("xhat0_final"), 1)

        @block.gpsimd
        def _(pool):
            for b in range(8):
                pool.memset(scratch[:, b:b + 1], 0.0).then_inc(edrained[b], 1)
            for b in range(4, 8):
                pool.memset(scratch[:, 4 + b:5 + b], 0.0).then_inc(drained[b], 1)
            pool.wait_ge(s_consts, 16)
            pool.wait_ge(s_setup, 16 * N_SETUP)
            pool.wait_ge(ev("memT_ready"), 1)

            def gained(place, l):
                gain = pcol(l, G_MEM, 8).unsqueeze(2).broadcast_to([P, 8, 256])
                return pool.tensor_tensor(place, memT[:, :, :], gain, ALU.mult)

            with pool.Fori(0, DEPTH) as l:
                chain = Chain(pool, pool_step, l * POOL_STEPS, POOL_STEPS, apart=True)

                def wait(name):
                    pool.wait_ge(ev(name), l + 1)
                    alone(pool)

                def tt_(out_ap, a, c, op):
                    return pool.tensor_tensor(out_ap, a, c, op)

                wait("h_mix")
                gained(memG_ring, l).then_inc(ev("memG_ring"), 1)
                pool.tensor_copy(cvw[:, :], pcol(l, CONVW, 6)).then_inc(ev("conv_w"), 1)
                chain.link(pool.memset(cv_u[:, :, 0:2], 0.0))
                chain.link(pool.memset(g_b, 1.0))
                chain.link(pool.memset(a0_b, 0.0))
                chain.link(pool.memset(xe[:, :, :, NCMP - 1], 0.0))
                chain.link(pool.memset(xe_b[:, 1024:1040], 0.0))
                pool.memset(a1_b, 0.0).then_inc(ev("a_zero"), 1)

                def halves(ap, L):
                    return ap.rearrange("p (n s u) -> p n s u", s=2, u=L)

                def lower(L):
                    return halves(g_b, L)[:, :, 0, :]

                wait("f_ready")
                tot_at = {}
                at = 0
                for L in HALVES[1:]:
                    tot_at[L] = tot[:, at:at + 512 // L]
                    at += 512 // L
                chain.link(pool.tensor_copy(lower(1), halves(f_b, 1)[:, :, 1, :]))
                ff = f_b.rearrange("p (n s) -> p n s", s=2)
                tt_(tot_at[2], ff[:, :, 0], ff[:, :, 1], ALU.mult).then_inc(ev("tot2"), 1)
                wait("tot2")
                wait("k_ready")
                for L in HALVES[1:] + [128]:
                    i = (HALVES + [128]).index(L)
                    if i >= 3:
                        bank_full(pool, l, f"lv{L // 4}_1")
                    tt_(kt_b[i % 2], k_b, g_b, ALU.mult).then_inc(ev(f"kt{L}"), 1)
                    if L == 128:
                        break
                    tv = tot_at[L].rearrange("p (n s) -> p n s", s=2)
                    wait(f"kt{L}")
                    chain.link(tt_(lower(L), lower(L), tv[:, :, 1].unsqueeze(2).broadcast_to([P, 256 // L, L]), ALU.mult))
                    if L < 64:
                        chain.link(tt_(tot_at[2 * L], tv[:, :, 0], tv[:, :, 1], ALU.mult))
                    if L == 4:
                        wait_drained(pool, l, "q0")
                        wait_drained(pool, l, "q1")
                        tt_(qrot, qraw, cos.unsqueeze(1).broadcast_to([P, GRP, 256]), ALU.mult).then_inc(ev("q_cos"), 1)
                    if L == 8:
                        wait_drained(pool, l, "ksvs")
                        wait_drained(pool, l, "kw")
                        tt_(krot, kraw, cos.unsqueeze(1).broadcast_to([P, 2, 256]), ALU.mult).then_inc(ev("k_cos"), 1)

                wait_drained(pool, l, "ch")
                wait_drained(pool, l, "cb")
                wait_drained(pool, l, "cc")
                wait("conv_w")
                chain.link(tt_(cv_u[:, :, 2:258], cv_c, cv_h, ALU.mult))
                for c in range(2):
                    ins = pool.tensor_scalar(cv_y[:, c, :], cv_u[:, c, 0:256], cvw[:, c * 3:c * 3 + 1], None, ALU.mult)
                chain.link(ins)
                for tap in (1, 2):
                    for c in range(2):
                        ins = pool.tensor_scalar(cv_h[:, c, :], cv_u[:, c, tap:tap + 256],
                                                 cvw[:, c * 3 + tap:c * 3 + tap + 1], None, ALU.mult)
                    chain.link(ins)
                    chain.link(tt_(cvy_b, cvy_b, cvh_b, ALU.add))
                tt_(flat(mixT[:, 4:6, :]), cvy_b, cvb_b, ALU.mult).then_inc(ev("conv_done"), 1)
                bank_full(pool, l, "rt")
                alone(pool)
                gained(xnT[:, :, :], (l + 1) % DEPTH).then_inc(ev("memG"), 1)
                chain.close()

        @block.vector
        def _(dve):
            V = dve
            MUL, ADD, SUB, MAX, MIN, EQ, GT = (ALU.mult, ALU.add, ALU.subtract, ALU.max, ALU.min, ALU.is_equal,
                                               ALU.is_gt)
            setup = Chain(dve, setup_step, 0, None)

            def bc(ap, *shape):
                return ap.broadcast_to([P, *shape])

            def inverse_root(link, y, squares, scale):
                n = y.shape[1]
                x, t = root_x[:, 0:n], root_t[:, 0:n]
                link(V.tensor_scalar(x, squares, scale, EPS, MUL, ADD))
                link(V.tensor_scalar(t.bitcast(I32), x.bitcast(I32), 1, None, ALU.logical_shift_right))
                link(V.tensor_scalar(y.bitcast(I32), t.bitcast(I32), -1.0, float(0x5F3759DF), MUL, ADD))
                for step in range(3):
                    link(V.tensor_tensor(t, y, y, MUL))
                    link(V.scalar_tensor_tensor(t, t, -0.5, x, MUL, MUL))
                    ins = V.scalar_tensor_tensor(y, t, 1.5, y, ADD, MUL)
                    if step < 2:
                        link(ins)
                return ins

            dve.wait_ge(s_mem, 16)
            dve.wait_ge(ev("mem_squares"), 1)
            setup.link(inverse_root(setup.link, rs, ssq, 1.0 / D))
            for tt in range(2):
                V.tensor_scalar(mem_raw[:, tt, :], mem_raw[:, tt, :], rs[:, tt:tt + 1], None,
                                MUL).then_inc(ev("mem_hat"), 1)
            dve.wait_ge(s_consts, 16)
            dve.wait_ge(s_setup, 16 * N_SETUP)
            V.tensor_copy(lvmask[:, :, :], mask_in).then_inc(ev("masks"), 1)
            V.tensor_copy(cbf[:, :], rest[:, 1024:1312]).then_inc(ev("masks"), 1)

            mx, tot_, run = lbt[:, 0:2], lbt[:, 2:4], lbt[:, 4:6]
            setup.link(V.tensor_reduce(mx, lb_in[:, :, :].rearrange("p l c -> p c l"), AX, MAX))
            V.tensor_tensor(lbf[:, :, :], lb_in[:, :, :], bc(mx.unsqueeze(1), DEPTH, 2), SUB).then_inc(ev("lb_in"), 1)
            V.memset(posv[:, :, MAXP * E:COLS], -1.0)
            V.memset(gates[:, :, MAXP * E:COLS], 0.0)
            dve.wait_ge(ev("lb_exp"), 1)
            setup.link(V.tensor_reduce(tot_, oml[:, :, :].rearrange("p l c -> p c l"), AX, ADD))
            setup.link(V.reciprocal(tot_, tot_))
            setup.link(V.tensor_tensor(oml[:, :, :], oml[:, :, :], bc(tot_.unsqueeze(1), DEPTH, 2), MUL))
            setup.link(V.tensor_copy(lbf[:, 0, :], oml[:, 0, :]))
            for j in range(1, DEPTH):
                setup.link(V.tensor_tensor(lbf[:, j, :], lbf[:, j - 1, :], oml[:, j, :], ADD))
            setup.link(V.tensor_copy(run, oml[:, 0, :]))
            setup.link(V.tensor_tensor(lbf[:, :, :], lbf[:, :, :], bc(run.unsqueeze(1), DEPTH, 2), SUB))
            setup.link(V.tensor_scalar(oml[:, :, :], lbf[:, :, :], -1.0, 1.0, MUL, ADD))
            setup.link(V.tensor_scalar(lbf[:, :, :], lbf[:, :, :], LB_FLOOR, None, MAX))
            dve.wait_ge(ev("mem_turned"), 1)
            for j in range(4):
                g = bc(pcol(0, G_MEM + 2 * j, 2).unsqueeze(2), 2, 256)
                ins = V.tensor_tensor(xnT[:, 2 * j:2 * j + 2, :], two(banks[j][:, 0:512]), g, MUL)
            ins.then_inc(ev("memG"), 1)
            for j in range(4):
                V.tensor_copy(flat(memT[:, 2 * j:2 * j + 2, :]), banks[j][:, 0:512]).then_inc(drained[j], 1)
            for j in range(4):
                dve.wait_ge(drained[j], 1)
            dve.wait_ge(ev("masks"), 2)
            V.memset(scratch[:, 24:25], 0.0).then_inc(ev("memT_ready"), 1)

            iters = dve.alloc_register("dve_iters")
            dve.reg_mov(iters, 0)
            with dve.Fori(0, DEPTH) as l:
                base = dve.snap(iters, min_val=0, max_val=DEPTH * MAXP * PAIRS)
                chain = Chain(dve, dve_step, l * DVE_STEPS, DVE_STEPS)
                link = chain.link

                def wait(name):
                    dve.wait_ge(ev(name), l + 1)

                def own(name, ins):
                    ins.then_inc(ev(name), 1)
                    wait(name)

                def norm(stage, tt):
                    wait(f"squares{tt}_{stage}")
                    own(f"rstd{tt}_{stage}", inverse_root(link, rs[:, tt:tt + 1], ssq[:, tt:tt + 1], 1.0 / D))
                    if tt == 1:
                        V.tensor_scalar(xhat[:, 1, :], h[:, 1, :], rs[:, 1:2], None,
                                        MUL).then_inc(ev("xhat1_" + stage), 1)

                def turned(prefix, gain, tt):
                    bk = bank_full(dve, l, f"{prefix}T{2 * tt}")
                    g = bc(pcol(l, gain, 4).unsqueeze(2), 4, P)
                    bank_drained(V.tensor_tensor(xnT[:, 0:4, tt * P:(tt + 1) * P],
                                                 bk[:, 0:512].rearrange("p (d t) -> p d t", d=4), g, MUL),
                                 f"{prefix}T{2 * tt}")

                def add_out(prefix, stage, tt):
                    for n in range(2):
                        use = f"{prefix}{tt * 2 + n}"
                        bk = bank_full(dve, l, use)
                        hh = h[:, tt, n * 512:(n + 1) * 512]
                        bank_drained(V.tensor_tensor(hh, hh, bk[:, 0:512], ADD), use)
                    for n in range(2):
                        wait_drained(dve, l, f"{prefix}{tt * 2 + n}")
                    done(f"h{tt}_{stage}", 28 + tt)

                def done(name, col):
                    V.memset(scratch[:, col:col + 1], 0.0).then_inc(ev(name), 1)

                done("h_mix", 25)
                wait("squares_mix")
                own("rstd_mix", inverse_root(link, rs, ssq, 1.0 / D))
                V.tensor_scalar(xhat[:, 1, :], h[:, 1, :], rs[:, 1:2], None, MUL).then_inc(ev("xhat1_mix"), 1)
                turned("x", G_MIX, 0)
                turned("x", G_MIX, 1)

                wait_drained(dve, l, "hf")
                link(V.tensor_scalar(tmp, f_b, 1e37, 1.0, MIN, ADD))
                link(V.reciprocal(tmp, tmp))
                link(V.scalar_tensor_tensor(k_b, f_b, 1e37, tmp, MIN, MUL))
                for c in range(2):
                    ins = V.tensor_scalar(f_[:, c, :], two(tmp)[:, c, :], oml[:, l, c:c + 1], lbf[:, l, c:c + 1],
                                          MUL, ADD)
                own("f_ready", ins)
                for c in range(2):
                    ins = V.tensor_scalar(k_[:, c, :], k_[:, c, :], oml[:, l, c:c + 1], None, MUL)
                ins.then_inc(ev("k_ready"), 1)

                def level_q(L):
                    i = (HALVES + [128]).index(L)
                    own(f"qt{L}", V.tensor_tensor(qt_b[i % 2], q_b, f_b, MUL))
                    if L == 1:
                        wait("tot2")
                    if L < 128:
                        ff = f_b.rearrange("p (n s u) -> p n s u", s=2, u=L)
                        link(V.tensor_tensor(ff[:, :, 1, :], ff[:, :, 1, :],
                                             bc(ff[:, :, 0, L - 1:L], 256 // L, L), MUL))

                def level_mask(name, m):
                    for half in range(2):
                        use = f"{name}_{half}"
                        bk = bank_full(dve, l, use)
                        if m > 0:
                            wait_drained(dve, l, f"{prev_level[name]}_{half}")
                        alone(dve)
                        bank_drained(V.copy_predicated(a01[:, :, half, :], bc(lvmask[:, m, :].unsqueeze(1), 4, P),
                                                       bk[:, 0:512].rearrange("p (n t) -> p n t", n=4)), use)

                prev_level = {"lv1": "dg"} | {f"lv{2 * L}": f"lv{L}" for L in HALVES[:-1]}
                def rotate(use, rot, name, last):
                    bk = bank_full(dve, l, use)
                    s = bc(sin.unsqueeze(1), 2, 256)
                    bank_drained(V.tensor_tensor(two(tmp), two(bk[:, 0:512]), s, MUL), use)
                    wait_drained(dve, l, use)
                    wait(name + "_cos")
                    ins = V.tensor_tensor(rot, rot, tmp, ADD)
                    if last:
                        ins.then_inc(ev(name + "rot"), 1)
                    else:
                        link(ins)

                def maxima(n):
                    nh = GROUPS[n][3]
                    for v in range(2):
                        bk = bank_full(dve, l, f"s{n}_{v}")
                        ins = V.tensor_reduce(att_mx[n % 2][:, v * nh:(v + 1) * nh],
                                              bk[:, 0:512].rearrange("p (h k) -> p h k", h=nh), AX, MAX)
                    link(ins)
                    V.tensor_scalar(att_nb[n % 2][:, 0:2 * nh], att_mx[n % 2][:, 0:2 * nh], -HD ** -0.5, None,
                                    MUL).then_inc(ev("max_ready"), 1)

                def normalise(n):
                    br, tt, i0, nh = GROUPS[n]
                    for v in range(2):
                        wait_drained(dve, l, f"s{n}_{v}")
                    r = att_rr[n % 2][:, 0:2 * nh]
                    link(V.reciprocal(r, att_sum[n % 2][:, 0:2 * nh]))
                    if br != "cross":
                        gv = gate[:, tt, :].rearrange("p (v i b) -> p v i b", v=KV, i=GRP)
                        r2 = r.rearrange("p (v i) -> p v i", v=KV)
                        link(V.tensor_tensor(r2, r2, gv[:, :, i0:i0 + nh, 1 if br == "sel" else 2], MUL))
                    pp = probs(n).rearrange("p (h k) -> p h k", h=2 * nh)
                    V.tensor_tensor(pp, pp, bc(r.unsqueeze(2), 2 * nh, 512 // nh), MUL).then_inc(ev("p_scaled"), 1)

                def keep_pT(n):
                    bk = bank_full(dve, l, f"t{n}_1")
                    bank_drained(V.tensor_copy(pT_of(n)[:, 512:1024], bk[:, 0:512]), f"t{n}_1")

                wait_drained(dve, l, "hq")
                level_q(1)
                bk = bank_full(dve, l, "ckv")
                b3 = bk[:, 0:512].rearrange("p (g u) -> p g u", g=4)
                for s in range(2):
                    for a in (0, 8):
                        pe_ = pcol(l, PE_C + s * 16 + a, 8).unsqueeze(1).unsqueeze(3)
                        ins = V.tensor_tensor(
                            xe[:, s * 2:s * 2 + 2, a:a + 8, 0:15],
                            b3[:, s * 2:s * 2 + 2, a:a + 120].rearrange("p g (c a) -> p g a c", a=8),
                            bc(pe_, 2, 8, 15), ADD)
                wait("a_zero")
                bank_drained(ins, "ckv")
                level_mask("dg", 0)
                level_q(2)
                bk = bank_full(dve, l, "cmph")
                wait("cmp_e")
                link(V.tensor_scalar(cmp_e, cmp_e, 1.0, None, ADD))
                link(V.reciprocal(cmp_e, cmp_e))
                own("cmp_hid", V.tensor_tensor(cmp_x, cmp_e, bk[:, 0:P], MUL))
                bank_drained(V.memset(scratch[:, 26:27], 0.0), "cmph")
                level_mask("lv1", 1)
                level_q(4)
                rotate("rq0", qrot_b[:, 0:512], "q", False)
                rotate("rq1", qrot_b[:, 512:1024], "q", True)
                level_mask("lv2", 2)
                level_q(8)
                wait_drained(dve, l, "vwgl")
                gf = flat(gate[:, :, :])
                link(V.tensor_scalar(gf, gf, 1.0, None, ADD))
                link(V.reciprocal(gf, gf))
                bk = bank_full(dve, l, "cmpo")
                V.tensor_copy(kc[:, :], bk[:, 0:NCMP])
                bank_drained(V.tensor_tensor(
                    vblk.rearrange("p i (v d) -> p i v d", v=KV),
                    bc(bk[:, 64:64 + P].rearrange("p (v d) -> p v d", v=KV).unsqueeze(1), GRP, KV, HD),
                    bc(own_block.unsqueeze(3), GRP, KV, HD), MUL), "cmpo")
                rotate("rk", krot_b, "k", True)
                level_mask("lv4", 3)
                level_q(16)

                cp = cmpP.rearrange("p (g c) -> p g c", c=NCMP)
                cp4 = cmpP.rearrange("p (g v c) -> p g v c", v=KV, c=NCMP)
                for v in range(KV):
                    bk = bank_full(dve, l, f"cmp_s_{v}")
                    sc = bk[:, 0:128].rearrange("p (g c) -> p g c", c=NCMP)
                    link(V.tensor_reduce(cmx[:, v * 8:(v + 1) * 8], sc, AX, MAX))
                    bank_drained(V.tensor_tensor(cp4[:, :, v, :], sc,
                                                 bc(cmx[:, v * 8:(v + 1) * 8].unsqueeze(2), 8, NCMP), SUB),
                                 f"cmp_s_{v}")
                for v in range(KV):
                    wait_drained(dve, l, f"cmp_s_{v}")
                done("cmp_shifted", 27)
                maxima(0)
                wait("cmp_exp")
                for tt in range(2):
                    ct = cmpP[:, tt * P:(tt + 1) * P].rearrange("p (g c) -> p g c", c=NCMP)
                    ins = V.tensor_tensor(ct, ct, bc(cmp_ok[:, tt, :].unsqueeze(1), 8, NCMP), MUL)
                link(ins)
                link(V.tensor_reduce(csum, cp, AX, ADD))
                link(V.tensor_scalar(csum, csum, 1e-30, None, MAX))
                link(V.reciprocal(crr, csum))
                g0 = gate[:, :, :].rearrange("p t (v i b) -> p t i v b", v=KV, i=GRP)
                for tt in range(2):
                    c2 = crr[:, tt * 8:(tt + 1) * 8].rearrange("p (i v) -> p i v", v=KV)
                    ins = V.tensor_tensor(c2, c2, g0[:, tt, :, :, 0], MUL)
                link(ins)
                V.tensor_tensor(cp, cp, bc(crr.unsqueeze(2), 16, NCMP), MUL).then_inc(ev("cmp_p"), 1)

                level_mask("lv8", 4)
                level_q(32)
                normalise(0)
                maxima(1)
                keep_pT(0)
                normalise(1)
                maxima(2)
                level_mask("lv16", 5)
                level_q(64)
                keep_pT(1)
                normalise(2)
                wait("o_tile0")
                V.tensor_copy(mixT[:, 2:4, 0:P], two(banks[7][:, 0:512])[:, :, 0:P]).then_inc(ev("mix0_heads23"), 1)
                maxima(3)
                level_mask("lv32", 6)
                level_q(128)
                keep_pT(2)
                normalise(3)
                maxima(4)
                level_mask("lv64", 7)
                keep_pT(3)
                wait_drained(dve, l, "hg")
                link(V.tensor_scalar(hgs_b, hgs_b, 1.0, None, ADD))
                link(V.reciprocal(hgs_b, hgs_b))
                link(V.tensor_tensor(hgs_b, hgs_b, hgr_b, MUL))
                normalise(4)
                maxima(5)
                keep_pT(4)
                normalise(5)
                wait("o_squares")
                link(V.tensor_reduce(hsum, kt0_b.rearrange("p (g e) -> p g e", e=HD), AX, ADD))
                link(inverse_root(link, hrs, hsum, 1.0 / HD))
                bk = bank_full(dve, l, "av")
                o_ = kt1_b.rearrange("p (g e) -> p g e", e=HD)
                bank_drained(V.tensor_tensor(o_, bk[:, 0:512].rearrange("p (g e) -> p g e", e=HD),
                                             bc(hrs.unsqueeze(2), 8, HD), MUL), "av")
                wait_drained(dve, l, "av")
                V.tensor_tensor(kt1_b, kt1_b, hgs_b, MUL).then_inc(ev("hgrn_o"), 1)
                keep_pT(5)
                bk = bank_full(dve, l, "o7")
                bank_drained(V.tensor_copy(mixT[:, 2:4, P:256], two(bk[:, 0:512])[:, :, P:256]), "o7")

                add_out("wo", "cross", 0)
                norm("cross", 0)
                add_out("wo", "cross", 1)
                turned("y", G_CROSS, 0)
                norm("cross", 1)
                maxima(NN)
                turned("y", G_CROSS, 1)
                normalise(NN)
                keep_pT(NN)
                maxima(NN + 1)
                bk = bank_full(dve, l, "xo0")
                bank_drained(V.tensor_copy(coT[:, :, 0:P], two(bk[:, 0:256])), "xo0")
                normalise(NN + 1)
                add_out("co", "ffn", 0)
                keep_pT(NN + 1)
                norm("ffn", 0)
                add_out("co", "ffn", 1)
                turned("z", G_FFN, 0)
                norm("ffn", 1)
                turned("z", G_FFN, 1)

                bk = bank_full(dve, l, "rt")
                lg = rl[:, :, 0:4]
                le = rl[:, :, 4:36]
                bank_drained(V.tensor_tensor(rl, bk[:, 0:72].rearrange("p (t c) -> p t c", t=2),
                                             bc(pcol(l, RBIAS, 36).unsqueeze(1), 2, 36), ADD), "rt")
                wait_drained(dve, l, "rt")

                def first_of_max(best, vals, iota, n, onehot):
                    link(V.tensor_tensor(onehot, vals, bc(best.unsqueeze(2), 2, n), EQ))
                    link(V.tensor_tensor(onehot, onehot, bc(iota.unsqueeze(1), 2, n), MUL))
                    link(V.tensor_reduce(r_min, onehot, AX, MIN))
                    link(V.tensor_tensor(onehot, bc(iota.unsqueeze(1), 2, n), bc(r_min.unsqueeze(2), 2, n), EQ))

                link(V.tensor_reduce(r_mg, lg, AX, MAX))
                first_of_max(r_mg, lg, iota_g, 4, r_g1)
                link(V.tensor_scalar(r_in.rearrange("p t (g e) -> p t g e", g=4), bc(r_g1.unsqueeze(3), 2, 4, 8),
                                     1e30, -1e30, MUL, ADD))
                link(V.tensor_tensor(le, le, r_in, ADD))
                link(V.tensor_reduce(r_e1, le, AX, MAX))
                first_of_max(r_e1, le, iota_e, 32, r_o1)
                link(V.scalar_tensor_tensor(r_in, r_o1, -1e30, le, MUL, ADD))
                link(V.tensor_reduce(r_e2, r_in, AX, MAX))
                first_of_max(r_e2, r_in, iota_e, 32, r_o2)
                own("chosen", V.tensor_tensor(chosen, r_o1, r_o2, ADD))
                V.tensor_tensor(rlog[:, :, 0:4], lg, bc(r_mg.unsqueeze(2), 2, 4), SUB)
                V.tensor_tensor(rlog[:, :, 4], r_e2, r_e1, SUB).then_inc(ev("route_in"), 1)
                wait("route_exp")
                link(V.tensor_reduce(r_sg, rexp[:, :, 0:4], AX, ADD))
                link(V.scalar_tensor_tensor(r_t, rexp[:, :, 4], 1.0, r_sg, ADD, MUL))
                link(V.reciprocal(r_e1, r_t))
                link(V.tensor_tensor(r_e2, r_e1, rexp[:, :, 4], MUL))
                link(V.tensor_tensor(r_o1, r_o1, bc(r_e1.unsqueeze(2), 2, 32), MUL))
                link(V.tensor_tensor(r_o2, r_o2, bc(r_e2.unsqueeze(2), 2, 32), MUL))
                for p_ in range(MAXP):
                    ins = V.tensor_tensor(gates[:, :, p_ * E:(p_ + 1) * E], r_o1, r_o2, ADD)
                link(ins)
                gbase = base + l

                def onehot(col):
                    for tt in range(2):
                        ins = V.tensor_tensor(pm[:, tt, :, :], bc(iota_slot.unsqueeze(1), 2, SLOTS),
                                              bc(posv[:, tt, col].unsqueeze(2), 2, SLOTS), EQ)
                    return ins

                bk = bank_full(dve, l, "pos")
                link(V.tensor_reduce(r_cnt, bk[:, 2 * E:3 * E], AX, MAX))
                pos0 = posv[:, :, 0:E]
                bank_drained(V.scalar_tensor_tensor(pos0, bk[:, 0:2 * E].rearrange("p (t e) -> p t e", t=2), 1.0,
                                                    chosen, ADD, MUL), "pos")
                wait_drained(dve, l, "pos")
                link(V.tensor_scalar(pos0, pos0, -1.0, None, ADD))
                onehot(slice(0, 2)).then_inc(onehot_ready, 1)
                for p_ in range(1, MAXP):
                    ins = V.tensor_scalar(posv[:, :, p_ * E:(p_ + 1) * E], pos0, -float(p_ * SLOTS), None, ADD)
                    link(ins)
                link(V.memset(r_np, 1.0))
                for p_ in range(1, MAXP):
                    link(V.scalar_tensor_tensor(r_np, r_cnt, float(p_ * SLOTS), r_np, GT, ADD))
                own("npass_ready", V.tensor_copy(npass_i[0:1, 0:1], r_np[0:1, :]))
                chain.close()

                alone(dve)
                npass = dve.value_load(npass_i[0:1, 0:1], min_val=1, max_val=MAXP)
                def gathered(n):
                    for b in range(2):
                        dve.wait_ge(efilled[b], gbase + n + 1)
                        g = bc(pcol(l, G_FFN + 4 * b, 4).unsqueeze(2), 4, P)
                        V.tensor_tensor(xg[:, 4 * b:4 * b + 4, :], banks[b][:, 0:512].rearrange("p (d s) -> p d s", d=4),
                                        g, MUL).then_inc(edrained[b], 1)

                gathered(0)
                with dve.Fori(0, npass * PAIRS) as t:
                    it = base + t
                    dve.wait_ge(onehot_ready, gbase + t + 1)
                    for tt in range(2):
                        ins = V.tensor_tensor(pg[:, tt, :, :], pm[:, tt, :, :],
                                              bc(gates[:, tt, bass.ds(t * 2, 2)].unsqueeze(2), 2, SLOTS), MUL)
                    ins.then_inc(pg_ready, 1)
                    dve.wait_ge(pg_ready, it + 1)
                    onehot(bass.ds(t * 2 + 2, 2)).then_inc(onehot_ready, 1)
                    dve.wait_ge(efilled[3], it + 1)
                    dve.wait_ge(edrained[2], it + 2)
                    V.tensor_tensor(hid, sgate, banks[3][:, 0:512], MUL).then_inc(edrained[3], 1)
                    gathered(t + 1)
                    dve.wait_ge(efilled[7], it * 2 + 1)
                    V.tensor_copy(pgT, banks[7][:, 0:256]).then_inc(edrained[7], 1)
                    dve.wait_ge(efilled[5], it * 2 + 1)
                    V.tensor_copy(ys_b[:, 512:1024], banks[5][:, 0:512]).then_inc(edrained[5], 1)
                    for tt in range(2):
                        for n in range(2):
                            b = (6 if tt == 0 else 4) + n
                            dve.wait_ge(efilled[b], it * 2 + 2)
                            hh = h[:, tt, n * 512:(n + 1) * 512]
                            V.tensor_tensor(hh, hh, banks[b][:, 0:512], ADD).then_inc(edrained[b], 1)
                    for b in (4, 5, 6, 7):
                        dve.wait_ge(edrained[b], it * 2 + 3)
                dve.reg_add(iters, iters, npass * PAIRS)

            V.memset(scratch[:, 31:32], 0.0).then_inc(ev("h_mix"), 1)
            dve.wait_ge(s_gain, 16)
            dve.wait_ge(ev("squares_final"), 1)
            inverse_root(setup.link, rs, ssq, 1.0 / D).then_inc(ev("rstd_final"), 1)
            dve.wait_ge(ev("rstd_final"), 1)
            setup.link(V.tensor_scalar(xhat[:, 1, :], h[:, 1, :], rs[:, 1:2], None, MUL))
            V.tensor_tensor(xhat[:, 1, :], xhat[:, 1, :], gain_row, MUL)
            dve.wait_ge(ev("xhat0_final"), 1)
            setup.link(V.tensor_tensor(xhat[:, 0, :], xhat[:, 0, :], gain_row, MUL))
            V.memset(scratch[:, 32:33], 0.0).then_inc(ev("out_ready"), 1)


def constants():
    import numpy as np

    p = np.arange(P)
    half = HD // 2
    inv = (10000.0 ** (-np.arange(half, dtype=np.float32) / half)).astype(np.float32)
    ang = (np.arange(256, dtype=np.float32)[None, :] * inv[p % half][:, None]).astype(np.float32)
    sign = np.where(p % HD < half, -1.0, 1.0)[:, None]
    eye = np.eye(P, dtype=np.float32)
    tok = np.arange(2)[None, :, None] * P + p[:, None, None]
    blk = np.arange(NCMP)[None, None, :]
    ok = ((blk * 16 + 31 <= tok) & (blk < NCMP - 1)).astype(np.float32)
    rows = np.arange(P) // NCMP
    own = np.zeros((P, GRP, KV), np.float32)
    own[p, rows // KV, rows % KV] = 1.0
    f = np.concatenate([
        eye, eye[p ^ half], (p[:, None] < p[None, :]).astype(np.float32), np.ones((P, P), np.float32),
        np.cos(ang), np.sin(ang) * sign,
        np.broadcast_to(np.arange(SLOTS, dtype=np.float32), (P, SLOTS)),
        np.broadcast_to(np.arange(4) - TOP_IDX, (P, 4)), np.broadcast_to(np.arange(32) - TOP_IDX, (P, 32)),
        ok.reshape(P, 32), own.reshape(P, 8)], axis=1).astype(np.float32)
    bf = np.concatenate([
        eye, np.where(p[None, :] > p[:, None], -1e30, 0.0), (1.0 - ok.reshape(P, 32)) * -1e30], axis=1)
    s, t = p[:, None], p[None, :]
    masks = [s == t] + [(s // (2 * L) == t // (2 * L)) & (s % (2 * L) < L) & (t % (2 * L) >= L) for L in HALVES]
    return f, np.concatenate([np.stack(masks, 1).reshape(P, -1), bf], axis=1).astype(np.float32)


def kernel(**inputs):
    import numpy as _np
    import concourse.bacc as _bacc
    from concourse import mybir as _mybir
    from concourse.bass_utils import run_bass_kernel_spmd as _run

    a = {k: _np.asarray(v) for k, v in inputs.items()}
    L = a["w_in"].shape[0]

    def cols(w):
        n = w.shape[1] // P
        return _np.moveaxis(w.reshape(L, n, P, -1), 1, 2).reshape(L, P, -1)

    def rows(w):
        return _np.broadcast_to(w[:, None, :], (L, P, w.shape[-1]))

    conv = _np.moveaxis(a["conv_w"].reshape(L, 3, 2, P), 3, 1).transpose(0, 1, 3, 2).reshape(L, P, 6)
    pe = a["cmp_pe"].reshape(L, 2, 16, 2, HD).transpose(0, 3, 4, 1, 2).reshape(L, P, 32)
    router = _np.concatenate([a["router_group_w"], a["router_expert_w"]], axis=2)
    params = _np.concatenate([
        cols(a["norm_mix"]), cols(a["norm_cross"]), cols(a["norm_mem"]), cols(a["norm_ffn"]), conv, pe,
        cols(a["hgrn_norm"]), rows(a["router_group_b"]), rows(a["router_expert_b"]), cols(router)], axis=2)
    w_q = a["w_in"][:, :, 0:512].reshape(L, D, KV, GRP, HD).transpose(0, 1, 3, 2, 4).reshape(L, D, 512)
    heads = a["w_out"][:, 0:512].reshape(L, KV, GRP, HD, D).transpose(0, 2, 1, 3, 4).reshape(L, 512, D)
    w_out = _np.concatenate([heads, a["w_out"][:, 512:]], axis=1)
    cmp_w1 = a["cmp_w1"].reshape(L, 2, 16, P, P).transpose(0, 3, 1, 2, 4).reshape(L, P, 4096)
    cmp_w2 = a["cmp_w2"].transpose(0, 2, 1, 3).reshape(L, P, 2 * HD)
    f, masks = constants()
    feeds = {
        "x": a["x"][0], "mem": a["mem"][0], "w_q": w_q, "w_in": a["w_in"], "cmp_w1": cmp_w1,
        "cmp_w2": cmp_w2, "w_out": w_out, "wq": a["cross_wq"], "wkv": a["cross_wkv"], "wo": a["cross_wo"],
        "w_gu": a["expert_w_gate_up"], "w_dn": a["expert_w_down"], "norm_final": a["norm_final"],
        "params": params, "lb_logits": a["hgrn_lb_logits"].reshape(L, 2, P).transpose(2, 0, 1),
        "consts": f, "masks": masks}
    nc = _bacc.Bacc("TRN2", target_bir_lowering=False, num_devices=1)
    arrays, args = {}, []
    for name, v in feeds.items():
        v = _np.ascontiguousarray(v)
        arrays[f"in_{name}"] = v
        args.append(nc.dram_tensor(f"in_{name}", v.shape, _mybir.dt.from_np(v.dtype), kind="ExternalInput").ap())
    out = nc.dram_tensor("out_y", (256, D), F32, kind="ExternalOutput").ap()
    hymba(nc, L, *args, out)
    r = _run(nc, [arrays], core_ids=[0])
    return r.results[0]["out_y"].reshape(a["x"].shape)
```
